# Optimizing a Trainium2 kernel written in Bass

```python
import math
import jax, jax.numpy as jnp
from jax import lax
import numpy as np

D_MODEL = 1024
BATCH = 1
SEQ = 1024
DEPTH = 1

PLE_DIM = 256
HEAD_DIM = 128
N_HGRN_HEADS = D_MODEL // (2 * HEAD_DIM)
N_GDN_HEADS = D_MODEL // (2 * HEAD_DIM)
D_HGRN = N_HGRN_HEADS * HEAD_DIM
D_GDN = N_GDN_HEADS * HEAD_DIM
D_MIX = D_HGRN + D_GDN
D_IN = 4 * D_HGRN + 4 * D_GDN + 2 * N_GDN_HEADS
GDN_CONV = 4
FFN_CONV = 3
D_FF = 2816
CHUNK = 64
EPS = 1e-6

kernel_name = "hymba_hgrn2_gdn_convffn_ple"

def rms_norm(x, w):
    xf = x.astype(jnp.float32)
    y = xf * lax.rsqrt(jnp.mean(xf * xf, axis=-1, keepdims=True) + EPS)
    return (y * w.astype(jnp.float32)).astype(x.dtype)

def l2_normalize(x):
    xf = x.astype(jnp.float32)
    return xf * lax.rsqrt(jnp.sum(xf * xf, axis=-1, keepdims=True) + EPS)

def causal_dwconv(x, w):
    k_width, ch = w.shape
    return lax.conv_general_dilated(
        x, w[:, None, :].astype(x.dtype), window_strides=(1,),
        padding=[(k_width - 1, 0)], dimension_numbers=("NWC", "WIO", "NWC"),
        feature_group_count=ch)

def to_heads(t):
    b, s, _ = t.shape
    return t.reshape(b, s, -1, HEAD_DIM).transpose(0, 2, 1, 3)

def from_heads(t):
    b, h, s, d = t.shape
    return t.transpose(0, 2, 1, 3).reshape(b, s, h * d)

def to_chunks(t):
    b, h, s = t.shape[:3]
    return t.reshape((b, h, s // CHUNK, CHUNK) + t.shape[3:])

def hgrn2_chunked(q, k, v, log_f):
    b, h, s, dk = q.shape
    dv = v.shape[-1]
    qc, kc, vc, gc = (jnp.moveaxis(to_chunks(t.astype(jnp.float32)), 2, 0)
                      for t in (q, k, v, log_f))
    bc = jnp.cumsum(gc, axis=-2)
    idx = jnp.arange(CHUNK)
    causal = (idx[:, None] >= idx[None, :])[:, :, None]

    def step(state, inp):
        qi, ki, vi, bi = inp
        diff = bi[..., :, None, :] - bi[..., None, :, :]
        decay = jnp.exp(jnp.where(causal, diff, -jnp.inf))
        scores = jnp.einsum("bhtd,bhsd,bhtsd->bhts", qi, ki, decay)
        o = (jnp.einsum("bhts,bhsv->bhtv", scores, vi)
             + jnp.einsum("bhtd,bhdv->bhtv", qi * jnp.exp(bi), state))
        b_last = bi[..., -1:, :]
        state = (jnp.exp(b_last[..., 0, :])[..., :, None] * state
                 + jnp.einsum("bhsd,bhsv->bhdv", ki * jnp.exp(b_last - bi), vi))
        return state, o

    s0 = jnp.zeros((b, h, dk, dv), jnp.float32)
    _, o = lax.scan(step, s0, (qc, kc, vc, bc))
    return jnp.moveaxis(o, 0, 2).reshape(b, h, s, dv)

def gated_delta_chunked(q, k, v, log_a, beta):
    b, h, s, dk = q.shape
    dv = v.shape[-1]
    qc, kc, vc = (to_chunks(t.astype(jnp.float32)) for t in (q, k, v))
    betac = to_chunks(beta.astype(jnp.float32))
    gcum = jnp.cumsum(to_chunks(log_a.astype(jnp.float32)), axis=-1)
    idx = jnp.arange(CHUNK)
    incl = idx[:, None] >= idx[None, :]
    strict = idx[:, None] > idx[None, :]
    diff = gcum[..., :, None] - gcum[..., None, :]
    k_beta = kc * betac[..., None]
    lower = (jnp.einsum("bhntd,bhnsd->bhnts", k_beta, kc)
             * jnp.exp(jnp.where(strict, diff, -jnp.inf)))
    system = jnp.eye(CHUNK, dtype=jnp.float32) + lower
    u = lax.linalg.triangular_solve(system, vc * betac[..., None], left_side=True,
                                    lower=True, unit_diagonal=True)
    w = lax.linalg.triangular_solve(system, k_beta * jnp.exp(gcum)[..., None], left_side=True,
                                    lower=True, unit_diagonal=True)
    attn = (jnp.einsum("bhntd,bhnsd->bhnts", qc, kc)
            * jnp.exp(jnp.where(incl, diff, -jnp.inf)))
    q_dec = qc * jnp.exp(gcum)[..., None]
    g_last = gcum[..., -1]
    k_dec = kc * jnp.exp(g_last[..., None] - gcum)[..., None]
    scan_in = tuple(jnp.moveaxis(t, 2, 0) for t in (q_dec, k_dec, u, w, attn, g_last))

    def step(state, inp):
        qi, ki, ui, wi, ai, gl = inp
        v_new = ui - jnp.einsum("bhcd,bhdv->bhcv", wi, state)
        o = (jnp.einsum("bhcd,bhdv->bhcv", qi, state)
             + jnp.einsum("bhts,bhsv->bhtv", ai, v_new))
        state = (state * jnp.exp(gl)[..., None, None]
                 + jnp.einsum("bhsd,bhsv->bhdv", ki, v_new))
        return state, o

    s0 = jnp.zeros((b, h, dk, dv), jnp.float32)
    _, o = lax.scan(step, s0, scan_in)
    return jnp.moveaxis(o, 0, 2).reshape(b, h, s, dv)

def hybrid_mixer(h, w_in, lb, hgrn_out_norm, gdn_conv, gdn_a_log, gdn_dt_bias,
                 gdn_out_norm, w_out):
    proj = h @ w_in
    cuts = [D_HGRN, 2 * D_HGRN, 3 * D_HGRN, 4 * D_HGRN,
            4 * D_HGRN + 3 * D_GDN, 4 * D_HGRN + 4 * D_GDN,
            4 * D_HGRN + 4 * D_GDN + N_GDN_HEADS]
    hq, hf, hi, hg, gqkv, gz, ga, gb = jnp.split(proj, cuts, axis=-1)

    f = lb + (1.0 - lb) * jax.nn.sigmoid(hf.astype(jnp.float32))
    o_a = hgrn2_chunked(to_heads(jax.nn.silu(hq)), to_heads(1.0 - f),
                        to_heads(hi), to_heads(jnp.log(f)))
    o_a = from_heads(rms_norm(o_a, hgrn_out_norm)) * jax.nn.silu(hg.astype(jnp.float32))

    qkv = jax.nn.silu(causal_dwconv(gqkv, gdn_conv))
    gq, gk, gv = jnp.split(qkv, 3, axis=-1)
    gq = l2_normalize(to_heads(gq)) * (HEAD_DIM ** -0.5)
    gk = l2_normalize(to_heads(gk))
    log_a = (-jnp.exp(gdn_a_log.astype(jnp.float32))
             * jax.nn.softplus(ga.astype(jnp.float32) + gdn_dt_bias.astype(jnp.float32)))
    beta = jax.nn.sigmoid(gb.astype(jnp.float32))
    o_b = gated_delta_chunked(gq, gk, to_heads(gv), log_a.transpose(0, 2, 1),
                              beta.transpose(0, 2, 1))
    o_b = from_heads(rms_norm(o_b, gdn_out_norm)) * jax.nn.silu(gz.astype(jnp.float32))

    mixed = jnp.concatenate([o_a, o_b], axis=-1).astype(h.dtype)
    return mixed @ w_out

def conv_gated_mlp(h, w_up, ffn_conv, w_down):
    u = causal_dwconv(h @ w_up, ffn_conv)
    gate, up = jnp.split(u, 2, axis=-1)
    return (jax.nn.silu(gate) * up) @ w_down

def setup_inputs(seed: int = 0) -> dict:
    key = jax.random.key(seed)
    ks = jax.random.split(key, 24)
    f32 = jnp.float32

    def nrm(k, shape, scale):
        return jax.random.normal(k, shape, f32) * scale

    def gain(k, shape):
        return 1.0 + 0.05 * jax.random.normal(k, shape, f32)

    dt = jnp.exp(jax.random.uniform(ks[9], (DEPTH, N_GDN_HEADS), f32,
                                    minval=math.log(1e-3), maxval=math.log(1e-1)))
    return {
        "x": nrm(ks[0], (BATCH, SEQ, D_MODEL), 1.0),
        "p": nrm(ks[1], (DEPTH, BATCH, SEQ, PLE_DIM), 1.0),
        "mix_norm_pre": gain(ks[2], (DEPTH, D_MODEL)),
        "mix_norm_post": gain(ks[3], (DEPTH, D_MODEL)),
        "w_in": nrm(ks[4], (DEPTH, D_MODEL, D_IN), D_MODEL ** -0.5),
        "hgrn_lb_logits": nrm(ks[5], (DEPTH + 1, D_HGRN), 0.5),
        "hgrn_out_norm": gain(ks[6], (DEPTH, HEAD_DIM)),
        "gdn_conv": nrm(ks[7], (DEPTH, GDN_CONV, 3 * D_GDN), GDN_CONV ** -0.5),
        "gdn_a_log": jnp.log(jax.random.uniform(ks[8], (DEPTH, N_GDN_HEADS), f32,
                                                minval=1.0, maxval=16.0)),
        "gdn_dt_bias": dt + jnp.log(-jnp.expm1(-dt)),
        "gdn_out_norm": gain(ks[10], (DEPTH, HEAD_DIM)),
        "w_out": nrm(ks[11], (DEPTH, D_MIX, D_MODEL), D_MIX ** -0.5),
        "ffn_norm_pre": gain(ks[12], (DEPTH, D_MODEL)),
        "ffn_norm_post": gain(ks[13], (DEPTH, D_MODEL)),
        "w_up": nrm(ks[14], (DEPTH, D_MODEL, 2 * D_FF), D_MODEL ** -0.5),
        "ffn_conv": nrm(ks[15], (DEPTH, FFN_CONV, 2 * D_FF), FFN_CONV ** -0.5),
        "w_down": nrm(ks[16], (DEPTH, D_FF, D_MODEL), D_FF ** -0.5),
        "w_ple": nrm(ks[17], (DEPTH, PLE_DIM, D_MODEL), PLE_DIM ** -0.5),
        "w_ple_gate": nrm(ks[18], (DEPTH, D_MODEL, D_MODEL), D_MODEL ** -0.5),
        "ple_norm_post": gain(ks[19], (DEPTH, D_MODEL)),
    }

def reference(x, p, mix_norm_pre, mix_norm_post, w_in, hgrn_lb_logits, hgrn_out_norm,
              gdn_conv, gdn_a_log, gdn_dt_bias, gdn_out_norm, w_out, ffn_norm_pre,
              ffn_norm_post, w_up, ffn_conv, w_down, w_ple, w_ple_gate, ple_norm_post):
    lower_bounds = jnp.cumsum(jax.nn.softmax(hgrn_lb_logits.astype(jnp.float32), axis=0),
                              axis=0)
    for i in range(DEPTH):
        h = rms_norm(x, mix_norm_pre[i])
        mix = hybrid_mixer(h, w_in[i], lower_bounds[i], hgrn_out_norm[i], gdn_conv[i],
                           gdn_a_log[i], gdn_dt_bias[i], gdn_out_norm[i], w_out[i])
        x = x + rms_norm(mix, mix_norm_post[i])
        h = rms_norm(x, ffn_norm_pre[i])
        x = x + rms_norm(conv_gated_mlp(h, w_up[i], ffn_conv[i], w_down[i]), ffn_norm_post[i])
        ple = (p[i] @ w_ple[i]) * jax.nn.sigmoid(x @ w_ple_gate[i])
        x = x + rms_norm(ple, ple_norm_post[i])
    return x


_drawn_inputs = setup_inputs


def setup_inputs(seed=0):
    import zlib

    import numpy as np

    out = dict(_drawn_inputs(seed))
    spreads = {}
    factors = {}
    for name, (base, spread) in spreads.items():
        noise = np.random.default_rng([zlib.crc32(name.encode()), seed]).standard_normal(out[name].shape)
        drawn = base * np.exp(spread * noise) if base else spread * noise
        out[name] = __import__('jax').numpy.asarray(drawn.astype(out[name].dtype))
    for name, factor in factors.items():
        out[name] = (out[name] * factor).astype(out[name].dtype)
    return out
```

```python
from contextlib import ExitStack

import numpy as np

import concourse.bass as bass
from concourse import mybir

F32 = mybir.dt.float32
F32R = mybir.dt.float32r
U32 = mybir.dt.uint32
ALU = mybir.AluOpType
ACT = mybir.ActivationFunctionType

P = 128
SEQ = 1024
DM = 1024
HD = 128
NH = 4
DG = NH * HD
DIN = 8 * DG + 2 * NH
DFF = 2816
DPLE = 256
EPS = 1e-6
NT = SEQ // P
KT = DM // P
FT = DFF // P
GK, FK = 4, 3
LEVELS = 7
HALF = SEQ // 2
BANK = 512

C_MIXPRE = 0
C_FFNPRE = C_MIXPRE + KT
C_HNORM = C_FFNPRE + KT
C_GNORM = C_HNORM + 1
C_LB = C_GNORM + 1
C_GCONV = C_LB + 2 * NH
C_FCONV = C_GCONV + GK * 3 * NH
N_ROWS = C_FCONV
N_COLS = C_FCONV + FK * 2 * FT


class Kit:

    def __init__(self, nc, ctx):
        self.nc, self.ctx = nc, ctx
        self.psum = ctx.enter_context(nc.psum_tensor("psum", [P, 8, BANK], F32))
        c = lambda name, shape: ctx.enter_context(nc.sbuf_tensor(name, shape, F32))
        self.ident = c("ident", [P, P])
        self.ones = c("ones", [P, P])
        self.tri = c("tri", [P, P])
        self.future = c("future", [P, P])
        self.mask = c("mask", [P, LEVELS, P])
        self.maskT = c("maskT", [P, LEVELS, P])
        self.cols = c("cols", [P, N_COLS])
        self.eps = c("eps", [P, 2])
        self.lb = c("lb", [P, 2 * NH])

        self.sems = []

    def sem(self, name):
        self.sems.append(self.nc.alloc_semaphore(name))
        return self.sems[-1]

    def recycle(self):
        self.nc.clear_and_free_semaphores(self.sems)
        self.nc.all_engine_barrier()
        self.sems = []


def alone(eng, passed):
    eng.sem_inc(passed, 1)


def prime(eng, sem, n=1):
    eng.sem_inc(sem, n)


def over_heads(ap):
    return ap.unsqueeze(1).broadcast_to([P, NH, ap.shape[1]])


def over_tokens(ap, n=P):
    return ap.unsqueeze(2).broadcast_to([P, ap.shape[1], n])


def heads(ap):
    return ap.rearrange("p (h t) -> p h t", h=NH)


def stage_setup(k, params):
    nc = k.nc
    made, loaded, turned, kept, soft = (k.sem("setup_" + n) for n in ("made", "loaded", "turned", "kept", "soft"))
    with ExitStack() as tmp:
        rows = tmp.enter_context(nc.sbuf_tensor("param_rows", [P, P], F32))
        frows = tmp.enter_context(nc.sbuf_tensor("ffn_conv_rows", [P, 2, P], F32))
        sm = tmp.enter_context(nc.sbuf_tensor("bound_work", [P, 6, NH], F32))
        half = FK * 2 * FT // 2
        with nc.Block() as block:
            @block.sync
            def _(sp):
                n = 0
                for at, src in ((C_MIXPRE, params["mix_norm_pre"].rearrange("o (r c) -> (o r) c", c=P)),
                                (C_FFNPRE, params["ffn_norm_pre"].rearrange("o (r c) -> (o r) c", c=P)),
                                (C_HNORM, params["hgrn_out_norm"]),
                                (C_GNORM, params["gdn_out_norm"]),
                                (C_LB, params["hgrn_lb_logits"].rearrange("o (r c) -> (o r) c", c=P)),
                                (C_GCONV, params["gdn_conv"].rearrange("o k (r c) -> (o k r) c", c=P))):
                    sp.dma_start(rows[at:at + src.shape[0], :], src).then_inc(loaded, 16)
                    n += 16
                fsrc = params["ffn_conv"].rearrange("o k (r c) -> (o k r) c", c=P)
                for i in range(2):
                    sp.dma_start(frows[0:half, i, :], fsrc[i * half:(i + 1) * half, :]).then_inc(loaded, 16)
                    n += 16
                assert n == 128

            @block.gpsimd
            def _(pool):
                step = 0

                def kept_step(ins):
                    ins.then_inc(made, 1)
                    pool.wait_ge(made, step)

                for t, v in ((k.ident, 0.0), (k.ones, 1.0), (k.tri, 1.0), (k.future, 0.0), (k.mask, 0.0), (k.maskT, 0.0)):
                    step += 1
                    pool.memset(t[:], v).then_inc(made, 1)
                step += 2
                pool.memset(k.eps[:, 0:1], EPS).then_inc(made, 1)
                pool.memset(k.eps[:, 1:2], HD * EPS).then_inc(made, 1)
                for lv in range(LEVELS):
                    m = 1 << lv
                    for t, side in ((k.mask, 1), (k.maskT, 0)):
                        step += 1
                        if step == 9:
                            pool.wait_ge(made, 8)
                        v = t[:, lv, :].rearrange("p (n two m) -> p n two m", two=2, m=m)[:, :, side, :]
                        pool.memset(v, 1.0).then_inc(made, 1)
                pool.wait_ge(made, step)
                step += 1
                kept_step(pool.affine_select(out=k.ident[:], in_=k.ident[:], pattern=[[-1, P]],
                                             compare_op=ALU.not_equal, fill=1.0, base=0, channel_multiplier=1))
                step += 1
                kept_step(pool.affine_select(out=k.tri[:], in_=k.tri[:], pattern=[[1, P]],
                                             compare_op=ALU.is_ge, fill=0.0, base=0, channel_multiplier=-1))
                step += 1
                kept_step(pool.affine_select(out=k.future[:], in_=k.future[:], pattern=[[1, P]],
                                             compare_op=ALU.is_ge, fill=-1e30, base=0, channel_multiplier=-1))
                for lv in range(LEVELS):
                    m = 1 << lv
                    n = P // (2 * m)
                    for t, side in ((k.mask, 1), (k.maskT, 0)):
                        v = t[:, lv, :].rearrange("p (n two m) -> p n two m", two=2, m=m)[:, :, side, :]
                        lowest = 0 if side else m
                        step += 1
                        kept_step(pool.affine_select(out=v, in_=v, pattern=[[-2 * m, n], [0, m]],
                                                     compare_op=ALU.is_ge, fill=0.0, base=-lowest,
                                                     channel_multiplier=1))
                        step += 1
                        kept_step(pool.affine_select(out=v, in_=v, pattern=[[2 * m, n], [0, m]],
                                                     compare_op=ALU.is_ge, fill=0.0, base=lowest + m - 1,
                                                     channel_multiplier=-1))

            @block.tensor
            def _(pe):
                pe.wait_ge(made, 8 + 2 * LEVELS + 1)
                pe.wait_ge(loaded, 128)
                pe.transpose(k.psum[:, 0, 0:N_ROWS], rows[0:N_ROWS, :], k.ident[0:N_ROWS, 0:N_ROWS]).then_inc(turned, 1)
                for i in range(2):
                    pe.transpose(k.psum[:, 1 + i, 0:half], frows[0:half, i, :],
                                 k.ident[0:half, 0:half]).then_inc(turned, 1)

            @block.vector
            def _(dve):
                dve.wait_ge(turned, 3)
                dve.tensor_copy(k.cols[:, 0:N_ROWS], k.psum[:, 0, 0:N_ROWS]).then_inc(kept, 1)
                for i in range(2):
                    at = C_FCONV + i * half
                    dve.tensor_copy(k.cols[:, at:at + half], k.psum[:, 1 + i, 0:half]).then_inc(kept, 1)
                dve.wait_ge(kept, 3)
                l0, l1 = k.cols[:, C_LB:C_LB + NH], k.cols[:, C_LB + NH:C_LB + 2 * NH]
                dve.tensor_tensor(sm[:, 0, :], l0, l1, ALU.max).then_inc(kept, 1)
                dve.wait_ge(kept, 4)
                dve.tensor_tensor(sm[:, 1, :], l0, sm[:, 0, :], ALU.subtract)
                dve.tensor_tensor(sm[:, 2, :], l1, sm[:, 0, :], ALU.subtract).then_inc(kept, 1)
                dve.wait_ge(soft, 1)
                dve.tensor_tensor(sm[:, 5, :], sm[:, 3, :], sm[:, 4, :], ALU.add).then_inc(kept, 1)
                dve.wait_ge(kept, 6)
                dve.reciprocal(sm[:, 0, :], sm[:, 5, :]).then_inc(kept, 1)
                dve.wait_ge(kept, 7)
                dve.tensor_tensor(k.lb[:, 0:NH], sm[:, 3, :], sm[:, 0, :], ALU.mult).then_inc(kept, 1)
                dve.wait_ge(kept, 8)
                dve.tensor_scalar(k.lb[:, NH:2 * NH], k.lb[:, 0:NH], -1.0, 1.0, ALU.mult, ALU.add)

            @block.scalar
            def _(act):
                act.wait_ge(kept, 5)
                act.activation(sm[:, 3:5, :], sm[:, 1:3, :], ACT.Exp).then_inc(soft, 1)


def stage_rms(k, name, src, tiles, dst):
    nc = k.nc
    n = len(tiles)
    squared, rooted, inverted = (k.sem(name + s) for s in ("_squared", "_rooted", "_inverted"))
    with ExitStack() as tmp:
        stat = tmp.enter_context(nc.sbuf_tensor(name + "_stat", [P, 3, NT], F32))
        junk = tmp.enter_context(nc.sbuf_tensor(name + "_junk", [P, DM], F32))
        with nc.Block() as block:
            @block.scalar
            def _(act):
                for i, t in enumerate(tiles):
                    if i:
                        act.wait_ge(squared, i)
                    act.activation(junk[:], src[:, t, :], ACT.Square, accum_out=stat[:, 0, i:i + 1]).then_inc(squared, 1)
                act.wait_ge(squared, n)
                act.activation(stat[:, 1, 0:n], stat[:, 0, 0:n], ACT.Sqrt, bias=k.eps[:, 0:1],
                               scale=1.0 / DM).then_inc(rooted, 1)

            @block.vector
            def _(dve):
                dve.wait_ge(rooted, 1)
                dve.reciprocal(stat[:, 2, 0:n], stat[:, 1, 0:n]).then_inc(inverted, 1)
                dve.wait_ge(inverted, 1)
                for i, t in enumerate(tiles):
                    dve.tensor_scalar(dst[:, i, :], src[:, t, :], stat[:, 2, i:i + 1], None, ALU.mult)


def stage_turn(k, name, src, tiles, hi, lo, scale, n_k=KT):
    nc = k.nc
    turned, rounded, rest = (k.sem(name + s) for s in ("_turned", "_rounded", "_rest"))
    quads = [(kt, q) for kt in range(n_k) for q in range(len(tiles) // 4)]
    with nc.Block() as block:
        @block.tensor
        def _(pe):
            for j, (kt, q) in enumerate(quads):
                if j >= 8:
                    pe.wait_ge(rest, j - 7)
                for i in range(4):
                    ins = pe.transpose(k.psum[:, j % 8, i * P:(i + 1) * P],
                                       src[:, tiles[4 * q + i], kt * P:(kt + 1) * P], k.ident[:])
                ins.then_inc(turned, 1)

        @block.scalar
        def _(act):
            for j, (kt, q) in enumerate(quads):
                act.wait_ge(turned, j + 1)
                s = scale(kt)
                act.activation(hi[:, kt, q * BANK:(q + 1) * BANK], k.psum[:, j % 8, :], ACT.Copy,
                               scale=1.0 if s is None else s).then_inc(rounded, 1)

        @block.vector
        def _(dve):
            for j, (kt, q) in enumerate(quads):
                dve.wait_ge(rounded, j + 1)
                s = scale(kt)
                dve.scalar_tensor_tensor(out=lo[:, kt, q * BANK:(q + 1) * BANK], in0=k.psum[:, j % 8, :],
                                         scalar=1.0 if s is None else s,
                                         in1=hi[:, kt, q * BANK:(q + 1) * BANK].bitcast(F32),
                                         op0=ALU.mult, op1=ALU.subtract).then_inc(rest, 1)


def stage_natural(k, name, hi, lo, t_tiles, n_k, weight, width, groups, take):
    nc = k.nc
    parts = width // BANK
    banks = t_tiles * parts
    RING = 2
    arrived = [k.sem(f"{name}_arrived{i}") for i in range(RING)]
    rounded, rest, summed, taken = (k.sem(name + s) for s in ("_rounded", "_rest", "_summed", "_taken"))
    slabs = [(g, kt) for g in range(groups) for kt in range(n_k)]
    with ExitStack() as tmp:
        raw = tmp.enter_context(nc.sbuf_tensor(name + "_raw", [P, RING, width], F32))
        whi = tmp.enter_context(nc.sbuf_tensor(name + "_whi", [P, RING, width], F32R))
        wlo = tmp.enter_context(nc.sbuf_tensor(name + "_wlo", [P, RING, width], F32R))
        with nc.Block() as block:
            @block.sync
            def _(sp):
                for j, (g, kt) in enumerate(slabs):
                    if j >= RING:
                        sp.wait_ge(rest, j - RING + 1)
                    sp.dma_start(raw[:, j % RING, :], weight(g, kt)).then_inc(arrived[j % RING], 16)

            @block.scalar
            def _(act):
                def out_of_banks(g):
                    for b in range(banks):
                        act.wait_ge(summed, ((g + 1) * n_k - 1) * banks + b + 1)
                        take(act, g, b // parts, b % parts, b).then_inc(taken, 1)

                for j, (g, kt) in enumerate(slabs):
                    act.wait_ge(arrived[j % RING], 16 * (j // RING + 1))
                    if j >= RING:
                        act.wait_ge(summed, (j - RING + 1) * banks)
                    act.activation(whi[:, j % RING, :], raw[:, j % RING, :], ACT.Copy).then_inc(rounded, 1)
                    if kt == 0 and g:
                        out_of_banks(g - 1)
                out_of_banks(groups - 1)

            @block.vector
            def _(dve):
                for j in range(len(slabs)):
                    dve.wait_ge(rounded, j + 1)
                    dve.tensor_tensor(wlo[:, j % RING, :], raw[:, j % RING, :],
                                      whi[:, j % RING, :].bitcast(F32), ALU.subtract).then_inc(rest, 1)

            @block.tensor
            def _(pe):
                for j, (g, kt) in enumerate(slabs):
                    pe.wait_ge(rest, j + 1)
                    r = j % RING
                    for b in range(banks):
                        t, n = b // parts, b % parts
                        if kt == 0 and g:
                            pe.wait_ge(taken, (g - 1) * banks + b + 1)
                        out = k.psum[:, b, :]
                        ah, al = hi[:, kt, t * P:(t + 1) * P], lo[:, kt, t * P:(t + 1) * P]
                        wh, wl = whi[:, r, n * BANK:(n + 1) * BANK], wlo[:, r, n * BANK:(n + 1) * BANK]
                        pe.matmul(out, ah, wh, start=(kt == 0), stop=False)
                        pe.matmul(out, ah, wl, start=False, stop=False)
                        pe.matmul(out, al, wh, start=False, stop=(kt == n_k - 1)).then_inc(summed, 1)


class Turned:

    def __init__(self, k, name, tmp, hi, lo, halves, pairs, weight):
        nc = k.nc
        self.k, self.hi, self.lo, self.halves, self.pairs, self.weight = k, hi, lo, halves, pairs, weight
        self.arrived = [k.sem(f"{name}_arrived{i}") for i in range(2)]
        self.rounded, self.rest, self.summed, self.taken = (
            k.sem(name + s) for s in ("_rounded", "_rest", "_summed", "_taken"))
        self.raw = tmp.enter_context(nc.sbuf_tensor(name + "_raw", [P, 2, KT, P], F32))
        self.whi = [tmp.enter_context(nc.sbuf_tensor(f"{name}_whi{u}", [P, KT, P], F32R)) for u in range(2)]
        self.wlo = [tmp.enter_context(nc.sbuf_tensor(f"{name}_wlo{u}", [P, KT, P], F32R)) for u in range(2)]

    def load(self, sp):
        def pair(i, first=False):
            for u in range(2):
                if not first:
                    sp.wait_ge(self.rest, 2 * i + u - 1)
                sp.dma_start(self.raw[:, u, :, :], self.weight(i, u)).then_inc(self.arrived[u], 16)

        pair(0, first=True)
        if self.pairs > 1:
            with sp.Fori(1, self.pairs) as i:
                pair(i)

    def round(self, act, i, u, first=False):
        act.wait_ge(self.arrived[u], i * 16 + 16)
        if not first:
            act.wait_ge(self.summed, (2 * i + u - 1) * self.halves)
        act.activation(self.whi[u][:], self.raw[:, u, :, :], ACT.Copy).then_inc(self.rounded, 1)

    def remainder(self, dve, i, u):
        dve.wait_ge(self.rounded, 2 * i + u + 1)
        dve.tensor_tensor(self.wlo[u][:], self.raw[:, u, :, :], self.whi[u][:].bitcast(F32),
                          ALU.subtract).then_inc(self.rest, 1)

    def bank(self, u, half):
        return self.k.psum[:, u * self.halves + half, :]

    def multiply(self, pe):
        def pair(i, first=False):
            for u in range(2):
                pe.wait_ge(self.rest, 2 * i + u + 1)
                for half in range(self.halves):
                    if not first:
                        pe.wait_ge(self.taken, (2 * i + u - 2) * self.halves + half + 1)
                    out = self.bank(u, half)
                    for kt in range(KT):
                        ah = self.hi[:, kt, half * BANK:(half + 1) * BANK]
                        al = self.lo[:, kt, half * BANK:(half + 1) * BANK]
                        pe.matmul(out, self.whi[u][:, kt, :], ah, start=(kt == 0), stop=False)
                        pe.matmul(out, self.whi[u][:, kt, :], al, start=False, stop=False)
                        ins = pe.matmul(out, self.wlo[u][:, kt, :], ah, start=False, stop=(kt == KT - 1))
                    ins.then_inc(self.summed, 1)

        pair(0, first=True)
        if self.pairs > 1:
            with pe.Fori(1, self.pairs) as i:
                pair(i)

    def each_pair(self, eng, body):
        if self.pairs > 1:
            with eng.Fori(0, self.pairs - 1) as i:
                body(i, True)
        body(self.pairs - 1, False)


def slab(w, rows, at):
    return w[0:rows, bass.ds(at, P)].rearrange("(kt p) c -> p kt c", p=P)


def stage_gdn_project(k, hi, lo, w_in, qkv):
    nc = k.nc
    freed, tapped, smooth = k.sem("gconv_freed"), k.sem("gconv_tapped"), k.sem("gconv_smooth")
    with ExitStack() as tmp:
        first_col = 4 * DG
        g = Turned(k, "gproj", tmp, hi, lo, 2, 3 * NH // 2, lambda i, u: slab(w_in, DM, (2 * i + u) * P + first_col))
        pad = GK - 1
        line = [tmp.enter_context(nc.sbuf_tensor(f"gconv_line{u}", [P, pad + SEQ], F32)) for u in range(2)]
        acc = [tmp.enter_context(nc.sbuf_tensor(f"gconv_acc{u}", [P, SEQ], F32)) for u in range(2)]
        with nc.Block() as block:
            @block.sync
            def _(sp):
                g.load(sp)

            @block.tensor
            def _(pe):
                g.multiply(pe)

            @block.scalar
            def _(act):
                g.round(act, 0, 0, first=True)
                g.round(act, 0, 1, first=True)

                def pair(i, more):
                    for u in range(2):
                        act.wait_ge(freed, 2 * i + u + 1)
                        for half in range(2):
                            act.wait_ge(g.summed, (2 * i + u) * 2 + half + 1)
                            act.activation(line[u][:, pad + half * BANK:pad + (half + 1) * BANK], g.bank(u, half),
                                           ACT.Copy).then_inc(g.taken, 1)
                        if more:
                            g.round(act, i + 1, u)
                        act.wait_ge(freed, 2 * i + u + 3)
                        act.activation(qkv[:, bass.ds(2 * i + u, 1), :].rearrange("p o t -> p (o t)"), acc[u][:],
                                       ACT.Silu).then_inc(smooth, 1)

                prime(act, smooth)
                g.each_pair(act, pair)

            @block.vector
            def _(dve):
                for u in range(2):
                    dve.memset(line[u][:, 0:pad], 0.0).then_inc(freed, 1)
                for u in range(2):
                    g.remainder(dve, 0, u)

                def pair(i, more):
                    for u in range(2):
                        tap = lambda q: k.cols[:, bass.ds(2 * i + u + (C_GCONV + q * 3 * NH), 1)]
                        dve.wait_ge(g.taken, (2 * i + u) * 2 + 2)
                        dve.wait_ge(smooth, 2 * i + u + 1)
                        dve.tensor_scalar(acc[u][:], line[u][:, 0:SEQ], tap(0), None, ALU.mult).then_inc(tapped, 1)
                        for q in range(1, GK):
                            dve.wait_ge(tapped, (2 * i + u) * (GK - 1) + q)
                            dve.scalar_tensor_tensor(out=acc[u][:], in0=line[u][:, q:q + SEQ], scalar=tap(q), in1=acc[u][:],
                                                     op0=ALU.mult, op1=ALU.add).then_inc(freed if q == GK - 1 else tapped, 1)
                        if more:
                            g.remainder(dve, i + 1, u)

                g.each_pair(dve, pair)


def stage_gdn_gates(k, hi, lo, w_in, a_log, dt_bias, small):
    nc = k.nc
    s_in, s_hi, s_lo, s_mm, s_row, s_turn, s_act, s_dve, s_sum = (
        k.sem("gate_" + n) for n in ("in", "hi", "lo", "mm", "row", "turn", "act", "dve", "sum"))
    NG = 2 * NH
    with ExitStack() as tmp:
        t = lambda name, shape, dt=F32: tmp.enter_context(nc.sbuf_tensor(name, shape, dt))
        raw, whi, wlo = t("gate_raw", [P, KT, P]), t("gate_whi", [P, KT, P], F32R), t("gate_wlo", [P, KT, P], F32R)
        row = t("gate_row", [NG, SEQ])
        par = t("gate_par", [P, 2, NH])
        z = t("gate_z", [P, 8, NT, NH])
        col = t("gate_col", [P, NT, NG])
        with nc.Block() as block:
            @block.sync
            def _(sp):
                sp.dma_start(raw[:], slab(w_in, DM, DIN - P)).then_inc(s_in, 16)
                sp.dma_start(par[:, 0, :], a_log.partition_broadcast(P)).then_inc(s_in, 16)
                sp.dma_start(par[:, 1, :], dt_bias.partition_broadcast(P)).then_inc(s_in, 16)

            @block.scalar
            def _(act):
                act.wait_ge(s_in, 48)
                act.activation(whi[:, :, 0:NG], raw[:, :, P - NG:P], ACT.Copy)
                act.activation(whi[:, :, NG:P], raw[:, :, 0:P - NG], ACT.Copy).then_inc(s_hi, 1)
                for half in range(2):
                    act.wait_ge(s_mm, half + 1)
                    act.activation(row[:, half * BANK:(half + 1) * BANK], k.psum[0:NG, half, :], ACT.Copy).then_inc(s_row, 1)
                act.wait_ge(s_dve, 3)
                act.activation(z[:, 2], z[:, 1], ACT.Exp, scale=-1.0).then_inc(s_act, 1)
                act.activation(z[:, 7, 0, :], par[:, 0, :], ACT.Exp).then_inc(s_act, 1)
                act.wait_ge(s_act, 2)
                act.activation(z[:, 3], z[:, 2], ACT.Ln, bias=1.0).then_inc(s_act, 1)
                act.activation(small[:, 1], col[:, :, NH:NG], ACT.Sigmoid).then_inc(s_act, 1)
                act.wait_ge(s_dve, 10)
                act.activation(z[:, 4], small[:, 0], ACT.Exp).then_inc(s_act, 1)
                act.activation(small[:, 3], z[:, 6], ACT.Exp)
                act.activation(small[:, 4], z[:, 5], ACT.Exp)

            @block.tensor
            def _(pe):
                pe.wait_ge(s_lo, 1)
                for half in range(2):
                    for kt in range(KT):
                        ah = hi[:, kt, half * BANK:(half + 1) * BANK]
                        al = lo[:, kt, half * BANK:(half + 1) * BANK]
                        pe.matmul(k.psum[:, half, :], whi[:, kt, :], ah, start=(kt == 0), stop=False)
                        pe.matmul(k.psum[:, half, :], whi[:, kt, :], al, start=False, stop=False)
                        ins = pe.matmul(k.psum[:, half, :], wlo[:, kt, :], ah, start=False, stop=(kt == KT - 1))
                    ins.then_inc(s_mm, 1)
                pe.wait_ge(s_row, 2)
                for c in range(NT):
                    ins = pe.transpose(k.psum[:, 2, c * NG:(c + 1) * NG], row[:, c * P:(c + 1) * P], k.ident[0:NG, 0:NG])
                ins.then_inc(s_turn, 1)
                pe.wait_ge(s_dve, 7)
                pe.matmul(k.psum[:, 3, 0:NT * NH], k.tri[:], z[:, 0].rearrange("p c h -> p (c h)"), start=True, stop=True)
                pe.matmul(k.psum[:, 4, 0:NT * NH], k.ones[:], z[:, 0].rearrange("p c h -> p (c h)"),
                          start=True, stop=True).then_inc(s_sum, 1)

            @block.vector
            def _(dve):
                def done(ins, n):
                    ins.then_inc(s_dve, 1)
                    dve.wait_ge(s_dve, n)

                dve.wait_ge(s_hi, 1)
                dve.tensor_tensor(wlo[:, :, 0:NG], raw[:, :, P - NG:P], whi[:, :, 0:NG].bitcast(F32), ALU.subtract)
                dve.tensor_tensor(wlo[:, :, NG:P], raw[:, :, 0:P - NG], whi[:, :, NG:P].bitcast(F32), ALU.subtract).then_inc(s_lo, 1)
                dve.wait_ge(s_turn, 1)
                done(dve.tensor_copy(col[:], k.psum[:, 2, 0:NT * NG].rearrange("p (c g) -> p c g", g=NG)), 1)
                bias = par[:, 1, :].unsqueeze(1).broadcast_to([P, NT, NH])
                done(dve.tensor_tensor(z[:, 0], col[:, :, 0:NH], bias, ALU.add), 2)
                done(dve.scalar_tensor_tensor(out=z[:, 1], in0=z[:, 0], scalar=-1.0, in1=z[:, 0], op0=ALU.mult, op1=ALU.max), 3)
                done(dve.tensor_scalar(z[:, 5], z[:, 0], 0.0, None, ALU.max), 4)
                dve.wait_ge(s_act, 4)
                done(dve.tensor_tensor(z[:, 6], z[:, 5], z[:, 3], ALU.add), 5)
                done(dve.tensor_scalar(z[:, 7, 1, :], z[:, 7, 0, :], -1.0, None, ALU.mult), 6)
                done(dve.tensor_tensor(z[:, 0], z[:, 6], z[:, 7, 1, :].unsqueeze(1).broadcast_to([P, NT, NH]), ALU.mult), 7)
                dve.wait_ge(s_sum, 1)
                done(dve.tensor_copy(small[:, 0], k.psum[:, 3, 0:NT * NH].rearrange("p (c h) -> p c h", h=NH)), 8)
                done(dve.tensor_copy(z[:, 5], k.psum[:, 4, 0:NT * NH].rearrange("p (c h) -> p c h", h=NH)), 9)
                done(dve.tensor_tensor(z[:, 6], z[:, 5], small[:, 0], ALU.subtract), 10)
                dve.wait_ge(s_act, 5)
                dve.tensor_tensor(small[:, 2], z[:, 4], small[:, 1], ALU.mult)


def stage_gdn_normalise(k, qkv):
    nc = k.nc
    s_sq, s_sum, s_log, s_exp, s_use = (k.sem("len_" + n) for n in ("sq", "sum", "log", "exp", "use"))
    with ExitStack() as tmp:
        sq = tmp.enter_context(nc.sbuf_tensor("len_sq", [P, 2, SEQ], F32))
        r = tmp.enter_context(nc.sbuf_tensor("len_r", [P, 2 * NH, SEQ], F32))
        n = 2 * NH
        with nc.Block() as block:
            @block.vector
            def _(dve):
                for m in range(n):
                    if m >= 2:
                        dve.wait_ge(s_sum, 2 * (m - 1))
                    dve.tensor_tensor(sq[:, m % 2, :], qkv[:, m, :], qkv[:, m, :], ALU.mult).then_inc(s_sq, 1)
                for m in range(n):
                    dve.wait_ge(s_exp, m + 1)
                    dve.tensor_tensor(qkv[:, m, :], qkv[:, m, :], r[:, m, :], ALU.mult)

            @block.tensor
            def _(pe):
                for m in range(n):
                    pe.wait_ge(s_sq, m + 1)
                    for half in range(2):
                        b = 2 * m + half
                        if b >= 8:
                            pe.wait_ge(s_log, b - 7)
                        pe.matmul(k.psum[:, b % 8, :], k.ones[:], sq[:, m % 2, half * BANK:(half + 1) * BANK],
                                  start=True, stop=True).then_inc(s_sum, 1)

            @block.scalar
            def _(act):
                for b in range(2 * n):
                    m, half = b // 2, b % 2
                    act.wait_ge(s_sum, b + 1)
                    is_q = m < NH
                    act.activation(r[:, m, half * BANK:(half + 1) * BANK], k.psum[:, b % 8, :], ACT.Ln,
                                   scale=float(HD) if is_q else 1.0,
                                   bias=k.eps[:, 1:2] if is_q else k.eps[:, 0:1]).then_inc(s_log, 1)
                act.wait_ge(s_log, 2 * n)
                for m in range(n):
                    act.activation(r[:, m, :], r[:, m, :], ACT.Exp, scale=-0.5).then_inc(s_exp, 1)


def stage_gdn_scan(k, qkv, small, o, ssq):
    nc = k.nc
    names = ("staged", "spread", "grams", "natural", "shifted", "decay", "masked", "eg", "lt", "prep", "seed",
             "y", "yout", "dd", "grown", "uw", "uwout", "ws", "vnew", "outs", "delta", "state", "oout", "step", "passed")
    s = {n: k.sem("gscan_" + n) for n in names}
    with ExitStack() as tmp:
        t = lambda name, n=DG: tmp.enter_context(nc.sbuf_tensor("gscan_" + name, [P, n], F32))
        kc, qc, vc, egb, dec, decb, lt, at, qd, x, xt, y = (
            t(n) for n in ("kc", "qc", "vc", "egb", "dec", "decb", "lt", "at", "qd", "x", "xt", "y"))
        kw, kd, vb, state = (t(n) for n in ("kw", "kd", "vb", "state"))
        u, w, vn = y, egb, decb
        junk = t("junk", HD)
        sc = t("sc", 5 * NH)
        scol = sc[:].rearrange("p (j h) -> p j h", h=NH)
        ps = k.psum
        hs = lambda ap, h: ap[:, h * P:(h + 1) * P]
        both = lambda ap, p: ap[:, p * 2 * P:(p + 1) * 2 * P]
        pairs2 = lambda ap: ap.rearrange("p (h t) -> p h t", h=2)
        GROW = 2 * LEVELS
        with nc.Block() as block:
            @block.vector
            def _(dve):
                dve.memset(state[:], 0.0).then_inc(s["state"], NH)

                def chunk(c):
                    base = c * 4

                    def own(ins, n):
                        ins.then_inc(s["step"], 1)
                        dve.wait_ge(s["step"], base + n)

                    span = bass.ds(c * P, P)
                    dve.wait_ge(s["outs"], c + 1)
                    dve.wait_ge(s["state"], (c + 1) * NH)
                    dve.tensor_copy(heads(qc[:]), qkv[:, 0:NH, span])
                    dve.tensor_copy(heads(kc[:]), qkv[:, NH:2 * NH, span])
                    dve.tensor_copy(heads(vc[:]), qkv[:, 2 * NH:3 * NH, span])
                    dve.tensor_copy(scol, small[:, :, bass.ds(c, 1), :].rearrange("p j o h -> p j (o h)")).then_inc(s["staged"], 1)
                    dve.wait_ge(s["spread"], c + 1)
                    own(dve.tensor_tensor(heads(dec[:]), heads(ps[:, 0, :]), over_tokens(scol[:, 0, :]), ALU.subtract), 1)
                    dve.tensor_tensor(heads(dec[:]), heads(dec[:]), over_heads(k.future[:]), ALU.add).then_inc(s["shifted"], 1)
                    dve.tensor_copy(heads(x[:]), over_heads(k.ident[:]))
                    dve.tensor_copy(heads(xt[:]), over_heads(k.ident[:])).then_inc(s["step"], 1)
                    dve.wait_ge(s["eg"], c + 1)
                    dve.tensor_tensor(qd[:], qc[:], egb[:], ALU.mult).then_inc(s["step"], 1)
                    dve.wait_ge(s["decay"], c + 1)
                    own(dve.tensor_tensor(decb[:], dec[:], ps[:, 1, :], ALU.mult), 4)
                    dve.wait_ge(s["grams"], c + 1)
                    dve.scalar_tensor_tensor(out=lt[:], in0=ps[:, 2, :], scalar=-1.0, in1=decb[:], op0=ALU.mult,
                                             op1=ALU.mult).then_inc(s["lt"], 1)
                    dve.tensor_tensor(at[:], ps[:, 3, :], dec[:], ALU.mult)
                    dve.wait_ge(s["natural"], c + 1)
                    dve.tensor_tensor(heads(kw[:]), heads(ps[:, 4, :]), over_tokens(scol[:, 2, :]), ALU.mult)
                    dve.tensor_tensor(heads(kd[:]), heads(ps[:, 4, :]), over_tokens(scol[:, 3, :]), ALU.mult)
                    dve.tensor_tensor(heads(vb[:]), heads(ps[:, 5, :]), over_tokens(scol[:, 1, :]), ALU.mult).then_inc(s["prep"], 1)
                    dve.wait_ge(s["lt"], c + 1)
                    for p in range(2):
                        alone(dve, s["passed"])
                        dve.copy_predicated(pairs2(both(xt, p)), k.mask[:, 0, :].bitcast(U32).unsqueeze(1).broadcast_to([P, 2, P]),
                                            pairs2(both(lt, p)))
                        dve.wait_ge(s["y"], c * GROW + p + 1)
                        alone(dve, s["passed"])
                        dve.copy_predicated(pairs2(both(x, p)), k.maskT[:, 0, :].bitcast(U32).unsqueeze(1).broadcast_to([P, 2, P]),
                                            pairs2(ps[:, 6 + p, 0:2 * P])).then_inc(s["grown"], 1)
                    for lv in range(1, LEVELS):
                        for p in range(2):
                            dve.wait_ge(s["dd"], c * (GROW - 2) + 2 * (lv - 1) + p + 1)
                            alone(dve, s["passed"])
                            if lv < LEVELS - 1:
                                dve.copy_predicated(pairs2(both(x, p)),
                                                    k.maskT[:, lv, :].bitcast(U32).unsqueeze(1).broadcast_to([P, 2, P]),
                                                    pairs2(ps[:, 4 + p, 0:2 * P]))
                            dve.copy_predicated(pairs2(both(xt, p)),
                                                k.mask[:, lv, :].bitcast(U32).unsqueeze(1).broadcast_to([P, 2, P]),
                                                pairs2(ps[:, 4 + p, 2 * P:4 * P])).then_inc(s["grown"], 1)
                    dve.wait_ge(s["uwout"], c + 1)
                    dve.wait_ge(s["ws"], c + 2)
                    dve.tensor_tensor(vn[:], u[:], ps[:, 2, :], ALU.subtract).then_inc(s["vnew"], 1)
                    dve.wait_ge(s["delta"], c + 1)
                    for h in range(NH):
                        dve.scalar_tensor_tensor(out=hs(state, h), in0=hs(state, h), scalar=scol[:, 4, h:h + 1],
                                                 in1=hs(ps[:, 4, :], h), op0=ALU.mult, op1=ALU.add).then_inc(s["state"], 1)

                with dve.Fori(0, NT) as c:
                    chunk(c)

            @block.scalar
            def _(act):
                def chunk(c):
                    act.wait_ge(s["ws"], c + 1)
                    act.wait_ge(s["shifted"], c + 1)
                    act.activation(egb[:], ps[:, 0, :], ACT.Exp).then_inc(s["eg"], 1)
                    act.activation(dec[:], dec[:], ACT.Exp).then_inc(s["decay"], 1)
                    for lv in range(1, LEVELS):
                        for p in range(2):
                            act.wait_ge(s["y"], c * GROW + 2 * lv + p + 1)
                            act.activation(both(y, p), ps[:, 6 + p, 0:2 * P], ACT.Copy).then_inc(s["yout"], 1)
                    act.wait_ge(s["uw"], c + 1)
                    act.activation(w[:], ps[:, 1, :], ACT.Copy)
                    act.activation(u[:], ps[:, 0, :], ACT.Copy).then_inc(s["uwout"], 1)
                    act.wait_ge(s["outs"], c + 2)
                    act.activation(o[:, bass.ds(c, 1), :].rearrange("p o n -> p (o n)"), ps[:, 3, :], ACT.Copy)
                    for h in range(NH):
                        ins = act.activation(junk[:], hs(ps[:, 3, :], h), ACT.Square, accum_out=ssq[:, bass.ds(c * NH + h, 1)])
                        ins.then_inc(s["oout"], 1)
                        act.wait_ge(s["oout"], (c + 1) * NH + h + 1)

                prime(act, s["oout"], NH)
                with act.Fori(0, NT) as c:
                    chunk(c)

            @block.tensor
            def _(pe):
                def chunk(c):
                    pe.wait_ge(s["staged"], c + 1)
                    pe.wait_ge(s["oout"], (c + 1) * NH)
                    for h in range(NH):
                        pe.transpose(hs(ps[:, 0, :], h), scol[:, 0, h:h + 1].to_broadcast([P, P]), k.ident[:])
                    for h in range(NH):
                        ins = pe.transpose(hs(ps[:, 1, :], h), scol[:, 1, h:h + 1].to_broadcast([P, P]), k.ident[:])
                    ins.then_inc(s["spread"], 1)
                    for h in range(NH):
                        pe.matmul(hs(ps[:, 2, :], h), hs(kc, h), hs(kc, h), start=True, stop=True)
                        ins = pe.matmul(hs(ps[:, 3, :], h), hs(kc, h), hs(qc, h), start=True, stop=True)
                    ins.then_inc(s["grams"], 1)
                    for h in range(NH):
                        pe.transpose(hs(ps[:, 4, :], h), hs(kc, h), k.ident[:])
                        ins = pe.transpose(hs(ps[:, 5, :], h), hs(vc, h), k.ident[:])
                    ins.then_inc(s["natural"], 1)
                    pe.wait_ge(s["lt"], c + 1)
                    for lv in range(LEVELS):
                        for p in range(2):
                            if lv:
                                pe.wait_ge(s["grown"], c * GROW + 2 * (lv - 1) + p + 1)
                            for h in (2 * p, 2 * p + 1):
                                ins = pe.matmul(hs(ps[:, 6 + p, :], h - 2 * p), hs(lt, h), hs(x, h) if lv else k.ident[:], start=True, stop=True)
                            ins.then_inc(s["y"], 1)
                        if lv == 0:
                            pe.wait_ge(s["prep"], c + 1)
                            continue
                        for p in range(2):
                            pe.wait_ge(s["yout"], c * (GROW - 2) + 2 * (lv - 1) + p + 1)
                            for h in (2 * p, 2 * p + 1):
                                if lv < LEVELS - 1:
                                    pe.matmul(hs(ps[:, 4 + p, :], h - 2 * p), hs(xt, h), hs(y, h), start=True, stop=True)
                                ins = pe.matmul(hs(ps[:, 4 + p, :], h - 2 * p + 2), hs(y, h), hs(xt, h), start=True, stop=True)
                            ins.then_inc(s["dd"], 1)
                    pe.wait_ge(s["grown"], (c + 1) * GROW)
                    for h in range(NH):
                        pe.matmul(hs(ps[:, 0, :], h), hs(xt, h), hs(vb, h), start=True, stop=True)
                        ins = pe.matmul(hs(ps[:, 1, :], h), hs(kw, h), hs(xt, h), start=True, stop=True)
                    ins.then_inc(s["uw"], 1)
                    pe.wait_ge(s["uwout"], c + 1)
                    pe.wait_ge(s["state"], (c + 1) * NH)
                    for h in range(NH):
                        ins = pe.matmul(hs(ps[:, 2, :], h), hs(w, h), hs(state, h), start=True, stop=True)
                    ins.then_inc(s["ws"], 1)
                    pe.wait_ge(s["vnew"], c + 1)
                    for h in range(NH):
                        pe.matmul(hs(ps[:, 3, :], h), hs(qd, h), hs(state, h), start=True, stop=False)
                        ins = pe.matmul(hs(ps[:, 3, :], h), hs(at, h), hs(vn, h), start=False, stop=True)
                    ins.then_inc(s["outs"], 1)
                    for h in range(NH):
                        ins = pe.matmul(hs(ps[:, 4, :], h), hs(kd, h), hs(vn, h), start=True, stop=True)
                    ins.then_inc(s["delta"], 1)

                prime(pe, s["outs"])
                prime(pe, s["ws"])
                with pe.Fori(0, NT) as c:
                    chunk(c)


def stage_gate_outputs(k, name, o, ssq, mix, at):
    nc = k.nc
    rooted, inverted = k.sem(name + "_rooted"), k.sem(name + "_inverted")
    with ExitStack() as tmp:
        r = tmp.enter_context(nc.sbuf_tensor(name + "_r", [P, 2, NT * NH], F32))
        with nc.Block() as block:
            @block.scalar
            def _(act):
                act.activation(r[:, 0, :], ssq[:], ACT.Sqrt, bias=k.eps[:, 0:1], scale=1.0 / HD).then_inc(rooted, 1)

            @block.vector
            def _(dve):
                dve.wait_ge(rooted, 1)
                dve.reciprocal(r[:, 1, :], r[:, 0, :]).then_inc(inverted, 1)
                dve.wait_ge(inverted, 1)
                for c in range(NT):
                    for h in range(NH):
                        dst = mix[:, c, at + h * P:at + (h + 1) * P]
                        dve.scalar_tensor_tensor(out=dst, in0=o[:, c, h * P:(h + 1) * P],
                                                 scalar=r[:, 1, c * NH + h:c * NH + h + 1], in1=dst,
                                                 op0=ALU.mult, op1=ALU.mult)


def stage_hgrn_project(k, hi, lo, w_in, q, f):
    nc = k.nc
    for name, dst, func, first_col in (("hq", q, ACT.Silu, 0), ("hf", f, ACT.Sigmoid, DG)):
        with ExitStack() as tmp:
            g = Turned(k, name, tmp, hi, lo, 2, NH // 2, lambda i, u, first_col=first_col: slab(w_in, DM, (2 * i + u) * P + first_col))
            with nc.Block() as block:
                @block.sync
                def _(sp):
                    g.load(sp)

                @block.tensor
                def _(pe):
                    g.multiply(pe)

                @block.scalar
                def _(act):
                    g.round(act, 0, 0, first=True)
                    g.round(act, 0, 1, first=True)

                    def pair(i, more):
                        for u in range(2):
                            for half in range(2):
                                act.wait_ge(g.summed, (2 * i + u) * 2 + half + 1)
                                act.activation(dst[:, bass.ds(2 * i + u, 1), half * BANK:(half + 1) * BANK]
                                               .rearrange("p o t -> p (o t)"), g.bank(u, half), func).then_inc(g.taken, 1)
                            if more:
                                g.round(act, i + 1, u)

                    g.each_pair(act, pair)

                @block.vector
                def _(dve):
                    for i in range(NH // 2):
                        for u in range(2):
                            g.remainder(dve, i, u)


def stage_hgrn_decay(k, f, kk, b):
    nc = k.nc
    bounded, logged = k.sem("hdecay_bounded"), k.sem("hdecay_logged")
    with ExitStack() as tmp:
        keep = tmp.enter_context(nc.sbuf_tensor("hdecay_keep", [P, SEQ], F32))
        with nc.Block() as block:
            @block.vector
            def _(dve):
                for h in range(NH):
                    dve.tensor_scalar(f[:, h, :], f[:, h, :], k.lb[:, NH + h:NH + h + 1], k.lb[:, h:h + 1],
                                      ALU.mult, ALU.add).then_inc(bounded, 1)
                dve.memset(keep[:], 1.0).then_inc(bounded, 1)
                dve.wait_ge(bounded, NH + 1)
                dve.memset(keep[:].rearrange("p (c t) -> p c t", t=P)[:, :, 0:1], 0.0).then_inc(bounded, 1)
                for h in range(NH):
                    dve.tensor_scalar(kk[:, h, :], f[:, h, :], -1.0, 1.0, ALU.mult, ALU.add).then_inc(bounded, 1)
                dve.wait_ge(bounded, NH + 2)
                for h in range(NH):
                    dve.wait_ge(logged, h + 1)
                    dve.tensor_tensor_scan(b[:, h, :], keep[:], f[:, h, :], 0.0, ALU.mult, ALU.add)

            @block.scalar
            def _(act):
                for h in range(NH):
                    act.wait_ge(bounded, NH + 3 + h)
                    act.activation(f[:, h, :], f[:, h, :], ACT.Ln).then_inc(logged, 1)


def stage_hgrn_scan(k, q, kk, b, v, o, ssq):
    nc = k.nc
    names = ("staged", "late", "early", "expd", "qs", "ks", "level", "placed", "edge", "edged", "qkd",
             "turned", "natural", "outs", "delta", "state", "oout", "passed", "zero")
    s = {n: k.sem("hscan_" + n) for n in names}
    with ExitStack() as tmp:
        t = lambda name, n=DG: tmp.enter_context(nc.sbuf_tensor("hscan_" + name, [P, n], F32))
        bc, kc, qc, vc, sc, qd, kdt, kd, state, e0, e1 = (
            t(n) for n in ("bc", "kc", "qc", "vc", "sc", "qd", "kdt", "kd", "state", "e0", "e1"))
        ed = [t(f"ed{i}") for i in range(2)]
        ql = [t(f"ql{i}") for i in range(LEVELS)]
        kl = [t(f"kl{i}") for i in range(LEVELS)]
        junk = t("junk", HD)
        elast = t("elast", NH)
        ps = k.psum
        hs = lambda ap, h: ap[:, h * P:(h + 1) * P]

        def half(ap, m, side):
            return ap[:].rearrange("p (n two m) -> p n two m", two=2, m=m)[:, :, side, :]

        def middle(m):
            v4 = bc[:].rearrange("p (n two m) -> p n two m", two=2, m=m)[:, :, 0, m - 1:m]
            return v4.broadcast_to([P, DG // (2 * m), m])

        with nc.Block() as block:
            @block.vector
            def _(dve):
                dve.memset(state[:], 0.0).then_inc(s["state"], NH)
                for i in range(LEVELS):
                    dve.memset(ql[i][:], 0.0)
                    dve.memset(kl[i][:], 0.0)
                dve.memset(sc[:], 0.0).then_inc(s["zero"], 1)
                dve.wait_ge(s["zero"], 1)

                def chunk(c):
                    span = bass.ds(c * P, P)
                    dve.wait_ge(s["delta"], c + 1)
                    dve.wait_ge(s["placed"], c * (LEVELS + 1) + 1)
                    dve.tensor_copy(heads(bc[:]), b[:, :, span])
                    dve.tensor_copy(heads(qc[:]), q[:, :, span])
                    dve.tensor_copy(heads(kc[:]), kk[:, :, span])
                    dve.tensor_copy(vc[:], v[:, bass.ds(c, 1), :].rearrange("p o n -> p (o n)")).then_inc(s["staged"], 1)
                    dve.wait_ge(s["staged"], c + 1)
                    dve.tensor_tensor(heads(e1[:]), heads(bc[:])[:, :, P - 1:P].broadcast_to([P, NH, P]),
                                      heads(bc[:]), ALU.subtract).then_inc(s["edge"], 1)

                    def differences(lv):
                        m = 1 << lv
                        if lv >= 2:
                            dve.wait_ge(s["qs"], c * LEVELS + lv - 1)
                            dve.wait_ge(s["ks"], c * LEVELS + lv - 1)
                        dve.tensor_tensor(half(ed[lv % 2], m, 1), half(bc, m, 1), middle(m), ALU.subtract)
                        dve.tensor_tensor(half(ed[lv % 2], m, 0), middle(m), half(bc, m, 0), ALU.subtract).then_inc(s["late"], 1)

                    def place(lv, mask):
                        dve.wait_ge(s["level"], c * (LEVELS + 1) + lv + 1)
                        dve.wait_ge(s["placed"], c * (LEVELS + 1) + lv + 1)
                        alone(dve, s["passed"])
                        dve.copy_predicated(heads(sc[:]), over_heads(mask.bitcast(U32)),
                                            heads(ps[:, lv % 4, :])).then_inc(s["placed"], 1)

                    differences(0)
                    differences(1)
                    dve.wait_ge(s["edged"], c + 1)
                    dve.tensor_tensor(qd[:], qc[:], e0[:], ALU.mult)
                    dve.tensor_tensor(kdt[:], kc[:], e1[:], ALU.mult).then_inc(s["qkd"], 1)
                    for lv in range(LEVELS):
                        m = 1 << lv
                        dve.wait_ge(s["expd"], c * LEVELS + lv + 1)
                        dve.tensor_tensor(half(kl[lv], m, 0), half(kc, m, 0), half(ed[lv % 2], m, 0), ALU.mult).then_inc(s["ks"], 1)
                        if lv + 2 < LEVELS:
                            differences(lv + 2)
                        if lv:
                            place(lv - 1, k.mask[:, lv - 1, :])
                    place(LEVELS - 1, k.mask[:, LEVELS - 1, :])
                    place(LEVELS, k.ident[:])
                    dve.wait_ge(s["delta"], c + 2)
                    for h in range(NH):
                        dve.scalar_tensor_tensor(out=hs(state, h), in0=hs(state, h), scalar=elast[:, h:h + 1],
                                                 in1=hs(ps[:, 6, :], h), op0=ALU.mult, op1=ALU.add).then_inc(s["state"], 1)

                prime(dve, s["placed"])
                with dve.Fori(0, NT) as c:
                    chunk(c)

            @block.gpsimd
            def _(pool):
                pool.wait_ge(s["zero"], 1)

                def chunk(c):
                    pool.wait_ge(s["staged"], c + 1)
                    for lv in range(LEVELS):
                        m = 1 << lv
                        pool.wait_ge(s["expd"], c * LEVELS + lv + 1)
                        pool.tensor_tensor(half(ql[lv], m, 1), half(qc, m, 1), half(ed[lv % 2], m, 1), ALU.mult).then_inc(s["qs"], 1)

                with pool.Fori(0, NT) as c:
                    chunk(c)

            @block.scalar
            def _(act):
                def chunk(c):
                    act.wait_ge(s["edge"], c + 1)
                    act.wait_ge(s["state"], (c + 1) * NH)
                    act.activation(e0[:], bc[:], ACT.Exp)
                    act.activation(elast[:], heads(bc[:])[:, :, P - 1], ACT.Exp)
                    act.activation(e1[:], e1[:], ACT.Exp).then_inc(s["edged"], 1)
                    for lv in range(LEVELS):
                        act.wait_ge(s["late"], c * LEVELS + lv + 1)
                        act.activation(ed[lv % 2][:], ed[lv % 2][:], ACT.Exp).then_inc(s["expd"], 1)
                    act.wait_ge(s["turned"], c + 1)
                    act.activation(kd[:], ps[:, 4, :], ACT.Copy).then_inc(s["natural"], 1)
                    act.wait_ge(s["outs"], c + 2)
                    act.activation(o[:, bass.ds(c, 1), :].rearrange("p o n -> p (o n)"), ps[:, 5, :], ACT.Copy)
                    for h in range(NH):
                        act.activation(junk[:], hs(ps[:, 5, :], h), ACT.Square,
                                       accum_out=ssq[:, bass.ds(c * NH + h, 1)]).then_inc(s["oout"], 1)
                        act.wait_ge(s["oout"], (c + 1) * NH + h + 1)

                prime(act, s["oout"], NH)
                with act.Fori(0, NT) as c:
                    chunk(c)

            @block.tensor
            def _(pe):
                def chunk(c):
                    pe.wait_ge(s["qkd"], c + 1)
                    for h in range(NH):
                        ins = pe.transpose(hs(ps[:, 4, :], h), hs(kdt, h), k.ident[:])
                    ins.then_inc(s["turned"], 1)
                    for lv in range(LEVELS + 1):
                        if lv < LEVELS:
                            pe.wait_ge(s["qs"], c * LEVELS + lv + 1)
                            pe.wait_ge(s["ks"], c * LEVELS + lv + 1)
                        if lv >= 4:
                            pe.wait_ge(s["placed"], c * (LEVELS + 1) + lv - 2)
                        for h in range(NH):
                            a, bq = (kl[lv], ql[lv]) if lv < LEVELS else (kc, qc)
                            ins = pe.matmul(hs(ps[:, lv % 4, :], h), hs(a, h), hs(bq, h), start=True, stop=True)
                        ins.then_inc(s["level"], 1)
                    pe.wait_ge(s["placed"], (c + 1) * (LEVELS + 1) + 1)
                    pe.wait_ge(s["natural"], c + 1)
                    pe.wait_ge(s["oout"], (c + 1) * NH)
                    for h in range(NH):
                        pe.matmul(hs(ps[:, 5, :], h), hs(qd, h), hs(state, h), start=True, stop=False)
                        ins = pe.matmul(hs(ps[:, 5, :], h), hs(sc, h), hs(vc, h), start=False, stop=True)
                    ins.then_inc(s["outs"], 1)
                    for h in range(NH):
                        ins = pe.matmul(hs(ps[:, 6, :], h), hs(kd, h), hs(vc, h), start=True, stop=True)
                    ins.then_inc(s["delta"], 1)

                prime(pe, s["outs"])
                prime(pe, s["delta"])
                with pe.Fori(0, NT) as c:
                    chunk(c)


def stage_add_normed(k, name, x, tiles, y, weight_row, out=None):
    nc = k.nc
    n = len(tiles)
    loaded, squared, rooted, inverted, scaled, added, stored = (
        k.sem(name + s) for s in ("_loaded", "_squared", "_rooted", "_inverted", "_scaled", "_added", "_stored"))
    with ExitStack() as tmp:
        stat = tmp.enter_context(nc.sbuf_tensor(name + "_stat", [P, 3, NT], F32))
        junk = tmp.enter_context(nc.sbuf_tensor(name + "_junk", [P, DM], F32))
        wrow = tmp.enter_context(nc.sbuf_tensor(name + "_w", [P, DM], F32))
        with nc.Block() as block:
            @block.sync
            def _(sp):
                sp.dma_start(wrow[:], weight_row.partition_broadcast(P)).then_inc(loaded, 16)
                if out is not None:
                    for i, t in enumerate(tiles):
                        sp.wait_ge(added, i + 1)
                        sp.dma_start(out[t * P:(t + 1) * P, :], x[:, t, :]).then_inc(stored, 16)
                    sp.wait_ge(stored, 16 * n)

            @block.scalar
            def _(act):
                for i in range(n):
                    if i:
                        act.wait_ge(squared, i)
                    act.activation(junk[:], y[:, i, :], ACT.Square, accum_out=stat[:, 0, i:i + 1]).then_inc(squared, 1)
                act.wait_ge(squared, n)
                act.activation(stat[:, 1, 0:n], stat[:, 0, 0:n], ACT.Sqrt, bias=k.eps[:, 0:1],
                               scale=1.0 / DM).then_inc(rooted, 1)

            @block.vector
            def _(dve):
                dve.wait_ge(rooted, 1)
                dve.reciprocal(stat[:, 2, 0:n], stat[:, 1, 0:n]).then_inc(inverted, 1)
                dve.wait_ge(inverted, 1)
                dve.wait_ge(loaded, 16)
                for i in range(n):
                    dve.scalar_tensor_tensor(out=y[:, i, :], in0=y[:, i, :], scalar=stat[:, 2, i:i + 1], in1=wrow[:],
                                             op0=ALU.mult, op1=ALU.mult).then_inc(scaled, 1)
                    if i:
                        dve.wait_ge(scaled, i)
                        dve.tensor_tensor(x[:, tiles[i - 1], :], x[:, tiles[i - 1], :], y[:, i - 1, :], ALU.add).then_inc(added, 1)
                dve.wait_ge(scaled, n)
                dve.tensor_tensor(x[:, tiles[n - 1], :], x[:, tiles[n - 1], :], y[:, n - 1, :], ALU.add).then_inc(added, 1)


def stage_ffn_up(k, name, part, hi, lo, w_up, halo, ghi, glo):
    nc = k.nc
    freed, tapped, smooth, gated, split, edge = (
        k.sem(name + s) for s in ("_freed", "_tapped", "_smooth", "_gated", "_split", "_edge"))
    pad = FK - 1
    with ExitStack() as tmp:
        g = Turned(k, name, tmp, hi, lo, 1, FT, lambda i, u: slab(w_up, DM, i * P + u * DFF))
        line = [tmp.enter_context(nc.sbuf_tensor(f"{name}_line{u}", [P, pad + HALF], F32)) for u in range(2)]
        acc = [tmp.enter_context(nc.sbuf_tensor(f"{name}_acc{u}", [P, HALF], F32)) for u in range(2)]
        act_out = tmp.enter_context(nc.sbuf_tensor(name + "_silu", [P, HALF], F32))
        with nc.Block() as block:
            @block.sync
            def _(sp):
                g.load(sp)

            @block.tensor
            def _(pe):
                g.multiply(pe)

            @block.scalar
            def _(act):
                g.round(act, 0, 0, first=True)
                g.round(act, 0, 1, first=True)

                def pair(i, more):
                    for u in range(2):
                        act.wait_ge(freed, 2 * i + u + 1)
                        act.wait_ge(g.summed, 2 * i + u + 1)
                        act.activation(line[u][:, pad:pad + HALF], g.bank(u, 0), ACT.Copy).then_inc(g.taken, 1)
                        if more:
                            g.round(act, i + 1, u)
                        act.wait_ge(freed, 2 * i + u + 3)
                        if u == 0:
                            act.activation(act_out[:], acc[0][:], ACT.Silu).then_inc(smooth, 1)
                        else:
                            act.wait_ge(gated, i + 1)
                            act.activation(ghi[:, bass.ds(i, 1), :].rearrange("p o t -> p (o t)"), acc[1][:],
                                           ACT.Copy).then_inc(split, 1)

                prime(act, smooth)
                prime(act, split)
                g.each_pair(act, pair)

            @block.vector
            def _(dve):
                for u in range(2):
                    dve.memset(line[u][:, 0:pad], 0.0).then_inc(freed, 1)
                for u in range(2):
                    g.remainder(dve, 0, u)

                def pair(i, more):
                    for u in range(2):
                        tap = lambda q: k.cols[:, bass.ds(i + (C_FCONV + q * 2 * FT + u * FT), 1)]
                        kept = halo[:, bass.ds(i + u * FT, 1), :].rearrange("p o t -> p (o t)")
                        n = 2 * i + u
                        dve.wait_ge(g.taken, n + 1)
                        if part == 0:
                            dve.tensor_copy(kept, line[u][:, HALF:HALF + pad]).then_inc(edge, 1)
                        else:
                            dve.tensor_copy(line[u][:, 0:pad], kept).then_inc(edge, 1)
                            dve.wait_ge(edge, n + 1)
                        if u == 0:
                            dve.wait_ge(smooth, i + 1)
                        else:
                            dve.wait_ge(split, i + 1)
                        dve.tensor_scalar(acc[u][:], line[u][:, 0:HALF], tap(0), None, ALU.mult).then_inc(tapped, 1)
                        for q in range(1, FK):
                            dve.wait_ge(tapped, n * (FK - 1) + q)
                            dve.scalar_tensor_tensor(out=acc[u][:], in0=line[u][:, q:q + HALF], scalar=tap(q), in1=acc[u][:],
                                                     op0=ALU.mult, op1=ALU.add).then_inc(freed if q == FK - 1 else tapped, 1)
                        if more:
                            g.remainder(dve, i + 1, u)
                    dve.wait_ge(smooth, i + 2)
                    dve.wait_ge(freed, 2 * i + 4)
                    dve.tensor_tensor(acc[1][:], acc[1][:], act_out[:], ALU.mult).then_inc(gated, 1)
                    dve.wait_ge(split, i + 2)
                    here = (slice(None), bass.ds(i, 1), slice(None))
                    dve.tensor_tensor(glo[here].rearrange("p o t -> p (o t)"), acc[1][:],
                                          ghi[here].bitcast(F32).rearrange("p o t -> p (o t)"), ALU.subtract)

                g.each_pair(dve, pair)


def build(nc, a, out):
    w_in, w_up, w_down, w_out = a["w_in"][0], a["w_up"][0], a["w_down"][0], a["w_out"][0]
    x_rows = a["x"][0].rearrange("(t p) d -> p t d", p=P)
    with ExitStack() as ctx:
        k = Kit(nc, ctx)
        stage_setup(k, a)

        def load(name, dst, src, n):
            s = k.sem(name)
            with nc.Block() as block:
                @block.sync
                def _(sp):
                    for t in range(n):
                        sp.dma_start(dst[:, t, :], src[:, t, :]).then_inc(s, 16)
                    sp.wait_ge(s, 16 * n)

        with ExitStack() as mixing:
            mix = mixing.enter_context(nc.sbuf_tensor("mix", [P, NT, DM], F32))
            with ExitStack() as heads_on:
                big = heads_on.enter_context(nc.sbuf_tensor("big", [P, 3 * NH, SEQ], F32))
                with ExitStack() as first:
                    hi = first.enter_context(nc.sbuf_tensor("h_hi", [P, KT, SEQ], F32R))
                    lo = first.enter_context(nc.sbuf_tensor("h_lo", [P, KT, SEQ], F32R))
                    load("x_loaded", mix, x_rows, NT)
                    stage_rms(k, "pre", mix, list(range(NT)), mix)
                    stage_turn(k, "hturn", mix, list(range(NT)), hi, lo, lambda kt: k.cols[:, C_MIXPRE + kt:C_MIXPRE + kt + 1])
                    gate_cols = (3 * DG, 7 * DG)
                    stage_natural(k, "gates", hi, lo, NT, KT,
                                  lambda g, kt: w_in[kt * P:(kt + 1) * P, gate_cols[g]:gate_cols[g] + DG], DG, 2,
                                  lambda act, g, t, n, b: act.activation(mix[:, t, g * DG:(g + 1) * DG], k.psum[:, b, :], ACT.Silu))
                    stage_gdn_project(k, hi, lo, w_in, big)
                    with ExitStack() as gdn:
                        small = gdn.enter_context(nc.sbuf_tensor("gdn_small", [P, 5, NT, NH], F32))
                        ssq = gdn.enter_context(nc.sbuf_tensor("gdn_ssq", [P, NT * NH], F32))
                        stage_gdn_gates(k, hi, lo, w_in, a["gdn_a_log"][0], a["gdn_dt_bias"][0], small)
                        stage_gdn_normalise(k, big)
                        og = gdn.enter_context(nc.sbuf_tensor("gdn_o", [P, NT, DG], F32))
                        stage_gdn_scan(k, big, small, og, ssq)
                        stage_gate_outputs(k, "gout", og, ssq, mix, DG)
                    k.recycle()
                    q, f = big[:, 0:NH, :], big[:, NH:2 * NH, :]
                    v = big[:, 2 * NH:3 * NH, :].rearrange("p h t -> p (h t)").rearrange("p (c n) -> p c n", n=DG)
                    stage_natural(k, "values", hi, lo, NT, KT,
                                  lambda g, kt: w_in[kt * P:(kt + 1) * P, 2 * DG:3 * DG], DG, 1,
                                  lambda act, g, t, n, b: act.activation(v[:, t, :], k.psum[:, b, :], ACT.Copy))
                    stage_hgrn_project(k, hi, lo, w_in, q, f)
                kk = heads_on.enter_context(nc.sbuf_tensor("hgrn_k", [P, NH, SEQ], F32))
                b = heads_on.enter_context(nc.sbuf_tensor("hgrn_b", [P, NH, SEQ], F32))
                oh = heads_on.enter_context(nc.sbuf_tensor("hgrn_o", [P, NT, DG], F32))
                hssq = heads_on.enter_context(nc.sbuf_tensor("hgrn_ssq", [P, NT * NH], F32))
                stage_hgrn_decay(k, f, kk, b)
                stage_hgrn_scan(k, q, kk, b, v, oh, hssq)
                stage_gate_outputs(k, "hout", oh, hssq, mix, 0)
            x = None
            with ExitStack() as outp:
                mhi = outp.enter_context(nc.sbuf_tensor("m_hi", [P, KT, SEQ], F32R))
                mlo = outp.enter_context(nc.sbuf_tensor("m_lo", [P, KT, SEQ], F32R))
                stage_turn(k, "mturn", mix, list(range(NT)), mhi, mlo,
                           lambda kt: k.cols[:, C_HNORM:C_HNORM + 1] if kt < NH else k.cols[:, C_GNORM:C_GNORM + 1])
                y = outp.enter_context(nc.sbuf_tensor("mix_y", [P, NT, DM], F32))
                stage_natural(k, "outp", mhi, mlo, NT, KT,
                              lambda g, kt: w_out[kt * P:(kt + 1) * P, g * BANK:(g + 1) * BANK], BANK, 2,
                              lambda act, g, t, n, b: act.activation(y[:, t, g * BANK:(g + 1) * BANK], k.psum[:, b, :], ACT.Copy))
                x = mix
                load("x_again", x, x_rows, NT)
                stage_add_normed(k, "mixpost", x, list(range(NT)), y, a["mix_norm_post"][0])

            halo = mixing.enter_context(nc.sbuf_tensor("ffn_halo", [P, 2 * FT, FK - 1], F32))
            for part in range(2):
                k.recycle()
                tiles = list(range(part * 4, part * 4 + 4))
                with ExitStack() as ffn:
                    fhi = ffn.enter_context(nc.sbuf_tensor(f"f_hi{part}", [P, KT, HALF], F32R))
                    flo = ffn.enter_context(nc.sbuf_tensor(f"f_lo{part}", [P, KT, HALF], F32R))
                    with ExitStack() as tmp:
                        xn = tmp.enter_context(nc.sbuf_tensor(f"f_xn{part}", [P, 4, DM], F32))
                        stage_rms(k, f"fpre{part}", x, tiles, xn)
                        stage_turn(k, f"fturn{part}", xn, list(range(4)), fhi, flo,
                                   lambda kt: k.cols[:, C_FFNPRE + kt:C_FFNPRE + kt + 1])
                    ghi = ffn.enter_context(nc.sbuf_tensor(f"g_hi{part}", [P, FT, HALF], F32R))
                    glo = ffn.enter_context(nc.sbuf_tensor(f"g_lo{part}", [P, FT, HALF], F32R))
                    stage_ffn_up(k, f"up{part}", part, fhi, flo, w_up, halo, ghi, glo)
                    fy = ffn.enter_context(nc.sbuf_tensor(f"f_y{part}", [P, 4, DM], F32))
                    stage_natural(k, f"down{part}", ghi, glo, 4, FT,
                                  lambda g, kt: w_down[kt * P:(kt + 1) * P, :], DM, 1,
                                  lambda act, g, t, n, b: act.activation(fy[:, t, n * BANK:(n + 1) * BANK], k.psum[:, b, :], ACT.Copy))
                    stage_add_normed(k, f"ffnpost{part}", x, tiles, fy, a["ffn_norm_post"][0])

            k.recycle()
            with ExitStack() as ple:
                s = lambda name, shape, dt=F32: ple.enter_context(nc.sbuf_tensor(name, shape, dt))
                xhi, xlo = s("x_hi", [P, KT, SEQ], F32R), s("x_lo", [P, KT, SEQ], F32R)
                phi, plo = s("p_hi", [P, 2, SEQ], F32R), s("p_lo", [P, 2, SEQ], F32R)
                e, pe_rows = s("ple_e", [P, NT, DM]), s("p_rows", [P, NT, DPLE])
                load("p_loaded", pe_rows, a["p"][0, 0].rearrange("(t p) d -> p t d", p=P), NT)
                stage_turn(k, "pturn", pe_rows, list(range(NT)), phi, plo, lambda kt: None, n_k=2)
                stage_turn(k, "xturn", x, list(range(NT)), xhi, xlo, lambda kt: None)
                stage_natural(k, "pgate", xhi, xlo, NT, KT,
                              lambda g, kt: a["w_ple_gate"][0, kt * P:(kt + 1) * P, g * BANK:(g + 1) * BANK], BANK, 2,
                              lambda act, g, t, n, b: act.activation(e[:, t, g * BANK:(g + 1) * BANK], k.psum[:, b, :], ACT.Sigmoid))
                pv = s("ple_pv", [P, NT, BANK])
                for g2 in range(2):
                    stage_natural(k, f"pvals{g2}", phi, plo, NT, 2,
                                  lambda g, kt, g2=g2: a["w_ple"][0, kt * P:(kt + 1) * P, g2 * BANK:(g2 + 1) * BANK], BANK, 1,
                                  lambda act, g, t, n, b: act.activation(pv[:, t, :], k.psum[:, b, :], ACT.Copy))
                    with nc.Block() as block:
                        @block.vector
                        def _(dve):
                            for t in range(NT):
                                half = e[:, t, g2 * BANK:(g2 + 1) * BANK]
                                dve.tensor_tensor(half, half, pv[:, t, :], ALU.mult)
                stage_add_normed(k, "plepost", x, list(range(NT)), e, a["ple_norm_post"][0], out=out[0])


_INS = ["x", "p", "mix_norm_pre", "mix_norm_post", "w_in", "hgrn_lb_logits", "hgrn_out_norm", "gdn_conv",
        "gdn_a_log", "gdn_dt_bias", "gdn_out_norm", "w_out", "ffn_norm_pre", "ffn_norm_post", "w_up", "ffn_conv",
        "w_down", "w_ple", "w_ple_gate", "ple_norm_post"]


def kernel(**inputs):
    from concourse import bacc
    from concourse.bass_utils import run_bass_kernel_spmd

    nc = bacc.Bacc("TRN2", target_bir_lowering=False, num_devices=1)
    arrays, args = {}, {}
    for name in _INS:
        v = np.ascontiguousarray(inputs[name])
        arrays["in_" + name] = v
        args[name] = nc.dram_tensor("in_" + name, v.shape, mybir.dt.from_np(v.dtype), kind="ExternalInput").ap()
    out = nc.dram_tensor("out", (1, SEQ, DM), F32, kind="ExternalOutput").ap()
    build(nc, args, out)
    r = run_bass_kernel_spmd(nc, [arrays], core_ids=[0])
    return r.results[0]["out"]
```

```python
from contextlib import ExitStack

import numpy as np

import concourse.bass as bass
from concourse import mybir

F32 = mybir.dt.float32
F32R = mybir.dt.float32r
U32 = mybir.dt.uint32
ALU = mybir.AluOpType
ACT = mybir.ActivationFunctionType

P = 128
SEQ = 1024
DM = 1024
HD = 128
NH = 4
DG = NH * HD
DIN = 8 * DG + 2 * NH
DFF = 2816
DPLE = 256
EPS = 1e-6
NT = SEQ // P
KT = DM // P
FT = DFF // P
GK, FK = 4, 3
LEVELS = 7
HALF = SEQ // 2
BANK = 512

C_MIXPRE = 0
C_FFNPRE = C_MIXPRE + KT
C_HNORM = C_FFNPRE + KT
C_GNORM = C_HNORM + 1
C_LB = C_GNORM + 1
C_GCONV = C_LB + 2 * NH
C_FCONV = C_GCONV + GK * 3 * NH
N_ROWS = C_FCONV
N_COLS = C_FCONV + FK * 2 * FT


class Kit:

    def __init__(self, nc, ctx):
        self.nc, self.ctx = nc, ctx
        self.psum = ctx.enter_context(nc.psum_tensor("psum", [P, 8, BANK], F32))
        c = lambda name, shape: ctx.enter_context(nc.sbuf_tensor(name, shape, F32))
        self.ident = c("ident", [P, P])
        self.ones = c("ones", [P, P])
        self.tri = c("tri", [P, P])
        self.future = c("future", [P, P])
        self.mask = c("mask", [P, LEVELS, P])
        self.maskT = c("maskT", [P, LEVELS, P])
        self.cols = c("cols", [P, N_COLS])
        self.eps = c("eps", [P, 2])
        self.lb = c("lb", [P, 2 * NH])

        self.spare = c("spare", [P, 1])
        self.sems = []

    def table(self, act, func):
        act.activation(self.spare[:], self.eps[:, 0:1], func)

    def sem(self, name):
        self.sems.append(self.nc.alloc_semaphore(name))
        return self.sems[-1]

    def recycle(self):
        self.nc.clear_and_free_semaphores(self.sems)
        self.nc.all_engine_barrier()
        self.sems = []


def alone(eng, passed):
    eng.sem_inc(passed, 1)


def prime(eng, sem, n=1):
    eng.sem_inc(sem, n)


def over_heads(ap):
    return ap.unsqueeze(1).broadcast_to([P, NH, ap.shape[1]])


def over_tokens(ap, n=P):
    return ap.unsqueeze(2).broadcast_to([P, ap.shape[1], n])


def heads(ap):
    return ap.rearrange("p (h t) -> p h t", h=NH)


def stage_setup(k, params):
    nc = k.nc
    made, loaded, turned, kept, soft = (k.sem("setup_" + n) for n in ("made", "loaded", "turned", "kept", "soft"))
    with ExitStack() as tmp:
        rows = tmp.enter_context(nc.sbuf_tensor("param_rows", [P, P], F32))
        frows = tmp.enter_context(nc.sbuf_tensor("ffn_conv_rows", [P, 2, P], F32))
        sm = tmp.enter_context(nc.sbuf_tensor("bound_work", [P, 6, NH], F32))
        half = FK * 2 * FT // 2
        with nc.Block() as block:
            @block.sync
            def _(sp):
                n = 0
                for at, src in ((C_MIXPRE, params["mix_norm_pre"].rearrange("o (r c) -> (o r) c", c=P)),
                                (C_FFNPRE, params["ffn_norm_pre"].rearrange("o (r c) -> (o r) c", c=P)),
                                (C_HNORM, params["hgrn_out_norm"]),
                                (C_GNORM, params["gdn_out_norm"]),
                                (C_LB, params["hgrn_lb_logits"].rearrange("o (r c) -> (o r) c", c=P)),
                                (C_GCONV, params["gdn_conv"].rearrange("o k (r c) -> (o k r) c", c=P))):
                    sp.dma_start(rows[at:at + src.shape[0], :], src).then_inc(loaded, 16)
                    n += 16
                fsrc = params["ffn_conv"].rearrange("o k (r c) -> (o k r) c", c=P)
                for i in range(2):
                    sp.dma_start(frows[0:half, i, :], fsrc[i * half:(i + 1) * half, :]).then_inc(loaded, 16)
                    n += 16
                assert n == 128

            @block.gpsimd
            def _(pool):
                step = 0

                def kept_step(ins):
                    ins.then_inc(made, 1)
                    pool.wait_ge(made, step)

                for t, v in ((k.ident, 0.0), (k.ones, 1.0), (k.tri, 1.0), (k.future, 0.0), (k.mask, 0.0), (k.maskT, 0.0)):
                    step += 1
                    pool.memset(t[:], v).then_inc(made, 1)
                step += 2
                pool.memset(k.eps[:, 0:1], EPS).then_inc(made, 1)
                pool.memset(k.eps[:, 1:2], HD * EPS).then_inc(made, 1)
                for lv in range(LEVELS):
                    m = 1 << lv
                    for t, side in ((k.mask, 1), (k.maskT, 0)):
                        step += 1
                        if step == 9:
                            pool.wait_ge(made, 8)
                        v = t[:, lv, :].rearrange("p (n two m) -> p n two m", two=2, m=m)[:, :, side, :]
                        pool.memset(v, 1.0).then_inc(made, 1)
                pool.wait_ge(made, step)
                step += 1
                kept_step(pool.affine_select(out=k.ident[:], in_=k.ident[:], pattern=[[-1, P]],
                                             compare_op=ALU.not_equal, fill=1.0, base=0, channel_multiplier=1))
                step += 1
                kept_step(pool.affine_select(out=k.tri[:], in_=k.tri[:], pattern=[[1, P]],
                                             compare_op=ALU.is_ge, fill=0.0, base=0, channel_multiplier=-1))
                step += 1
                kept_step(pool.affine_select(out=k.future[:], in_=k.future[:], pattern=[[1, P]],
                                             compare_op=ALU.is_ge, fill=-1e30, base=0, channel_multiplier=-1))
                for lv in range(LEVELS):
                    m = 1 << lv
                    n = P // (2 * m)
                    for t, side in ((k.mask, 1), (k.maskT, 0)):
                        v = t[:, lv, :].rearrange("p (n two m) -> p n two m", two=2, m=m)[:, :, side, :]
                        lowest = 0 if side else m
                        step += 1
                        kept_step(pool.affine_select(out=v, in_=v, pattern=[[-2 * m, n], [0, m]],
                                                     compare_op=ALU.is_ge, fill=0.0, base=-lowest,
                                                     channel_multiplier=1))
                        step += 1
                        kept_step(pool.affine_select(out=v, in_=v, pattern=[[2 * m, n], [0, m]],
                                                     compare_op=ALU.is_ge, fill=0.0, base=lowest + m - 1,
                                                     channel_multiplier=-1))

            @block.tensor
            def _(pe):
                pe.wait_ge(made, 8 + 2 * LEVELS + 1)
                pe.wait_ge(loaded, 128)
                pe.transpose(k.psum[:, 0, 0:N_ROWS], rows[0:N_ROWS, :], k.ident[0:N_ROWS, 0:N_ROWS]).then_inc(turned, 1)
                for i in range(2):
                    pe.transpose(k.psum[:, 1 + i, 0:half], frows[0:half, i, :],
                                 k.ident[0:half, 0:half]).then_inc(turned, 1)

            @block.vector
            def _(dve):
                dve.wait_ge(turned, 3)
                dve.tensor_copy(k.cols[:, 0:N_ROWS], k.psum[:, 0, 0:N_ROWS]).then_inc(kept, 1)
                for i in range(2):
                    at = C_FCONV + i * half
                    dve.tensor_copy(k.cols[:, at:at + half], k.psum[:, 1 + i, 0:half]).then_inc(kept, 1)
                dve.wait_ge(kept, 3)
                l0, l1 = k.cols[:, C_LB:C_LB + NH], k.cols[:, C_LB + NH:C_LB + 2 * NH]
                dve.tensor_tensor(sm[:, 0, :], l0, l1, ALU.max).then_inc(kept, 1)
                dve.wait_ge(kept, 4)
                dve.tensor_tensor(sm[:, 1, :], l0, sm[:, 0, :], ALU.subtract)
                dve.tensor_tensor(sm[:, 2, :], l1, sm[:, 0, :], ALU.subtract).then_inc(kept, 1)
                dve.wait_ge(soft, 1)
                dve.tensor_tensor(sm[:, 5, :], sm[:, 3, :], sm[:, 4, :], ALU.add).then_inc(kept, 1)
                dve.wait_ge(kept, 6)
                dve.reciprocal(sm[:, 0, :], sm[:, 5, :]).then_inc(kept, 1)
                dve.wait_ge(kept, 7)
                dve.tensor_tensor(k.lb[:, 0:NH], sm[:, 3, :], sm[:, 0, :], ALU.mult).then_inc(kept, 1)
                dve.wait_ge(kept, 8)
                dve.tensor_scalar(k.lb[:, NH:2 * NH], k.lb[:, 0:NH], -1.0, 1.0, ALU.mult, ALU.add)

            @block.scalar
            def _(act):
                act.wait_ge(kept, 5)
                act.activation(sm[:, 3:5, :], sm[:, 1:3, :], ACT.Exp).then_inc(soft, 1)


def stage_rms(k, name, src, tiles, dst):
    nc = k.nc
    n = len(tiles)
    squared, rooted, inverted = (k.sem(name + s) for s in ("_squared", "_rooted", "_inverted"))
    with ExitStack() as tmp:
        stat = tmp.enter_context(nc.sbuf_tensor(name + "_stat", [P, 3, NT], F32))
        junk = tmp.enter_context(nc.sbuf_tensor(name + "_junk", [P, DM], F32))
        with nc.Block() as block:
            @block.scalar
            def _(act):
                for i, t in enumerate(tiles):
                    if i:
                        act.wait_ge(squared, i)
                    act.activation(junk[:], src[:, t, :], ACT.Square, accum_out=stat[:, 0, i:i + 1]).then_inc(squared, 1)
                act.wait_ge(squared, n)
                act.activation(stat[:, 1, 0:n], stat[:, 0, 0:n], ACT.Sqrt, bias=k.eps[:, 0:1],
                               scale=1.0 / DM).then_inc(rooted, 1)

            @block.vector
            def _(dve):
                dve.wait_ge(rooted, 1)
                dve.reciprocal(stat[:, 2, 0:n], stat[:, 1, 0:n]).then_inc(inverted, 1)
                dve.wait_ge(inverted, 1)
                for i, t in enumerate(tiles):
                    dve.tensor_scalar(dst[:, i, :], src[:, t, :], stat[:, 2, i:i + 1], None, ALU.mult)


def stage_turn(k, name, src, tiles, hi, lo, scale, n_k=KT):
    nc = k.nc
    turned, rounded, rest = (k.sem(name + s) for s in ("_turned", "_rounded", "_rest"))
    quads = [(kt, q) for kt in range(n_k) for q in range(len(tiles) // 4)]
    with nc.Block() as block:
        @block.tensor
        def _(pe):
            for j, (kt, q) in enumerate(quads):
                if j >= 8:
                    pe.wait_ge(rest, j - 7)
                for i in range(4):
                    ins = pe.transpose(k.psum[:, j % 8, i * P:(i + 1) * P],
                                       src[:, tiles[4 * q + i], kt * P:(kt + 1) * P], k.ident[:])
                ins.then_inc(turned, 1)

        @block.scalar
        def _(act):
            for j, (kt, q) in enumerate(quads):
                act.wait_ge(turned, j + 1)
                s = scale(kt)
                act.activation(hi[:, kt, q * BANK:(q + 1) * BANK], k.psum[:, j % 8, :], ACT.Copy,
                               scale=1.0 if s is None else s).then_inc(rounded, 1)

        @block.vector
        def _(dve):
            for j, (kt, q) in enumerate(quads):
                dve.wait_ge(rounded, j + 1)
                s = scale(kt)
                dve.scalar_tensor_tensor(out=lo[:, kt, q * BANK:(q + 1) * BANK], in0=k.psum[:, j % 8, :],
                                         scalar=1.0 if s is None else s,
                                         in1=hi[:, kt, q * BANK:(q + 1) * BANK].bitcast(F32),
                                         op0=ALU.mult, op1=ALU.subtract).then_inc(rest, 1)


def stage_natural(k, name, hi, lo, t_tiles, n_k, weight, width, groups, take):
    nc = k.nc
    parts = width // BANK
    banks = t_tiles * parts
    RING = 2
    arrived = [k.sem(f"{name}_arrived{i}") for i in range(RING)]
    rounded, rest, summed, taken = (k.sem(name + s) for s in ("_rounded", "_rest", "_summed", "_taken"))
    slabs = [(g, kt) for g in range(groups) for kt in range(n_k)]
    with ExitStack() as tmp:
        raw = tmp.enter_context(nc.sbuf_tensor(name + "_raw", [P, RING, width], F32))
        whi = tmp.enter_context(nc.sbuf_tensor(name + "_whi", [P, RING, width], F32R))
        wlo = tmp.enter_context(nc.sbuf_tensor(name + "_wlo", [P, RING, width], F32R))
        with nc.Block() as block:
            @block.sync
            def _(sp):
                for j, (g, kt) in enumerate(slabs):
                    if j >= RING:
                        sp.wait_ge(rest, j - RING + 1)
                    sp.dma_start(raw[:, j % RING, :], weight(g, kt)).then_inc(arrived[j % RING], 16)

            @block.scalar
            def _(act):
                def out_of_banks(g):
                    for b in range(banks):
                        act.wait_ge(summed, ((g + 1) * n_k - 1) * banks + b + 1)
                        take(act, g, b // parts, b % parts, b).then_inc(taken, 1)

                for j, (g, kt) in enumerate(slabs):
                    act.wait_ge(arrived[j % RING], 16 * (j // RING + 1))
                    if j >= RING:
                        act.wait_ge(summed, (j - RING + 1) * banks)
                    act.activation(whi[:, j % RING, :], raw[:, j % RING, :], ACT.Copy).then_inc(rounded, 1)
                    if kt == 0 and g:
                        out_of_banks(g - 1)
                out_of_banks(groups - 1)

            @block.vector
            def _(dve):
                for j in range(len(slabs)):
                    dve.wait_ge(rounded, j + 1)
                    dve.tensor_tensor(wlo[:, j % RING, :], raw[:, j % RING, :],
                                      whi[:, j % RING, :].bitcast(F32), ALU.subtract).then_inc(rest, 1)

            @block.tensor
            def _(pe):
                for j, (g, kt) in enumerate(slabs):
                    pe.wait_ge(rest, j + 1)
                    r = j % RING
                    for b in range(banks):
                        t, n = b // parts, b % parts
                        if kt == 0 and g:
                            pe.wait_ge(taken, (g - 1) * banks + b + 1)
                        out = k.psum[:, b, :]
                        ah, al = hi[:, kt, t * P:(t + 1) * P], lo[:, kt, t * P:(t + 1) * P]
                        wh, wl = whi[:, r, n * BANK:(n + 1) * BANK], wlo[:, r, n * BANK:(n + 1) * BANK]
                        pe.matmul(out, ah, wh, start=(kt == 0), stop=False)
                        pe.matmul(out, ah, wl, start=False, stop=False)
                        pe.matmul(out, al, wh, start=False, stop=(kt == n_k - 1)).then_inc(summed, 1)


class Turned:

    def __init__(self, k, name, tmp, hi, lo, halves, pairs, weight):
        nc = k.nc
        self.k, self.hi, self.lo, self.halves, self.pairs, self.weight = k, hi, lo, halves, pairs, weight
        self.arrived = [k.sem(f"{name}_arrived{i}") for i in range(2)]
        self.rounded, self.rest, self.summed, self.taken = (
            k.sem(name + s) for s in ("_rounded", "_rest", "_summed", "_taken"))
        self.raw = tmp.enter_context(nc.sbuf_tensor(name + "_raw", [P, 2, KT, P], F32))
        self.whi = [tmp.enter_context(nc.sbuf_tensor(f"{name}_whi{u}", [P, KT, P], F32R)) for u in range(2)]
        self.wlo = [tmp.enter_context(nc.sbuf_tensor(f"{name}_wlo{u}", [P, KT, P], F32R)) for u in range(2)]

    def load(self, sp, first=True, rest=True):
        def pair(i, first=False):
            for u in range(2):
                if not first:
                    sp.wait_ge(self.rest, 2 * i + u - 1)
                sp.dma_start(self.raw[:, u, :, :], self.weight(i, u)).then_inc(self.arrived[u], 16)

        if first:
            pair(0, first=True)
        if rest and self.pairs > 1:
            with sp.Fori(1, self.pairs) as i:
                pair(i)

    def round(self, act, i, u, first=False):
        act.wait_ge(self.arrived[u], i * 16 + 16)
        if not first:
            act.wait_ge(self.summed, (2 * i + u - 1) * self.halves)
        act.activation(self.whi[u][:], self.raw[:, u, :, :], ACT.Copy).then_inc(self.rounded, 1)

    def remainder(self, dve, i, u):
        dve.wait_ge(self.rounded, 2 * i + u + 1)
        dve.tensor_tensor(self.wlo[u][:], self.raw[:, u, :, :], self.whi[u][:].bitcast(F32),
                          ALU.subtract).then_inc(self.rest, 1)

    def bank(self, u, half):
        return self.k.psum[:, u * self.halves + half, :]

    def multiply(self, pe):
        def pair(i, first=False):
            for u in range(2):
                pe.wait_ge(self.rest, 2 * i + u + 1)
                for half in range(self.halves):
                    if not first:
                        pe.wait_ge(self.taken, (2 * i + u - 2) * self.halves + half + 1)
                    out = self.bank(u, half)
                    for kt in range(KT):
                        ah = self.hi[:, kt, half * BANK:(half + 1) * BANK]
                        al = self.lo[:, kt, half * BANK:(half + 1) * BANK]
                        pe.matmul(out, self.whi[u][:, kt, :], ah, start=(kt == 0), stop=False)
                        pe.matmul(out, self.whi[u][:, kt, :], al, start=False, stop=False)
                        ins = pe.matmul(out, self.wlo[u][:, kt, :], ah, start=False, stop=(kt == KT - 1))
                    ins.then_inc(self.summed, 1)

        pair(0, first=True)
        if self.pairs > 1:
            with pe.Fori(1, self.pairs) as i:
                pair(i)

    def each_pair(self, eng, body):
        if self.pairs > 1:
            with eng.Fori(0, self.pairs - 1) as i:
                body(i, True)
        body(self.pairs - 1, False)


def slab(w, rows, at):
    return w[0:rows, bass.ds(at, P)].rearrange("(kt p) c -> p kt c", p=P)


def stage_gdn_project(k, hi, lo, w_in, qkv, gates, gate_rows):
    nc = k.nc
    freed, tapped, smooth, kept = (k.sem("gconv_" + n) for n in ("freed", "tapped", "smooth", "kept"))
    with ExitStack() as tmp:
        first_col = 4 * DG
        g = Turned(k, "gproj", tmp, hi, lo, 2, 3 * NH // 2, lambda i, u: slab(w_in, DM, (2 * i + u) * P + first_col))
        pad = GK - 1
        line = [tmp.enter_context(nc.sbuf_tensor(f"gconv_line{u}", [P, pad + SEQ], F32)) for u in range(2)]
        acc = [tmp.enter_context(nc.sbuf_tensor("gconv_acc", [P, SEQ], F32))] * 2
        with nc.Block() as block:
            @block.sync
            def _(sp):
                g.load(sp, rest=False)
                for t in range(NT):
                    sp.dma_start(gate_rows[t * P:(t + 1) * P, :], gates[:, t, :]).then_inc(kept, 16)
                g.load(sp, first=False)
                sp.wait_ge(kept, 16 * NT)

            @block.tensor
            def _(pe):
                g.multiply(pe)

            @block.scalar
            def _(act):
                k.table(act, ACT.Silu)
                g.round(act, 0, 0, first=True)
                g.round(act, 0, 1, first=True)

                def pair(i, more):
                    for u in range(2):
                        act.wait_ge(freed, 2 * i + u + 1)
                        for half in range(2):
                            act.wait_ge(g.summed, (2 * i + u) * 2 + half + 1)
                            act.activation(line[u][:, pad + half * BANK:pad + (half + 1) * BANK], g.bank(u, half),
                                           ACT.Copy).then_inc(g.taken, 1)
                        if more:
                            g.round(act, i + 1, u)
                        act.wait_ge(freed, 2 * i + u + 3)
                        act.activation(qkv[:, bass.ds(2 * i + u, 1), :].rearrange("p o t -> p (o t)"), acc[u][:],
                                       ACT.Silu).then_inc(smooth, 1)

                prime(act, smooth)
                g.each_pair(act, pair)

            @block.vector
            def _(dve):
                for u in range(2):
                    dve.memset(line[u][:, 0:pad], 0.0).then_inc(freed, 1)
                for u in range(2):
                    g.remainder(dve, 0, u)

                def pair(i, more):
                    for u in range(2):
                        tap = lambda q: k.cols[:, bass.ds(2 * i + u + (C_GCONV + q * 3 * NH), 1)]
                        dve.wait_ge(g.taken, (2 * i + u) * 2 + 2)
                        dve.wait_ge(smooth, 2 * i + u + 1)
                        dve.tensor_scalar(acc[u][:], line[u][:, 0:SEQ], tap(0), None, ALU.mult).then_inc(tapped, 1)
                        for q in range(1, GK):
                            dve.wait_ge(tapped, (2 * i + u) * (GK - 1) + q)
                            dve.scalar_tensor_tensor(out=acc[u][:], in0=line[u][:, q:q + SEQ], scalar=tap(q), in1=acc[u][:],
                                                     op0=ALU.mult, op1=ALU.add).then_inc(freed if q == GK - 1 else tapped, 1)
                        if more:
                            g.remainder(dve, i + 1, u)

                g.each_pair(dve, pair)


def stage_gdn_gates(k, hi, lo, w_in, a_log, dt_bias, small):
    nc = k.nc
    s_in, s_hi, s_lo, s_mm, s_row, s_turn, s_act, s_dve, s_sum = (
        k.sem("gate_" + n) for n in ("in", "hi", "lo", "mm", "row", "turn", "act", "dve", "sum"))
    NG = 2 * NH
    with ExitStack() as tmp:
        t = lambda name, shape, dt=F32: tmp.enter_context(nc.sbuf_tensor(name, shape, dt))
        raw, whi, wlo = t("gate_raw", [P, KT, P]), t("gate_whi", [P, KT, P], F32R), t("gate_wlo", [P, KT, P], F32R)
        row = t("gate_row", [NG, SEQ])
        par = t("gate_par", [P, 2, NH])
        z = t("gate_z", [P, 8, NT, NH])
        col = t("gate_col", [P, NT, NG])
        with nc.Block() as block:
            @block.sync
            def _(sp):
                sp.dma_start(raw[:], slab(w_in, DM, DIN - P)).then_inc(s_in, 16)
                sp.dma_start(par[:, 0, :], a_log.partition_broadcast(P)).then_inc(s_in, 16)
                sp.dma_start(par[:, 1, :], dt_bias.partition_broadcast(P)).then_inc(s_in, 16)

            @block.scalar
            def _(act):
                act.wait_ge(s_in, 48)
                act.activation(whi[:, :, 0:NG], raw[:, :, P - NG:P], ACT.Copy)
                act.activation(whi[:, :, NG:P], raw[:, :, 0:P - NG], ACT.Copy).then_inc(s_hi, 1)
                for half in range(2):
                    act.wait_ge(s_mm, half + 1)
                    act.activation(row[:, half * BANK:(half + 1) * BANK], k.psum[0:NG, half, :], ACT.Copy).then_inc(s_row, 1)
                act.wait_ge(s_dve, 3)
                act.activation(z[:, 2], z[:, 1], ACT.Exp, scale=-1.0).then_inc(s_act, 1)
                act.activation(z[:, 7, 0, :], par[:, 0, :], ACT.Exp).then_inc(s_act, 1)
                act.wait_ge(s_act, 2)
                act.activation(z[:, 3], z[:, 2], ACT.Ln, bias=1.0).then_inc(s_act, 1)
                act.activation(small[:, 1], col[:, :, NH:NG], ACT.Sigmoid).then_inc(s_act, 1)
                act.wait_ge(s_dve, 10)
                act.activation(z[:, 4], small[:, 0], ACT.Exp).then_inc(s_act, 1)
                act.activation(small[:, 3], z[:, 6], ACT.Exp)
                act.activation(small[:, 4], z[:, 5], ACT.Exp)

            @block.tensor
            def _(pe):
                pe.wait_ge(s_lo, 1)
                for half in range(2):
                    for kt in range(KT):
                        ah = hi[:, kt, half * BANK:(half + 1) * BANK]
                        al = lo[:, kt, half * BANK:(half + 1) * BANK]
                        pe.matmul(k.psum[:, half, :], whi[:, kt, :], ah, start=(kt == 0), stop=False)
                        pe.matmul(k.psum[:, half, :], whi[:, kt, :], al, start=False, stop=False)
                        ins = pe.matmul(k.psum[:, half, :], wlo[:, kt, :], ah, start=False, stop=(kt == KT - 1))
                    ins.then_inc(s_mm, 1)
                pe.wait_ge(s_row, 2)
                for c in range(NT):
                    ins = pe.transpose(k.psum[:, 2, c * NG:(c + 1) * NG], row[:, c * P:(c + 1) * P], k.ident[0:NG, 0:NG])
                ins.then_inc(s_turn, 1)
                pe.wait_ge(s_dve, 7)
                pe.matmul(k.psum[:, 3, 0:NT * NH], k.tri[:], z[:, 0].rearrange("p c h -> p (c h)"), start=True, stop=True)
                pe.matmul(k.psum[:, 4, 0:NT * NH], k.ones[:], z[:, 0].rearrange("p c h -> p (c h)"),
                          start=True, stop=True).then_inc(s_sum, 1)

            @block.vector
            def _(dve):
                def done(ins, n):
                    ins.then_inc(s_dve, 1)
                    dve.wait_ge(s_dve, n)

                dve.wait_ge(s_hi, 1)
                dve.tensor_tensor(wlo[:, :, 0:NG], raw[:, :, P - NG:P], whi[:, :, 0:NG].bitcast(F32), ALU.subtract)
                dve.tensor_tensor(wlo[:, :, NG:P], raw[:, :, 0:P - NG], whi[:, :, NG:P].bitcast(F32), ALU.subtract).then_inc(s_lo, 1)
                dve.wait_ge(s_turn, 1)
                done(dve.tensor_copy(col[:], k.psum[:, 2, 0:NT * NG].rearrange("p (c g) -> p c g", g=NG)), 1)
                bias = par[:, 1, :].unsqueeze(1).broadcast_to([P, NT, NH])
                done(dve.tensor_tensor(z[:, 0], col[:, :, 0:NH], bias, ALU.add), 2)
                done(dve.scalar_tensor_tensor(out=z[:, 1], in0=z[:, 0], scalar=-1.0, in1=z[:, 0], op0=ALU.mult, op1=ALU.max), 3)
                done(dve.tensor_scalar(z[:, 5], z[:, 0], 0.0, None, ALU.max), 4)
                dve.wait_ge(s_act, 4)
                done(dve.tensor_tensor(z[:, 6], z[:, 5], z[:, 3], ALU.add), 5)
                done(dve.tensor_scalar(z[:, 7, 1, :], z[:, 7, 0, :], -1.0, None, ALU.mult), 6)
                done(dve.tensor_tensor(z[:, 0], z[:, 6], z[:, 7, 1, :].unsqueeze(1).broadcast_to([P, NT, NH]), ALU.mult), 7)
                dve.wait_ge(s_sum, 1)
                done(dve.tensor_copy(small[:, 0], k.psum[:, 3, 0:NT * NH].rearrange("p (c h) -> p c h", h=NH)), 8)
                done(dve.tensor_copy(z[:, 5], k.psum[:, 4, 0:NT * NH].rearrange("p (c h) -> p c h", h=NH)), 9)
                done(dve.tensor_tensor(z[:, 6], z[:, 5], small[:, 0], ALU.subtract), 10)
                dve.wait_ge(s_act, 5)
                dve.tensor_tensor(small[:, 2], z[:, 4], small[:, 1], ALU.mult)


def stage_gdn_normalise(k, qkv, r):
    nc = k.nc
    s_sq, s_sum, s_log, s_exp, s_use = (k.sem("len_" + n) for n in ("sq", "sum", "log", "exp", "use"))
    with ExitStack() as tmp:
        sq = tmp.enter_context(nc.sbuf_tensor("len_sq", [P, 2, SEQ], F32))
        n = 2 * NH
        with nc.Block() as block:
            @block.vector
            def _(dve):
                for m in range(n):
                    if m >= 2:
                        dve.wait_ge(s_sum, 2 * (m - 1))
                    dve.tensor_tensor(sq[:, m % 2, :], qkv[:, m, :], qkv[:, m, :], ALU.mult).then_inc(s_sq, 1)
                for m in range(n):
                    dve.wait_ge(s_exp, m + 1)
                    dve.tensor_tensor(qkv[:, m, :], qkv[:, m, :], r[:, m, :], ALU.mult)

            @block.tensor
            def _(pe):
                for m in range(n):
                    pe.wait_ge(s_sq, m + 1)
                    for half in range(2):
                        b = 2 * m + half
                        if b >= 8:
                            pe.wait_ge(s_log, b - 7)
                        pe.matmul(k.psum[:, b % 8, :], k.ones[:], sq[:, m % 2, half * BANK:(half + 1) * BANK],
                                  start=True, stop=True).then_inc(s_sum, 1)

            @block.scalar
            def _(act):
                for b in range(2 * n):
                    m, half = b // 2, b % 2
                    act.wait_ge(s_sum, b + 1)
                    is_q = m < NH
                    act.activation(r[:, m, half * BANK:(half + 1) * BANK], k.psum[:, b % 8, :], ACT.Ln,
                                   scale=float(HD) if is_q else 1.0,
                                   bias=k.eps[:, 1:2] if is_q else k.eps[:, 0:1]).then_inc(s_log, 1)
                act.wait_ge(s_log, 2 * n)
                for m in range(n):
                    act.activation(r[:, m, :], r[:, m, :], ACT.Exp, scale=-0.5).then_inc(s_exp, 1)


def stage_hgrn_project(k, hi, lo, w_in, q, f):
    nc = k.nc
    for name, dst, func, first_col in (("hq", q, ACT.Silu, 0), ("hf", f, ACT.Sigmoid, DG)):
        with ExitStack() as tmp:
            g = Turned(k, name, tmp, hi, lo, 2, NH // 2, lambda i, u, first_col=first_col: slab(w_in, DM, (2 * i + u) * P + first_col))
            with nc.Block() as block:
                @block.sync
                def _(sp):
                    g.load(sp)

                @block.tensor
                def _(pe):
                    g.multiply(pe)

                @block.scalar
                def _(act):
                    g.round(act, 0, 0, first=True)
                    g.round(act, 0, 1, first=True)

                    def pair(i, more):
                        for u in range(2):
                            for half in range(2):
                                act.wait_ge(g.summed, (2 * i + u) * 2 + half + 1)
                                act.activation(dst[:, bass.ds(2 * i + u, 1), half * BANK:(half + 1) * BANK]
                                               .rearrange("p o t -> p (o t)"), g.bank(u, half), func).then_inc(g.taken, 1)
                            if more:
                                g.round(act, i + 1, u)

                    g.each_pair(act, pair)

                @block.vector
                def _(dve):
                    for i in range(NH // 2):
                        for u in range(2):
                            g.remainder(dve, i, u)


def stage_hgrn_decay(k, f, kk):
    nc = k.nc
    bounded, logged = k.sem("hdecay_bounded"), k.sem("hdecay_logged")
    with ExitStack() as tmp:
        keep = tmp.enter_context(nc.sbuf_tensor("hdecay_keep", [P, SEQ], F32))
        with nc.Block() as block:
            @block.vector
            def _(dve):
                for h in range(NH):
                    dve.tensor_scalar(f[:, h, :], f[:, h, :], k.lb[:, NH + h:NH + h + 1], k.lb[:, h:h + 1],
                                      ALU.mult, ALU.add).then_inc(bounded, 1)
                dve.memset(keep[:], 1.0).then_inc(bounded, 1)
                dve.wait_ge(bounded, NH + 1)
                dve.memset(keep[:].rearrange("p (c t) -> p c t", t=P)[:, :, 0:1], 0.0).then_inc(bounded, 1)
                for h in range(NH):
                    dve.tensor_scalar(kk[:, h, :], f[:, h, :], -1.0, 1.0, ALU.mult, ALU.add).then_inc(bounded, 1)
                dve.wait_ge(bounded, NH + 2)
                for h in range(NH):
                    dve.wait_ge(logged, h + 1)
                    dve.tensor_tensor_scan(f[:, h, :], keep[:], f[:, h, :], 0.0, ALU.mult, ALU.add)

            @block.scalar
            def _(act):
                for h in range(NH):
                    act.wait_ge(bounded, NH + 3 + h)
                    act.activation(f[:, h, :], f[:, h, :], ACT.Ln).then_inc(logged, 1)


def stage_scans(k, qkv, small, q, kk, b, v, o_rows, ssq):
    nc = k.nc
    g = {n: k.sem("g_" + n) for n in (
        "staged", "tiles", "spread", "kk", "qk", "vnat", "knat", "shifted", "decay", "eg", "weighed", "lt", "at",
        "factors", "seeded", "y", "yout", "dd", "grown", "uw", "uwout", "ws", "vnew", "outs", "delta", "state",
        "oout", "stored", "passed")}
    hg = {n: k.sem("h_" + n) for n in (
        "staged", "tiles", "late", "expd", "qs", "ks", "level", "placed", "edge", "edged", "qkd",
        "turned", "natural", "outs", "delta", "state", "oout", "zero", "stored")}
    with ExitStack() as tmp:
        t = lambda name, n=DG: tmp.enter_context(nc.sbuf_tensor(name, [P, n], F32))
        kc, qc, vc, egb, dec, decb, lt, at, qd, x, xt, y, kw, kd, vb, w, vn, state, og = (t("g_t_" + n) for n in (
            "kc", "qc", "vc", "egb", "dec", "decb", "lt", "at", "qd", "x", "xt", "y", "kw", "kd", "vb", "w", "vn",
            "state", "o"))
        u = y
        hb, hk, hq, hv, sc, hqd, hkdt, hkd, hstate, oh = (t("h_t_" + n) for n in (
            "b", "k", "q", "v", "scores", "qd", "kdt", "kd", "state", "o"))
        RING = 3
        ed = [t(f"h_t_ed{i}") for i in range(2)]
        ql = [t(f"h_t_ql{i}") for i in range(RING)]
        kl = [t(f"h_t_kl{i}") for i in range(RING)]
        gjunk, hjunk, elast, glast = t("g_t_junk", HD), t("h_t_junk", HD), t("h_t_elast", NH), t("g_t_last", NH)
        sc5 = t("g_t_cols", 5 * NH)
        scol = sc5[:].rearrange("p (j h) -> p j h", h=NH)
        ps = k.psum
        hs = lambda ap, h: ap[:, h * P:(h + 1) * P]
        both = lambda ap, p: ap[:, p * 2 * P:(p + 1) * 2 * P]
        pairs2 = lambda ap: ap.rearrange("p (h t) -> p h t", h=2)
        for_pair = lambda m: m.bitcast(U32).unsqueeze(1).broadcast_to([P, 2, P])
        row = lambda ap, c: ap[:, bass.ds(c, 1), :].rearrange("p o n -> p (o n)")
        GROW = 2 * LEVELS
        HL = LEVELS + 1
        NF = 4

        def half(ap, m, side):
            return ap[:].rearrange("p (n two m) -> p n two m", two=2, m=m)[:, :, side, :]

        def middle(m):
            v4 = hb[:].rearrange("p (n two m) -> p n two m", two=2, m=m)[:, :, 0, m - 1:m]
            return v4.broadcast_to([P, DG // (2 * m), m])

        with nc.Block() as block:
            @block.vector
            def _(dve):
                dve.memset(state[:], 0.0).then_inc(g["state"], NH)
                dve.memset(hstate[:], 0.0).then_inc(hg["state"], NH)
                for i in range(RING):
                    dve.memset(ql[i][:], 0.0)
                    dve.memset(kl[i][:], 0.0)
                dve.memset(sc[:], 0.0).then_inc(hg["zero"], 1)
                dve.wait_ge(hg["zero"], 1)
                prime(dve, hg["placed"])
                prime(dve, g["factors"], NF)

                def g_stage(c):
                    span = bass.ds(c * P, P)
                    dve.wait_ge(g["factors"], (c + 1) * NF)
                    dve.tensor_copy(scol, small[:, :, bass.ds(c, 1), :].rearrange("p j o h -> p j (o h)")).then_inc(g["staged"], 1)
                    dve.tensor_copy(heads(kc[:]), qkv[:, NH:2 * NH, span])
                    dve.tensor_copy(heads(vc[:]), qkv[:, 2 * NH:3 * NH, span])
                    dve.tensor_copy(heads(qc[:]), qkv[:, 0:NH, span]).then_inc(g["tiles"], 1)

                def g_identity(c):
                    dve.wait_ge(g["uw"], c + 1)
                    dve.tensor_copy(heads(x[:]), over_heads(k.ident[:]))
                    dve.tensor_copy(heads(xt[:]), over_heads(k.ident[:])).then_inc(g["seeded"], 1)

                def g_shift(c):
                    dve.wait_ge(g["spread"], c + 1)
                    for h in range(NH):
                        ins = dve.scalar_tensor_tensor(out=hs(dec, h), in0=hs(ps[:, 0, :], h), scalar=scol[:, 0, h:h + 1],
                                                       in1=k.future[:], op0=ALU.subtract, op1=ALU.add)
                    ins.then_inc(g["shifted"], 1)

                def g_weigh(c):
                    dve.wait_ge(g["decay"], c + 1)
                    dve.tensor_tensor(decb[:], dec[:], ps[:, 1, :], ALU.mult).then_inc(g["weighed"], 1)

                def factor(out, bank, j):
                    dve.tensor_tensor(heads(out[:]), heads(ps[:, bank, :]), over_tokens(scol[:, j, :]),
                                      ALU.mult).then_inc(g["factors"], 1)

                def main(c, more):
                    def h_differ(lv):
                        m = 1 << lv
                        if lv >= 2:
                            dve.wait_ge(hg["qs"], c * LEVELS + lv - 1)
                            dve.wait_ge(hg["ks"], c * LEVELS + lv - 1)
                        dve.tensor_tensor(half(ed[lv % 2], m, 1), half(hb, m, 1), middle(m), ALU.subtract)
                        dve.tensor_tensor(half(ed[lv % 2], m, 0), middle(m), half(hb, m, 0), ALU.subtract).then_inc(hg["late"], 1)

                    def h_place(n):
                        mask = k.mask[:, n - 1, :] if n else k.ident[:]
                        dve.wait_ge(hg["level"], c * HL + n + 1 + RING)
                        dve.wait_ge(hg["placed"], c * HL + n + 1)
                        alone(dve, g["passed"])
                        dve.copy_predicated(heads(sc[:]), over_heads(mask.bitcast(U32)),
                                            heads(ps[:, 6 + n % 2, :])).then_inc(hg["placed"], 1)

                    def g_grow(lv):
                        for p in range(2):
                            dve.wait_ge(g["dd"], c * (GROW - 2) + 2 * (lv - 1) + p + 1)
                            alone(dve, g["passed"])
                            if lv < LEVELS - 1:
                                dve.copy_predicated(pairs2(both(x, p)), for_pair(k.maskT[:, lv, :]), pairs2(ps[:, 2 + p, 0:2 * P]))
                            dve.copy_predicated(pairs2(both(xt, p)), for_pair(k.mask[:, lv, :]),
                                                pairs2(ps[:, 2 + p, 2 * P:4 * P])).then_inc(g["grown"], 1)

                    dve.wait_ge(hg["staged"], c + 1)
                    h_differ(0)
                    dve.wait_ge(g["state"], (c + 1) * NH)
                    dve.tensor_copy(glast[:], small[:, 4, bass.ds(c, 1), :].rearrange("p o h -> p (o h)"))
                    dve.wait_ge(g["kk"], c + 1)
                    dve.wait_ge(g["weighed"], c + 1)
                    dve.scalar_tensor_tensor(out=lt[:], in0=ps[:, 2, :], scalar=-1.0, in1=decb[:], op0=ALU.mult,
                                             op1=ALU.mult).then_inc(g["lt"], 1)
                    h_differ(1)
                    dve.wait_ge(g["lt"], c + 1)
                    dve.wait_ge(g["seeded"], c + 1)
                    for p in range(2):
                        alone(dve, g["passed"])
                        dve.copy_predicated(pairs2(both(xt, p)), for_pair(k.mask[:, 0, :]), pairs2(both(lt, p)))
                    for p in range(2):
                        dve.wait_ge(g["y"], c * GROW + p + 1)
                        alone(dve, g["passed"])
                        dve.copy_predicated(pairs2(both(x, p)), for_pair(k.maskT[:, 0, :]),
                                            pairs2(ps[:, p, 0:2 * P])).then_inc(g["grown"], 1)
                    dve.wait_ge(g["qk"], c + 1)
                    dve.tensor_tensor(at[:], ps[:, 3, :], dec[:], ALU.mult).then_inc(g["at"], 1)
                    h_place(0)
                    for lv in range(1, LEVELS):
                        h_place(lv)
                        if lv + 1 < LEVELS:
                            h_differ(lv + 1)
                        g_grow(lv)
                        if lv == 1:
                            dve.wait_ge(g["vnat"], c + 1)
                            factor(vb, 5, 1)
                        elif lv == 2:
                            dve.wait_ge(g["knat"], c + 1)
                            factor(kw, 4, 2)
                        elif lv == 3:
                            factor(kd, 4, 3)
                            dve.tensor_tensor(heads(hkdt[:]), heads(hb[:])[:, :, P - 1:P].broadcast_to([P, NH, P]),
                                              heads(hb[:]), ALU.subtract).then_inc(hg["edge"], 1)
                        elif lv == 4:
                            dve.wait_ge(g["eg"], c + 1)
                            dve.tensor_tensor(qd[:], qc[:], egb[:], ALU.mult).then_inc(g["factors"], 1)
                        elif lv == 5:
                            dve.wait_ge(hg["edged"], c + 1)
                            dve.tensor_tensor(hkdt[:], hk[:], hkdt[:], ALU.mult)
                            dve.tensor_tensor(hqd[:], hq[:], hqd[:], ALU.mult).then_inc(hg["qkd"], 1)
                            if more:
                                g_stage(c + 1)
                    h_place(LEVELS)
                    if more:
                        g_identity(c + 1)
                    dve.wait_ge(g["uwout"], c + 1)
                    dve.wait_ge(g["ws"], c + 1)
                    dve.tensor_tensor(vn[:], u[:], ps[:, 2, :], ALU.subtract).then_inc(g["vnew"], 1)
                    if more:
                        g_shift(c + 1)
                    dve.wait_ge(hg["delta"], c + 2)
                    for h in range(NH):
                        dve.scalar_tensor_tensor(out=hs(hstate, h), in0=hs(hstate, h), scalar=elast[:, h:h + 1],
                                                 in1=hs(ps[:, 6, :], h), op0=ALU.mult, op1=ALU.add).then_inc(hg["state"], 1)
                    if more:
                        g_weigh(c + 1)
                    dve.wait_ge(g["delta"], c + 1)
                    dve.wait_ge(g["outs"], c + 2)
                    for h in range(NH):
                        dve.scalar_tensor_tensor(out=hs(state, h), in0=hs(state, h), scalar=glast[:, h:h + 1],
                                                 in1=hs(ps[:, 4, :], h), op0=ALU.mult, op1=ALU.add).then_inc(g["state"], 1)

                g_stage(0)
                g_identity(0)
                g_shift(0)
                g_weigh(0)
                with dve.Fori(0, NT - 1) as c:
                    main(c, True)
                main(NT - 1, False)

            @block.gpsimd
            def _(pool):
                pool.wait_ge(hg["zero"], 1)

                def chunk(c):
                    pool.wait_ge(hg["tiles"], c + 1)
                    for lv in range(LEVELS):
                        m = 1 << lv
                        pool.wait_ge(hg["expd"], c * LEVELS + lv + 1)
                        pool.wait_ge(hg["level"], c * HL + lv - 1 + RING)
                        pool.tensor_tensor(half(kl[lv % RING], m, 0), half(hk, m, 0), half(ed[lv % 2], m, 0), ALU.mult).then_inc(hg["ks"], 1)
                        pool.tensor_tensor(half(ql[lv % RING], m, 1), half(hq, m, 1), half(ed[lv % 2], m, 1), ALU.mult).then_inc(hg["qs"], 1)

                with pool.Fori(0, NT) as c:
                    chunk(c)

            @block.scalar
            def _(act):
                def g_exp(c):
                    act.wait_ge(g["shifted"], c + 1)
                    act.activation(dec[:], dec[:], ACT.Exp).then_inc(g["decay"], 1)
                    act.activation(egb[:], ps[:, 0, :], ACT.Exp).then_inc(g["eg"], 1)

                def h_stage(c):
                    span = bass.ds(c * P, P)
                    act.wait_ge(hg["delta"], c + 1)
                    act.wait_ge(hg["state"], (c + 1) * NH)
                    act.activation(heads(hb[:]), b[:, :, span], ACT.Copy).then_inc(hg["staged"], 1)
                    act.activation(heads(hk[:]), kk[:, :, span], ACT.Copy)
                    act.activation(heads(hq[:]), q[:, :, span], ACT.Copy)
                    act.activation(hv[:], row(v, c), ACT.Copy).then_inc(hg["tiles"], 1)

                def outputs(c, s, bank, o, junk, at_col):
                    act.wait_ge(s["outs"], c + 2)
                    act.wait_ge(s["stored"], (c + 1) * 16)
                    act.activation(o[:], ps[:, bank, :], ACT.Copy).then_inc(s["oout"], 1)
                    for h in range(NH):
                        act.activation(junk[:], hs(ps[:, bank, :], h), ACT.Square,
                                       accum_out=ssq[:, bass.ds(c * NH + (at_col + h), 1)]).then_inc(s["oout"], 1)
                        act.wait_ge(s["oout"], (c + 1) * (NH + 1) + h + 2)

                def main(c, more):
                    def h_exp(lv):
                        act.wait_ge(hg["late"], c * LEVELS + lv + 1)
                        act.activation(ed[lv % 2][:], ed[lv % 2][:], ACT.Exp).then_inc(hg["expd"], 1)

                    h_exp(0)
                    h_exp(1)
                    act.wait_ge(hg["tiles"], c + 1)
                    act.activation(hqd[:], hb[:], ACT.Exp)
                    act.activation(elast[:], heads(hb[:])[:, :, P - 1], ACT.Exp)
                    for lv in range(1, LEVELS):
                        for p in range(2):
                            act.wait_ge(g["y"], c * GROW + 2 * lv + p + 1)
                            act.activation(both(y, p), ps[:, p, 0:2 * P], ACT.Copy).then_inc(g["yout"], 1)
                        if lv + 1 < LEVELS:
                            h_exp(lv + 1)
                        if lv == 4:
                            act.wait_ge(hg["edge"], c + 1)
                            act.activation(hkdt[:], hkdt[:], ACT.Exp).then_inc(hg["edged"], 1)
                    act.wait_ge(hg["turned"], c + 1)
                    act.activation(hkd[:], ps[:, 6, :], ACT.Copy).then_inc(hg["natural"], 1)
                    act.wait_ge(g["uw"], c + 2)
                    act.activation(w[:], ps[:, 5, :], ACT.Copy)
                    act.activation(u[:], ps[:, 4, :], ACT.Copy).then_inc(g["uwout"], 1)
                    outputs(c, hg, 7, oh, hjunk, 0)
                    if more:
                        g_exp(c + 1)
                        h_stage(c + 1)
                    outputs(c, g, 3, og, gjunk, NT * NH)

                prime(act, g["oout"], NH + 1)
                prime(act, hg["oout"], NH + 1)
                h_stage(0)
                g_exp(0)
                with act.Fori(0, NT - 1) as c:
                    main(c, True)
                main(NT - 1, False)

            @block.sync
            def _(sp):
                prime(sp, g["stored"], 16)
                prime(sp, hg["stored"], 16)
                with sp.Fori(0, NT) as c:
                    for s, o, half_at in ((hg, oh, 0), (g, og, 1)):
                        sp.wait_ge(s["oout"], (c + 1) * (NH + 1) + 1)
                        sp.dma_start(o_rows[half_at, bass.ds(c * P, P), :], o[:]).then_inc(s["stored"], 16)
                for s in (hg, g):
                    sp.wait_ge(s["stored"], (NT + 1) * 16)

            @block.tensor
            def _(pe):
                def g_spread(c):
                    pe.wait_ge(g["staged"], c + 1)
                    for h in range(NH):
                        pe.transpose(hs(ps[:, 0, :], h), scol[:, 0, h:h + 1].to_broadcast([P, P]), k.ident[:])
                    for h in range(NH):
                        ins = pe.transpose(hs(ps[:, 1, :], h), scol[:, 1, h:h + 1].to_broadcast([P, P]), k.ident[:])
                    ins.then_inc(g["spread"], 1)

                def main(c, more):
                    def h_scores(n):
                        if n:
                            pe.wait_ge(hg["qs"], c * LEVELS + n)
                        else:
                            pe.wait_ge(hg["tiles"], c + 1)
                        if n == 1:
                            pe.wait_ge(hg["oout"], (c + 1) * (NH + 1))
                        elif n > 1:
                            pe.wait_ge(hg["placed"], c * HL + n)
                        for h in range(NH):
                            a, bq = (kl[(n - 1) % RING], ql[(n - 1) % RING]) if n else (hk, hq)
                            ins = pe.matmul(hs(ps[:, 6 + n % 2, :], h), hs(a, h), hs(bq, h), start=True, stop=True)
                        ins.then_inc(hg["level"], 1)

                    def g_y(lv, p):
                        if lv:
                            pe.wait_ge(g["grown"], c * GROW + 2 * (lv - 1) + p + 1)
                        for h in (2 * p, 2 * p + 1):
                            ins = pe.matmul(hs(ps[:, p, :], h - 2 * p), hs(lt, h), hs(x, h) if lv else k.ident[:],
                                            start=True, stop=True)
                        ins.then_inc(g["y"], 1)

                    def g_d(lv, p):
                        pe.wait_ge(g["yout"], c * (GROW - 2) + 2 * (lv - 1) + p + 1)
                        for h in (2 * p, 2 * p + 1):
                            if lv < LEVELS - 1:
                                pe.matmul(hs(ps[:, 2 + p, :], h - 2 * p), hs(xt, h), hs(y, h), start=True, stop=True)
                            ins = pe.matmul(hs(ps[:, 2 + p, :], h - 2 * p + 2), hs(y, h), hs(xt, h), start=True, stop=True)
                        ins.then_inc(g["dd"], 1)

                    pe.wait_ge(g["tiles"], c + 1)
                    for h in range(NH):
                        ins = pe.matmul(hs(ps[:, 2, :], h), hs(kc, h), hs(kc, h), start=True, stop=True)
                    ins.then_inc(g["kk"], 1)
                    for h in range(NH):
                        ins = pe.transpose(hs(ps[:, 5, :], h), hs(vc, h), k.ident[:])
                    ins.then_inc(g["vnat"], 1)
                    pe.wait_ge(hg["state"], (c + 1) * NH)
                    h_scores(0)
                    pe.wait_ge(g["oout"], (c + 1) * (NH + 1))
                    for h in range(NH):
                        ins = pe.matmul(hs(ps[:, 3, :], h), hs(kc, h), hs(qc, h), start=True, stop=True)
                    ins.then_inc(g["qk"], 1)
                    pe.wait_ge(g["eg"], c + 1)
                    pe.wait_ge(g["lt"], c + 1)
                    g_y(0, 0)
                    g_y(0, 1)
                    pe.wait_ge(g["state"], (c + 1) * NH)
                    for h in range(NH):
                        ins = pe.transpose(hs(ps[:, 4, :], h), hs(kc, h), k.ident[:])
                    ins.then_inc(g["knat"], 1)
                    h_scores(1)
                    for lv in range(1, LEVELS):
                        h_scores(lv + 1)
                        g_y(lv, 0)
                        g_y(lv, 1)
                        if lv == 1:
                            pe.wait_ge(g["at"], c + 1)
                        g_d(lv, 0)
                        g_d(lv, 1)
                    pe.wait_ge(hg["qkd"], c + 1)
                    pe.wait_ge(hg["placed"], c * HL + LEVELS + 1)
                    for h in range(NH):
                        ins = pe.transpose(hs(ps[:, 6, :], h), hs(hkdt, h), k.ident[:])
                    ins.then_inc(hg["turned"], 1)
                    pe.wait_ge(g["factors"], (c + 2) * NF)
                    pe.wait_ge(g["grown"], (c + 1) * GROW)
                    for h in range(NH):
                        pe.matmul(hs(ps[:, 4, :], h), hs(xt, h), hs(vb, h), start=True, stop=True)
                        ins = pe.matmul(hs(ps[:, 5, :], h), hs(kw, h), hs(xt, h), start=True, stop=True)
                    ins.then_inc(g["uw"], 1)
                    if more:
                        g_spread(c + 1)
                    pe.wait_ge(g["uwout"], c + 1)
                    for h in range(NH):
                        ins = pe.matmul(hs(ps[:, 2, :], h), hs(w, h), hs(state, h), start=True, stop=True)
                    ins.then_inc(g["ws"], 1)
                    pe.wait_ge(hg["placed"], (c + 1) * HL + 1)
                    for h in range(NH):
                        pe.matmul(hs(ps[:, 7, :], h), hs(hqd, h), hs(hstate, h), start=True, stop=False)
                        ins = pe.matmul(hs(ps[:, 7, :], h), hs(sc, h), hs(hv, h), start=False, stop=True)
                    ins.then_inc(hg["outs"], 1)
                    pe.wait_ge(hg["natural"], c + 1)
                    for h in range(NH):
                        ins = pe.matmul(hs(ps[:, 6, :], h), hs(hkd, h), hs(hv, h), start=True, stop=True)
                    ins.then_inc(hg["delta"], 1)
                    pe.wait_ge(g["vnew"], c + 1)
                    for h in range(NH):
                        ins = pe.matmul(hs(ps[:, 4, :], h), hs(kd, h), hs(vn, h), start=True, stop=True)
                    ins.then_inc(g["delta"], 1)
                    for h in range(NH):
                        pe.matmul(hs(ps[:, 3, :], h), hs(qd, h), hs(state, h), start=True, stop=False)
                        ins = pe.matmul(hs(ps[:, 3, :], h), hs(at, h), hs(vn, h), start=False, stop=True)
                    ins.then_inc(g["outs"], 1)

                for s in (g["outs"], g["uw"], hg["outs"], hg["delta"]):
                    prime(pe, s)
                prime(pe, hg["level"], RING)
                g_spread(0)
                with pe.Fori(0, NT - 1) as c:
                    main(c, True)
                main(NT - 1, False)


def stage_mix_turn(k, o_rows, gate_rows, ssq, hi, lo):
    nc = k.nc
    rooted, inverted, gated, turned, rounded, rest = (
        k.sem("mix_" + n) for n in ("rooted", "inverted", "gated", "turned", "rounded", "rest"))
    loaded = [k.sem(f"mix_loaded{t}") for t in range(NT)]
    quads = [(q, kt) for q in range(NT // 4) for kt in range(KT)]
    scale = lambda kt: k.cols[:, C_HNORM:C_HNORM + 1] if kt < NH else k.cols[:, C_GNORM:C_GNORM + 1]
    with ExitStack() as tmp:
        r = tmp.enter_context(nc.sbuf_tensor("mix_r", [P, 2, 2 * NT * NH], F32))
        o = tmp.enter_context(nc.sbuf_tensor("mix_o", [P, NT, DM], F32))
        gate = tmp.enter_context(nc.sbuf_tensor("mix_gate", [P, NT, DM], F32))
        with nc.Block() as block:
            @block.sync
            def _(sp):
                for t in range(NT):
                    for group in range(2):
                        sp.dma_start(o[:, t, group * DG:(group + 1) * DG],
                                     o_rows[group, t * P:(t + 1) * P, :]).then_inc(loaded[t], 16)
                    sp.dma_start(gate[:, t, :], gate_rows[t * P:(t + 1) * P, :]).then_inc(loaded[t], 16)

            @block.vector
            def _(dve):
                dve.wait_ge(rooted, 1)
                dve.reciprocal(r[:, 1, :], r[:, 0, :]).then_inc(inverted, 1)
                dve.wait_ge(inverted, 1)

                def gate_tile(t):
                    dve.wait_ge(loaded[t], 48)
                    for h in range(2 * NH):
                        at = (h // NH) * NT * NH + t * NH + h % NH
                        dst = o[:, t, h * P:(h + 1) * P]
                        ins = dve.scalar_tensor_tensor(out=dst, in0=dst, scalar=r[:, 1, at:at + 1],
                                                       in1=gate[:, t, h * P:(h + 1) * P], op0=ALU.mult, op1=ALU.mult)
                    ins.then_inc(gated, 1)

                def remainder(j):
                    q, kt = quads[j]
                    dve.wait_ge(rounded, j + 1)
                    dve.scalar_tensor_tensor(out=lo[:, kt, q * BANK:(q + 1) * BANK], in0=k.psum[:, j % 8, :],
                                             scalar=scale(kt), in1=hi[:, kt, q * BANK:(q + 1) * BANK].bitcast(F32),
                                             op0=ALU.mult, op1=ALU.subtract).then_inc(rest, 1)

                for t in range(4):
                    gate_tile(t)
                for t in range(4, NT):
                    remainder(2 * t - 8)
                    remainder(2 * t - 7)
                    gate_tile(t)
                for j in range(8, len(quads)):
                    remainder(j)

            @block.tensor
            def _(pe):
                for j, (q, kt) in enumerate(quads):
                    if kt == 0:
                        pe.wait_ge(gated, 4 * q + 4)
                    if j >= 8:
                        pe.wait_ge(rest, j - 7)
                    for i in range(4):
                        ins = pe.transpose(k.psum[:, j % 8, i * P:(i + 1) * P],
                                           o[:, 4 * q + i, kt * P:(kt + 1) * P], k.ident[:])
                    ins.then_inc(turned, 1)

            @block.scalar
            def _(act):
                act.activation(r[:, 0, :], ssq[:], ACT.Sqrt, bias=k.eps[:, 0:1], scale=1.0 / HD).then_inc(rooted, 1)
                for j, (q, kt) in enumerate(quads):
                    act.wait_ge(turned, j + 1)
                    act.activation(hi[:, kt, q * BANK:(q + 1) * BANK], k.psum[:, j % 8, :], ACT.Copy,
                                   scale=scale(kt)).then_inc(rounded, 1)


def stage_add_normed(k, name, x, tiles, y, weight_row, out=None):
    nc = k.nc
    n = len(tiles)
    loaded, squared, rooted, inverted, scaled, added, stored = (
        k.sem(name + s) for s in ("_loaded", "_squared", "_rooted", "_inverted", "_scaled", "_added", "_stored"))
    with ExitStack() as tmp:
        stat = tmp.enter_context(nc.sbuf_tensor(name + "_stat", [P, 3, NT], F32))
        junk = tmp.enter_context(nc.sbuf_tensor(name + "_junk", [P, DM], F32))
        wrow = tmp.enter_context(nc.sbuf_tensor(name + "_w", [P, DM], F32))
        with nc.Block() as block:
            @block.sync
            def _(sp):
                sp.dma_start(wrow[:], weight_row.partition_broadcast(P)).then_inc(loaded, 16)
                if out is not None:
                    for i, t in enumerate(tiles):
                        sp.wait_ge(added, i + 1)
                        sp.dma_start(out[t * P:(t + 1) * P, :], x[:, t, :]).then_inc(stored, 16)
                    sp.wait_ge(stored, 16 * n)

            @block.scalar
            def _(act):
                for i in range(n):
                    if i:
                        act.wait_ge(squared, i)
                    act.activation(junk[:], y[:, i, :], ACT.Square, accum_out=stat[:, 0, i:i + 1]).then_inc(squared, 1)
                act.wait_ge(squared, n)
                act.activation(stat[:, 1, 0:n], stat[:, 0, 0:n], ACT.Sqrt, bias=k.eps[:, 0:1],
                               scale=1.0 / DM).then_inc(rooted, 1)

            @block.vector
            def _(dve):
                dve.wait_ge(rooted, 1)
                dve.reciprocal(stat[:, 2, 0:n], stat[:, 1, 0:n]).then_inc(inverted, 1)
                dve.wait_ge(inverted, 1)
                dve.wait_ge(loaded, 16)
                for i in range(n):
                    dve.scalar_tensor_tensor(out=y[:, i, :], in0=y[:, i, :], scalar=stat[:, 2, i:i + 1], in1=wrow[:],
                                             op0=ALU.mult, op1=ALU.mult).then_inc(scaled, 1)
                    if i:
                        dve.wait_ge(scaled, i)
                        dve.tensor_tensor(x[:, tiles[i - 1], :], x[:, tiles[i - 1], :], y[:, i - 1, :], ALU.add).then_inc(added, 1)
                dve.wait_ge(scaled, n)
                dve.tensor_tensor(x[:, tiles[n - 1], :], x[:, tiles[n - 1], :], y[:, n - 1, :], ALU.add).then_inc(added, 1)


def stage_ffn_up(k, name, part, hi, lo, w_up, halo, ghi, glo):
    nc = k.nc
    freed, tapped, smooth, gated, split, edge = (
        k.sem(name + s) for s in ("_freed", "_tapped", "_smooth", "_gated", "_split", "_edge"))
    pad = FK - 1
    with ExitStack() as tmp:
        g = Turned(k, name, tmp, hi, lo, 1, FT, lambda i, u: slab(w_up, DM, i * P + u * DFF))
        line = [tmp.enter_context(nc.sbuf_tensor(f"{name}_line{u}", [P, pad + HALF], F32)) for u in range(2)]
        acc = [tmp.enter_context(nc.sbuf_tensor(f"{name}_acc{u}", [P, HALF], F32)) for u in range(2)]
        act_out = tmp.enter_context(nc.sbuf_tensor(name + "_silu", [P, HALF], F32))
        with nc.Block() as block:
            @block.sync
            def _(sp):
                g.load(sp)

            @block.tensor
            def _(pe):
                g.multiply(pe)

            @block.scalar
            def _(act):
                k.table(act, ACT.Silu)
                g.round(act, 0, 0, first=True)
                g.round(act, 0, 1, first=True)

                def pair(i, more):
                    for u in range(2):
                        act.wait_ge(freed, 2 * i + u + 1)
                        act.wait_ge(g.summed, 2 * i + u + 1)
                        act.activation(line[u][:, pad:pad + HALF], g.bank(u, 0), ACT.Copy).then_inc(g.taken, 1)
                        if more:
                            g.round(act, i + 1, u)
                        act.wait_ge(freed, 2 * i + u + 3)
                        if u == 0:
                            act.activation(act_out[:], acc[0][:], ACT.Silu).then_inc(smooth, 1)
                        else:
                            act.wait_ge(gated, i + 1)
                            act.activation(ghi[:, bass.ds(i, 1), :].rearrange("p o t -> p (o t)"), acc[1][:],
                                           ACT.Copy).then_inc(split, 1)

                prime(act, smooth)
                prime(act, split)
                g.each_pair(act, pair)

            @block.vector
            def _(dve):
                for u in range(2):
                    dve.memset(line[u][:, 0:pad], 0.0).then_inc(freed, 1)
                for u in range(2):
                    g.remainder(dve, 0, u)

                def pair(i, more):
                    for u in range(2):
                        tap = lambda q: k.cols[:, bass.ds(i + (C_FCONV + q * 2 * FT + u * FT), 1)]
                        kept = halo[:, bass.ds(i + u * FT, 1), :].rearrange("p o t -> p (o t)")
                        n = 2 * i + u
                        dve.wait_ge(g.taken, n + 1)
                        if part == 0:
                            dve.tensor_copy(kept, line[u][:, HALF:HALF + pad]).then_inc(edge, 1)
                        else:
                            dve.tensor_copy(line[u][:, 0:pad], kept).then_inc(edge, 1)
                            dve.wait_ge(edge, n + 1)
                        if u == 0:
                            dve.wait_ge(smooth, i + 1)
                        else:
                            dve.wait_ge(split, i + 1)
                        dve.tensor_scalar(acc[u][:], line[u][:, 0:HALF], tap(0), None, ALU.mult).then_inc(tapped, 1)
                        for q in range(1, FK):
                            dve.wait_ge(tapped, n * (FK - 1) + q)
                            dve.scalar_tensor_tensor(out=acc[u][:], in0=line[u][:, q:q + HALF], scalar=tap(q), in1=acc[u][:],
                                                     op0=ALU.mult, op1=ALU.add).then_inc(freed if q == FK - 1 else tapped, 1)
                        if more:
                            g.remainder(dve, i + 1, u)
                    dve.wait_ge(smooth, i + 2)
                    dve.wait_ge(freed, 2 * i + 4)
                    dve.tensor_tensor(acc[1][:], acc[1][:], act_out[:], ALU.mult).then_inc(gated, 1)
                    dve.wait_ge(split, i + 2)
                    here = (slice(None), bass.ds(i, 1), slice(None))
                    dve.tensor_tensor(glo[here].rearrange("p o t -> p (o t)"), acc[1][:],
                                          ghi[here].bitcast(F32).rearrange("p o t -> p (o t)"), ALU.subtract)

                g.each_pair(dve, pair)


def build(nc, a, out):
    w_in, w_up, w_down, w_out = a["w_in"][0], a["w_up"][0], a["w_down"][0], a["w_out"][0]
    x_rows = a["x"][0].rearrange("(t p) d -> p t d", p=P)
    with ExitStack() as ctx:
        k = Kit(nc, ctx)
        stage_setup(k, a)

        def load(name, dst, src, n):
            s = k.sem(name)
            with nc.Block() as block:
                @block.sync
                def _(sp):
                    for t in range(n):
                        sp.dma_start(dst[:, t, :], src[:, t, :]).then_inc(s, 16)
                    sp.wait_ge(s, 16 * n)

        gate_rows = nc.dram_tensor("gate_rows", (SEQ, DM), F32, kind="Internal").ap()
        o_rows = nc.dram_tensor("o_rows", (2, SEQ, DG), F32, kind="Internal").ap()
        with ExitStack() as body:
            ssq = body.enter_context(nc.sbuf_tensor("out_ssq", [P, 2 * NT * NH], F32))
            with ExitStack() as heads_on:
                s = lambda name, shape: heads_on.enter_context(nc.sbuf_tensor(name, shape, F32))
                qkv, small = s("qkv", [P, 3 * NH, SEQ]), s("gdn_small", [P, 5, NT, NH])
                qf, v = s("hgrn_qf", [P, 2 * NH, SEQ]), s("hgrn_v", [P, NT, DG])
                q, f = qf[:, 0:NH, :], qf[:, NH:2 * NH, :]
                work = qf
                with ExitStack() as projecting:
                    hi = projecting.enter_context(nc.sbuf_tensor("h_hi", [P, KT, SEQ], F32R))
                    lo = projecting.enter_context(nc.sbuf_tensor("h_lo", [P, KT, SEQ], F32R))
                    load("x_loaded", work, x_rows, NT)
                    stage_rms(k, "pre", work, list(range(NT)), work)
                    stage_turn(k, "hturn", work, list(range(NT)), hi, lo, lambda kt: k.cols[:, C_MIXPRE + kt:C_MIXPRE + kt + 1])
                    gate_cols = (3 * DG, 7 * DG)
                    stage_natural(k, "gates", hi, lo, NT, KT,
                                  lambda g, kt: w_in[kt * P:(kt + 1) * P, gate_cols[g]:gate_cols[g] + DG], DG, 2,
                                  lambda act, g, t, n, b: act.activation(work[:, t, g * DG:(g + 1) * DG], k.psum[:, b, :], ACT.Silu))
                    stage_gdn_project(k, hi, lo, w_in, qkv, work, gate_rows)
                    stage_gdn_gates(k, hi, lo, w_in, a["gdn_a_log"][0], a["gdn_dt_bias"][0], small)
                    stage_gdn_normalise(k, qkv, work)
                    stage_natural(k, "values", hi, lo, NT, KT,
                                  lambda g, kt: w_in[kt * P:(kt + 1) * P, 2 * DG:3 * DG], DG, 1,
                                  lambda act, g, t, n, b: act.activation(v[:, t, :], k.psum[:, b, :], ACT.Copy))
                    stage_hgrn_project(k, hi, lo, w_in, q, f)
                kk = s("hgrn_k", [P, NH, SEQ])
                stage_hgrn_decay(k, f, kk)
                k.recycle()
                stage_scans(k, qkv, small, q, kk, f, v, o_rows, ssq)
            x = body.enter_context(nc.sbuf_tensor("x", [P, NT, DM], F32))
            with ExitStack() as outp:
                mhi = outp.enter_context(nc.sbuf_tensor("m_hi", [P, KT, SEQ], F32R))
                mlo = outp.enter_context(nc.sbuf_tensor("m_lo", [P, KT, SEQ], F32R))
                stage_mix_turn(k, o_rows, gate_rows, ssq, mhi, mlo)
                y = outp.enter_context(nc.sbuf_tensor("mix_y", [P, NT, DM], F32))
                stage_natural(k, "outp", mhi, mlo, NT, KT,
                              lambda g, kt: w_out[kt * P:(kt + 1) * P, g * BANK:(g + 1) * BANK], BANK, 2,
                              lambda act, g, t, n, b: act.activation(y[:, t, g * BANK:(g + 1) * BANK], k.psum[:, b, :], ACT.Copy))
                load("x_again", x, x_rows, NT)
                stage_add_normed(k, "mixpost", x, list(range(NT)), y, a["mix_norm_post"][0])

            halo = body.enter_context(nc.sbuf_tensor("ffn_halo", [P, 2 * FT, FK - 1], F32))
            for part in range(2):
                k.recycle()
                tiles = list(range(part * 4, part * 4 + 4))
                with ExitStack() as ffn:
                    fhi = ffn.enter_context(nc.sbuf_tensor(f"f_hi{part}", [P, KT, HALF], F32R))
                    flo = ffn.enter_context(nc.sbuf_tensor(f"f_lo{part}", [P, KT, HALF], F32R))
                    with ExitStack() as tmp:
                        xn = tmp.enter_context(nc.sbuf_tensor(f"f_xn{part}", [P, 4, DM], F32))
                        stage_rms(k, f"fpre{part}", x, tiles, xn)
                        stage_turn(k, f"fturn{part}", xn, list(range(4)), fhi, flo,
                                   lambda kt: k.cols[:, C_FFNPRE + kt:C_FFNPRE + kt + 1])
                    ghi = ffn.enter_context(nc.sbuf_tensor(f"g_hi{part}", [P, FT, HALF], F32R))
                    glo = ffn.enter_context(nc.sbuf_tensor(f"g_lo{part}", [P, FT, HALF], F32R))
                    stage_ffn_up(k, f"up{part}", part, fhi, flo, w_up, halo, ghi, glo)
                    fy = ffn.enter_context(nc.sbuf_tensor(f"f_y{part}", [P, 4, DM], F32))
                    stage_natural(k, f"down{part}", ghi, glo, 4, FT,
                                  lambda g, kt: w_down[kt * P:(kt + 1) * P, :], DM, 1,
                                  lambda act, g, t, n, b: act.activation(fy[:, t, n * BANK:(n + 1) * BANK], k.psum[:, b, :], ACT.Copy))
                    stage_add_normed(k, f"ffnpost{part}", x, tiles, fy, a["ffn_norm_post"][0])

            k.recycle()
            with ExitStack() as ple:
                s = lambda name, shape, dt=F32: ple.enter_context(nc.sbuf_tensor(name, shape, dt))
                xhi, xlo = s("x_hi", [P, KT, SEQ], F32R), s("x_lo", [P, KT, SEQ], F32R)
                phi, plo = s("p_hi", [P, 2, SEQ], F32R), s("p_lo", [P, 2, SEQ], F32R)
                e, pe_rows = s("ple_e", [P, NT, DM]), s("p_rows", [P, NT, DPLE])
                load("p_loaded", pe_rows, a["p"][0, 0].rearrange("(t p) d -> p t d", p=P), NT)
                stage_turn(k, "pturn", pe_rows, list(range(NT)), phi, plo, lambda kt: None, n_k=2)
                stage_turn(k, "xturn", x, list(range(NT)), xhi, xlo, lambda kt: None)
                stage_natural(k, "pgate", xhi, xlo, NT, KT,
                              lambda g, kt: a["w_ple_gate"][0, kt * P:(kt + 1) * P, g * BANK:(g + 1) * BANK], BANK, 2,
                              lambda act, g, t, n, b: act.activation(e[:, t, g * BANK:(g + 1) * BANK], k.psum[:, b, :], ACT.Sigmoid))
                pv = s("ple_pv", [P, NT, BANK])
                for g2 in range(2):
                    stage_natural(k, f"pvals{g2}", phi, plo, NT, 2,
                                  lambda g, kt, g2=g2: a["w_ple"][0, kt * P:(kt + 1) * P, g2 * BANK:(g2 + 1) * BANK], BANK, 1,
                                  lambda act, g, t, n, b: act.activation(pv[:, t, :], k.psum[:, b, :], ACT.Copy))
                    with nc.Block() as block:
                        @block.vector
                        def _(dve):
                            for t in range(NT):
                                half = e[:, t, g2 * BANK:(g2 + 1) * BANK]
                                dve.tensor_tensor(half, half, pv[:, t, :], ALU.mult)
                stage_add_normed(k, "plepost", x, list(range(NT)), e, a["ple_norm_post"][0], out=out[0])


_INS = ["x", "p", "mix_norm_pre", "mix_norm_post", "w_in", "hgrn_lb_logits", "hgrn_out_norm", "gdn_conv",
        "gdn_a_log", "gdn_dt_bias", "gdn_out_norm", "w_out", "ffn_norm_pre", "ffn_norm_post", "w_up", "ffn_conv",
        "w_down", "w_ple", "w_ple_gate", "ple_norm_post"]


def kernel(**inputs):
    from concourse import bacc
    from concourse.bass_utils import run_bass_kernel_spmd

    nc = bacc.Bacc("TRN2", target_bir_lowering=False, num_devices=1)
    arrays, args = {}, {}
    for name in _INS:
        v = np.ascontiguousarray(inputs[name])
        arrays["in_" + name] = v
        args[name] = nc.dram_tensor("in_" + name, v.shape, mybir.dt.from_np(v.dtype), kind="ExternalInput").ap()
    out = nc.dram_tensor("out", (1, SEQ, DM), F32, kind="ExternalOutput").ap()
    build(nc, args, out)
    r = run_bass_kernel_spmd(nc, [arrays], core_ids=[0])
    return r.results[0]["out"]
```

```python
from contextlib import ExitStack

import numpy as np

import concourse.bass as bass
from concourse import mybir

F32 = mybir.dt.float32
F32R = mybir.dt.float32r
U32 = mybir.dt.uint32
ALU = mybir.AluOpType
ACT = mybir.ActivationFunctionType

P = 128
SEQ = 1024
DM = 1024
HD = 128
NH = 4
DG = NH * HD
DIN = 8 * DG + 2 * NH
DFF = 2816
DPLE = 256
EPS = 1e-6
NT = SEQ // P
KT = DM // P
FT = DFF // P
GK, FK = 4, 3
LEVELS = 7
HALF = SEQ // 2
BANK = 512

C_MIXPRE = 0
C_FFNPRE = C_MIXPRE + KT
C_HNORM = C_FFNPRE + KT
C_GNORM = C_HNORM + 1
C_LB = C_GNORM + 1
C_GCONV = C_LB + 2 * NH
C_FCONV = C_GCONV + GK * 3 * NH
N_ROWS = C_FCONV
N_COLS = C_FCONV + FK * 2 * FT


class Kit:

    def __init__(self, nc, ctx):
        self.nc, self.ctx = nc, ctx
        self.psum = ctx.enter_context(nc.psum_tensor("psum", [P, 8, BANK], F32))
        c = lambda name, shape: ctx.enter_context(nc.sbuf_tensor(name, shape, F32))
        self.ident = c("ident", [P, P])
        self.ones = c("ones", [P, P])
        self.tri = c("tri", [P, P])
        self.future = c("future", [P, P])
        self.mask = c("mask", [P, LEVELS, P])
        self.maskT = c("maskT", [P, LEVELS, P])
        self.cols = c("cols", [P, N_COLS])
        self.eps = c("eps", [P, 2])
        self.lb = c("lb", [P, 2 * NH])

        self.spare = c("spare", [P, 1])
        self.raw = c("weights_raw", [P, 2, DM])
        self.arrived = [nc.alloc_semaphore(f"weights_arrived{u}") for u in range(2)]
        self.pairs_sent = 0
        self.sems = []

    def table(self, act, func):
        act.activation(self.spare[:], self.eps[:, 0:1], func)

    def sem(self, name):
        self.sems.append(self.nc.alloc_semaphore(name))
        return self.sems[-1]

    def recycle(self):
        self.nc.clear_and_free_semaphores(self.sems)
        self.nc.all_engine_barrier()
        self.sems = []


def alone(eng, passed):
    eng.sem_inc(passed, 1)


def prime(eng, sem, n=1):
    eng.sem_inc(sem, n)


def over_heads(ap):
    return ap.unsqueeze(1).broadcast_to([P, NH, ap.shape[1]])


def over_tokens(ap, n=P):
    return ap.unsqueeze(2).broadcast_to([P, ap.shape[1], n])


def heads(ap):
    return ap.rearrange("p (h t) -> p h t", h=NH)


class Weights:

    def __init__(self, k, pairs, src, width=None):
        self.k, self.pairs, self.src = k, pairs, src
        self.raw = [k.raw[:, u, 0:width] if width else k.raw[:, u, :].rearrange("p (kt c) -> p kt c", c=P)
                    for u in range(2)]
        self.before = k.pairs_sent
        k.pairs_sent += pairs

    def load(self, sp, i, u):
        sp.dma_start(self.raw[u], self.src(i, u)).then_inc(self.k.arrived[u], 16)

    def wait(self, eng, i, u):
        eng.wait_ge(self.k.arrived[u], (i + self.before + 1) * 16)

    def load_first_of(self, following, sp, rest):
        for u in range(2):
            sp.wait_ge(rest, 2 * self.pairs - 1 + u)
            following.load(sp, 0, u)


def natural_weights(k, w, n_k, columns, width):
    def src(i, u):
        g, kt = divmod(2 * i + u, n_k)
        return w[kt * P:(kt + 1) * P, columns[g]:columns[g] + width]

    return Weights(k, len(columns) * n_k // 2, src, width)


def turned_weights(k, w, pairs, column):
    return Weights(k, pairs, lambda i, u: slab(w, DM, column(i, u)))


class Rows:

    def __init__(self, k, name, dst, src):
        self.dst, self.src = dst, src
        self.arrived = [k.sem(f"{name}_arrived{t}") for t in range(NT)]

    def send(self, sp):
        for t in range(NT):
            sp.dma_start(self.dst[:, t, :], self.src[:, t, :]).then_inc(self.arrived[t], 16)

    def wait(self, eng, t):
        eng.wait_ge(self.arrived[t], 16)


def stage_setup(k, params, rows_to_come, following, squares):
    nc = k.nc
    made, loaded, turned, kept, soft, squared = (
        k.sem("setup_" + n) for n in ("made", "loaded", "turned", "kept", "soft", "squared"))
    with ExitStack() as tmp:
        rows = tmp.enter_context(nc.sbuf_tensor("param_rows", [P, P], F32))
        frows = tmp.enter_context(nc.sbuf_tensor("ffn_conv_rows", [P, 2, P], F32))
        sm = tmp.enter_context(nc.sbuf_tensor("bound_work", [P, 6, NH], F32))
        junk = tmp.enter_context(nc.sbuf_tensor("setup_junk", [P, DM], F32))
        half = FK * 2 * FT // 2
        with nc.Block() as block:
            @block.sync
            def _(sp):
                n = 0
                for at, src in ((C_MIXPRE, params["mix_norm_pre"].rearrange("o (r c) -> (o r) c", c=P)),
                                (C_FFNPRE, params["ffn_norm_pre"].rearrange("o (r c) -> (o r) c", c=P)),
                                (C_HNORM, params["hgrn_out_norm"]),
                                (C_GNORM, params["gdn_out_norm"]),
                                (C_LB, params["hgrn_lb_logits"].rearrange("o (r c) -> (o r) c", c=P)),
                                (C_GCONV, params["gdn_conv"].rearrange("o k (r c) -> (o k r) c", c=P))):
                    sp.dma_start(rows[at:at + src.shape[0], :], src).then_inc(loaded, 16)
                    n += 16
                fsrc = params["ffn_conv"].rearrange("o k (r c) -> (o k r) c", c=P)
                for i in range(2):
                    sp.dma_start(frows[0:half, i, :], fsrc[i * half:(i + 1) * half, :]).then_inc(loaded, 16)
                    n += 16
                assert n == 128
                rows_to_come.send(sp)
                for u in range(2):
                    following.load(sp, 0, u)

            @block.gpsimd
            def _(pool):
                step = 0

                def kept_step(ins):
                    ins.then_inc(made, 1)
                    pool.wait_ge(made, step)

                for t, v in ((k.ident, 0.0), (k.ones, 1.0), (k.tri, 1.0), (k.future, 0.0), (k.mask, 0.0), (k.maskT, 0.0)):
                    step += 1
                    pool.memset(t[:], v).then_inc(made, 1)
                step += 2
                pool.memset(k.eps[:, 0:1], EPS).then_inc(made, 1)
                pool.memset(k.eps[:, 1:2], HD * EPS).then_inc(made, 1)
                for lv in range(LEVELS):
                    m = 1 << lv
                    for t, side in ((k.mask, 1), (k.maskT, 0)):
                        step += 1
                        if step == 9:
                            pool.wait_ge(made, 8)
                        v = t[:, lv, :].rearrange("p (n two m) -> p n two m", two=2, m=m)[:, :, side, :]
                        pool.memset(v, 1.0).then_inc(made, 1)
                pool.wait_ge(made, step)
                step += 1
                kept_step(pool.affine_select(out=k.ident[:], in_=k.ident[:], pattern=[[-1, P]],
                                             compare_op=ALU.not_equal, fill=1.0, base=0, channel_multiplier=1))
                step += 1
                kept_step(pool.affine_select(out=k.tri[:], in_=k.tri[:], pattern=[[1, P]],
                                             compare_op=ALU.is_ge, fill=0.0, base=0, channel_multiplier=-1))
                step += 1
                kept_step(pool.affine_select(out=k.future[:], in_=k.future[:], pattern=[[1, P]],
                                             compare_op=ALU.is_ge, fill=-1e30, base=0, channel_multiplier=-1))
                for lv in range(LEVELS):
                    m = 1 << lv
                    n = P // (2 * m)
                    for t, side in ((k.mask, 1), (k.maskT, 0)):
                        v = t[:, lv, :].rearrange("p (n two m) -> p n two m", two=2, m=m)[:, :, side, :]
                        lowest = 0 if side else m
                        step += 1
                        kept_step(pool.affine_select(out=v, in_=v, pattern=[[-2 * m, n], [0, m]],
                                                     compare_op=ALU.is_ge, fill=0.0, base=-lowest,
                                                     channel_multiplier=1))
                        step += 1
                        kept_step(pool.affine_select(out=v, in_=v, pattern=[[2 * m, n], [0, m]],
                                                     compare_op=ALU.is_ge, fill=0.0, base=lowest + m - 1,
                                                     channel_multiplier=-1))

            @block.tensor
            def _(pe):
                pe.wait_ge(made, 8 + 2 * LEVELS + 1)
                pe.wait_ge(loaded, 128)
                pe.transpose(k.psum[:, 0, 0:N_ROWS], rows[0:N_ROWS, :], k.ident[0:N_ROWS, 0:N_ROWS]).then_inc(turned, 1)
                for i in range(2):
                    pe.transpose(k.psum[:, 1 + i, 0:half], frows[0:half, i, :],
                                 k.ident[0:half, 0:half]).then_inc(turned, 1)

            @block.vector
            def _(dve):
                dve.wait_ge(turned, 3)
                dve.tensor_copy(k.cols[:, 0:N_ROWS], k.psum[:, 0, 0:N_ROWS]).then_inc(kept, 1)
                for i in range(2):
                    at = C_FCONV + i * half
                    dve.tensor_copy(k.cols[:, at:at + half], k.psum[:, 1 + i, 0:half]).then_inc(kept, 1)
                dve.wait_ge(kept, 3)
                l0, l1 = k.cols[:, C_LB:C_LB + NH], k.cols[:, C_LB + NH:C_LB + 2 * NH]
                dve.tensor_tensor(sm[:, 0, :], l0, l1, ALU.max).then_inc(kept, 1)
                dve.wait_ge(kept, 4)
                dve.tensor_tensor(sm[:, 1, :], l0, sm[:, 0, :], ALU.subtract)
                dve.tensor_tensor(sm[:, 2, :], l1, sm[:, 0, :], ALU.subtract).then_inc(kept, 1)
                dve.wait_ge(soft, 1)
                dve.tensor_tensor(sm[:, 5, :], sm[:, 3, :], sm[:, 4, :], ALU.add).then_inc(kept, 1)
                dve.wait_ge(kept, 6)
                dve.reciprocal(sm[:, 0, :], sm[:, 5, :]).then_inc(kept, 1)
                dve.wait_ge(kept, 7)
                dve.tensor_tensor(k.lb[:, 0:NH], sm[:, 3, :], sm[:, 0, :], ALU.mult).then_inc(kept, 1)
                dve.wait_ge(kept, 8)
                dve.tensor_scalar(k.lb[:, NH:2 * NH], k.lb[:, 0:NH], -1.0, 1.0, ALU.mult, ALU.add)

            @block.scalar
            def _(act):
                for t in range(NT):
                    rows_to_come.wait(act, t)
                    if t:
                        act.wait_ge(squared, t)
                    act.activation(junk[:], rows_to_come.dst[:, t, :], ACT.Square,
                                   accum_out=squares[:, t:t + 1]).then_inc(squared, 1)
                act.wait_ge(kept, 5)
                act.activation(sm[:, 3:5, :], sm[:, 1:3, :], ACT.Exp).then_inc(soft, 1)


def stage_turn(k, name, src, tiles, hi, lo, scale, n_k=KT, squares=None, scaled=None, rows=None, rows_to_come=None):
    nc = k.nc
    turned, rounded, rest, rooted, inverted, divided = (
        k.sem(name + s) for s in ("_turned", "_rounded", "_rest", "_rooted", "_inverted", "_divided"))
    n = len(tiles)
    quads = [(kt, q) for q in range(n // 4) for kt in range(n_k)]
    with ExitStack() as tmp:
        root = tmp.enter_context(nc.sbuf_tensor(name + "_root", [P, 2, n], F32))
        with nc.Block() as block:
            if rows_to_come:
                @block.sync
                def _(sp):
                    rows_to_come.send(sp)

            @block.tensor
            def _(pe):
                for j, (kt, q) in enumerate(quads):
                    if j >= 8:
                        pe.wait_ge(rest, j - 7)
                    if squares is not None and kt == 0:
                        pe.wait_ge(divided, 4 * q + 4)
                    for i in range(4):
                        if rows and kt == 0:
                            rows.wait(pe, tiles[4 * q + i])
                        part = slice(kt * P, (kt + 1) * P)
                        tile = src[:, tiles[4 * q + i], part] if squares is None else scaled[:, 4 * q + i, part]
                        ins = pe.transpose(k.psum[:, j % 8, i * P:(i + 1) * P], tile, k.ident[:])
                    ins.then_inc(turned, 1)

            @block.scalar
            def _(act):
                if squares is not None:
                    act.activation(root[:, 0, :], squares[:, 0:n], ACT.Sqrt, bias=k.eps[:, 0:1],
                                   scale=1.0 / DM).then_inc(rooted, 1)
                for j, (kt, q) in enumerate(quads):
                    act.wait_ge(turned, j + 1)
                    s = scale(kt)
                    act.activation(hi[:, kt, q * BANK:(q + 1) * BANK], k.psum[:, j % 8, :], ACT.Copy,
                                   scale=1.0 if s is None else s).then_inc(rounded, 1)

            @block.vector
            def _(dve):
                def divide(i):
                    dve.tensor_scalar(scaled[:, i, :], src[:, tiles[i], :], root[:, 1, i:i + 1], None,
                                      ALU.mult).then_inc(divided, 1)

                if squares is not None:
                    dve.wait_ge(rooted, 1)
                    dve.reciprocal(root[:, 1, :], root[:, 0, :]).then_inc(inverted, 1)
                    dve.wait_ge(inverted, 1)
                    for i in range(4):
                        divide(i)
                for j, (kt, q) in enumerate(quads):
                    dve.wait_ge(rounded, j + 1)
                    s = scale(kt)
                    dve.scalar_tensor_tensor(out=lo[:, kt, q * BANK:(q + 1) * BANK], in0=k.psum[:, j % 8, :],
                                             scalar=1.0 if s is None else s,
                                             in1=hi[:, kt, q * BANK:(q + 1) * BANK].bitcast(F32),
                                             op0=ALU.mult, op1=ALU.subtract).then_inc(rest, 1)
                    if squares is not None and q + 1 < n // 4 and kt % 2:
                        divide(4 * (q + 1) + kt // 2)


def stage_natural(k, name, hi, lo, t_tiles, n_k, weights, following, width, groups, dst, func=ACT.Copy, squares=None,
                  product=False, rows_to_come=None):
    nc = k.nc
    parts = width // BANK
    banks = t_tiles * parts
    RING = 2
    rounded, rest, summed, taken, squared = (
        k.sem(name + s) for s in ("_rounded", "_rest", "_summed", "_taken", "_squared"))
    slabs = [(g, kt) for g in range(groups) for kt in range(n_k)]
    with ExitStack() as tmp:
        whi = tmp.enter_context(nc.sbuf_tensor(name + "_whi", [P, RING, width], F32R))
        wlo = tmp.enter_context(nc.sbuf_tensor(name + "_wlo", [P, RING, width], F32R))
        junk = tmp.enter_context(nc.sbuf_tensor(name + "_junk", [P, 2, BANK], F32)) if squares is not None else None
        with nc.Block() as block:
            @block.sync
            def _(sp):
                for j in range(RING, len(slabs)):
                    sp.wait_ge(rest, j - RING + 1)
                    weights.load(sp, j // RING, j % RING)
                    if rows_to_come and j == 2 * RING - 1:
                        rows_to_come.send(sp)
                if following:
                    weights.load_first_of(following, sp, rest)

            @block.scalar
            def _(act):
                def out_of_banks(g):
                    for b in range(banks):
                        t, n, at = b // parts, b % parts, g * banks + b
                        if product:
                            act.wait_ge(taken, at + 1)
                            src = dst(g, t, n)
                        else:
                            act.wait_ge(summed, ((g + 1) * n_k - 1) * banks + b + 1)
                            src = k.psum[:, b, :]
                        if squares is not None:
                            if at >= 2:
                                act.wait_ge(squared, at - 1)
                            act.activation(junk[:, at % 2, :], src, ACT.Square,
                                           accum_out=squares[:, g * parts + n, t:t + 1]).then_inc(squared, 1)
                        if not product:
                            act.activation(dst(g, t, n), src, func).then_inc(taken, 1)

                for j, (g, kt) in enumerate(slabs):
                    weights.wait(act, j // RING, j % RING)
                    if j >= RING:
                        act.wait_ge(summed, (j - RING + 1) * banks)
                    act.activation(whi[:, j % RING, :], weights.raw[j % RING], ACT.Copy).then_inc(rounded, 1)
                    if kt == 0 and g:
                        out_of_banks(g - 1)
                out_of_banks(groups - 1)

            @block.vector
            def _(dve):
                def products(g):
                    for b in range(banks):
                        dve.wait_ge(summed, ((g + 1) * n_k - 1) * banks + b + 1)
                        here = dst(g, b // parts, b % parts)
                        dve.tensor_tensor(here, k.psum[:, b, :], here, ALU.mult).then_inc(taken, 1)

                for j, (g, kt) in enumerate(slabs):
                    dve.wait_ge(rounded, j + 1)
                    dve.tensor_tensor(wlo[:, j % RING, :], weights.raw[j % RING],
                                      whi[:, j % RING, :].bitcast(F32), ALU.subtract).then_inc(rest, 1)
                    if product and kt == 0 and g:
                        products(g - 1)
                if product:
                    products(groups - 1)

            @block.tensor
            def _(pe):
                for j, (g, kt) in enumerate(slabs):
                    pe.wait_ge(rest, j + 1)
                    r = j % RING
                    for b in range(banks):
                        t, n = b // parts, b % parts
                        if kt == 0 and g:
                            pe.wait_ge(taken, (g - 1) * banks + b + 1)
                        out = k.psum[:, b, :]
                        ah, al = hi[:, kt, t * P:(t + 1) * P], lo[:, kt, t * P:(t + 1) * P]
                        wh, wl = whi[:, r, n * BANK:(n + 1) * BANK], wlo[:, r, n * BANK:(n + 1) * BANK]
                        pe.matmul(out, ah, wh, start=(kt == 0), stop=False)
                        pe.matmul(out, ah, wl, start=False, stop=False)
                        pe.matmul(out, al, wh, start=False, stop=(kt == n_k - 1)).then_inc(summed, 1)


class Turned:

    def __init__(self, k, name, tmp, hi, lo, halves, weights, following):
        nc = k.nc
        self.k, self.hi, self.lo, self.halves, self.weights, self.following = k, hi, lo, halves, weights, following
        self.pairs = weights.pairs
        self.rounded, self.rest, self.summed, self.taken = (
            k.sem(name + s) for s in ("_rounded", "_rest", "_summed", "_taken"))
        self.whi = [tmp.enter_context(nc.sbuf_tensor(f"{name}_whi{u}", [P, KT, P], F32R)) for u in range(2)]
        self.wlo = [tmp.enter_context(nc.sbuf_tensor(f"{name}_wlo{u}", [P, KT, P], F32R)) for u in range(2)]

    def load(self, sp):
        with sp.Fori(1, self.pairs) as i:
            for u in range(2):
                sp.wait_ge(self.rest, 2 * i + u - 1)
                self.weights.load(sp, i, u)
        if self.following:
            self.weights.load_first_of(self.following, sp, self.rest)

    def round(self, act, i, u, first=False):
        self.weights.wait(act, i, u)
        if not first:
            act.wait_ge(self.summed, (2 * i + u - 1) * self.halves)
        act.activation(self.whi[u][:], self.weights.raw[u], ACT.Copy).then_inc(self.rounded, 1)

    def remainder(self, dve, i, u):
        dve.wait_ge(self.rounded, 2 * i + u + 1)
        dve.tensor_tensor(self.wlo[u][:], self.weights.raw[u], self.whi[u][:].bitcast(F32),
                          ALU.subtract).then_inc(self.rest, 1)

    def bank(self, u, half):
        return self.k.psum[:, u * self.halves + half, :]

    def multiply(self, pe):
        def pair(i, first=False):
            for u in range(2):
                pe.wait_ge(self.rest, 2 * i + u + 1)
                for half in range(self.halves):
                    if not first:
                        pe.wait_ge(self.taken, (2 * i + u - 2) * self.halves + half + 1)
                    out = self.bank(u, half)
                    for kt in range(KT):
                        ah = self.hi[:, kt, half * BANK:(half + 1) * BANK]
                        al = self.lo[:, kt, half * BANK:(half + 1) * BANK]
                        pe.matmul(out, self.whi[u][:, kt, :], ah, start=(kt == 0), stop=False)
                        pe.matmul(out, self.whi[u][:, kt, :], al, start=False, stop=False)
                        ins = pe.matmul(out, self.wlo[u][:, kt, :], ah, start=False, stop=(kt == KT - 1))
                    ins.then_inc(self.summed, 1)

        pair(0, first=True)
        if self.pairs > 1:
            with pe.Fori(1, self.pairs) as i:
                pair(i)

    def each_pair(self, eng, body):
        if self.pairs > 1:
            with eng.Fori(0, self.pairs - 1) as i:
                body(i, True)
        body(self.pairs - 1, False)


def slab(w, rows, at):
    return w[0:rows, bass.ds(at, P)].rearrange("(kt p) c -> p kt c", p=P)


def stage_gdn_project(k, hi, lo, weights, following, qkv, gates, gate_rows):
    nc = k.nc
    freed, tapped, smooth, kept = (k.sem("gconv_" + n) for n in ("freed", "tapped", "smooth", "kept"))
    with ExitStack() as tmp:
        g = Turned(k, "gproj", tmp, hi, lo, 2, weights, following)
        pad = GK - 1
        line = [tmp.enter_context(nc.sbuf_tensor(f"gconv_line{u}", [P, pad + SEQ], F32)) for u in range(2)]
        acc = tmp.enter_context(nc.sbuf_tensor("gconv_acc", [P, SEQ], F32))
        with nc.Block() as block:
            @block.sync
            def _(sp):
                for t in range(NT):
                    sp.dma_start(gate_rows[t * P:(t + 1) * P, :], gates[:, t, :]).then_inc(kept, 16)
                g.load(sp)
                sp.wait_ge(kept, 16 * NT)

            @block.tensor
            def _(pe):
                g.multiply(pe)

            @block.scalar
            def _(act):
                k.table(act, ACT.Silu)
                g.round(act, 0, 0, first=True)
                g.round(act, 0, 1, first=True)

                def pair(i, more):
                    for u in range(2):
                        act.wait_ge(freed, 2 * i + u + 1)
                        for half in range(2):
                            act.wait_ge(g.summed, (2 * i + u) * 2 + half + 1)
                            act.activation(line[u][:, pad + half * BANK:pad + (half + 1) * BANK], g.bank(u, half),
                                           ACT.Copy).then_inc(g.taken, 1)
                        if more:
                            g.round(act, i + 1, u)
                        act.wait_ge(freed, 2 * i + u + 3)
                        act.activation(qkv[:, bass.ds(2 * i + u, 1), :].rearrange("p o t -> p (o t)"), acc[:],
                                       ACT.Silu).then_inc(smooth, 1)

                prime(act, smooth)
                g.each_pair(act, pair)

            @block.vector
            def _(dve):
                for u in range(2):
                    dve.memset(line[u][:, 0:pad], 0.0).then_inc(freed, 1)
                for u in range(2):
                    g.remainder(dve, 0, u)

                def pair(i, more):
                    for u in range(2):
                        tap = lambda q: k.cols[:, bass.ds(2 * i + u + (C_GCONV + q * 3 * NH), 1)]
                        dve.wait_ge(g.taken, (2 * i + u) * 2 + 2)
                        dve.wait_ge(smooth, 2 * i + u + 1)
                        dve.tensor_scalar(acc[:], line[u][:, 0:SEQ], tap(0), None, ALU.mult).then_inc(tapped, 1)
                        for q in range(1, GK):
                            dve.wait_ge(tapped, (2 * i + u) * (GK - 1) + q)
                            dve.scalar_tensor_tensor(out=acc[:], in0=line[u][:, q:q + SEQ], scalar=tap(q), in1=acc[:],
                                                     op0=ALU.mult, op1=ALU.add).then_inc(freed if q == GK - 1 else tapped, 1)
                        if more:
                            g.remainder(dve, i + 1, u)

                g.each_pair(dve, pair)


class Lengths:

    def __init__(self, k, tmp, qkv, r):
        self.k, self.qkv, self.r, self.n = k, qkv, r, 2 * NH
        self.squared, self.summed, self.logged, self.inverted = (
            k.sem("len_" + n) for n in ("squared", "summed", "logged", "inverted"))
        self.sq = tmp.enter_context(k.nc.sbuf_tensor("len_sq", [P, 2, SEQ], F32))

    def square(self, dve, heads_):
        for m in heads_:
            if m >= 2:
                dve.wait_ge(self.summed, 2 * (m - 1))
            dve.tensor_tensor(self.sq[:, m % 2, :], self.qkv[:, m, :], self.qkv[:, m, :], ALU.mult).then_inc(self.squared, 1)

    def sum(self, pe):
        for m in range(self.n):
            pe.wait_ge(self.squared, m + 1)
            for half in range(2):
                b = 2 * m + half
                if b >= 8:
                    pe.wait_ge(self.logged, b - 7)
                pe.matmul(self.k.psum[:, b % 8, :], self.k.ones[:], self.sq[:, m % 2, half * BANK:(half + 1) * BANK],
                          start=True, stop=True).then_inc(self.summed, 1)

    def invert(self, act):
        for b in range(2 * self.n):
            m, half = b // 2, b % 2
            is_q = m < NH
            act.wait_ge(self.summed, b + 1)
            act.activation(self.r[:, m, half * BANK:(half + 1) * BANK], self.k.psum[:, b % 8, :], ACT.Ln,
                           scale=float(HD) if is_q else 1.0,
                           bias=self.k.eps[:, 1:2] if is_q else self.k.eps[:, 0:1]).then_inc(self.logged, 1)
        act.wait_ge(self.logged, 2 * self.n)
        for m in range(self.n):
            act.activation(self.r[:, m, :], self.r[:, m, :], ACT.Exp, scale=-0.5).then_inc(self.inverted, 1)

    def divide(self, dve):
        for m in range(self.n):
            dve.wait_ge(self.inverted, m + 1)
            dve.tensor_tensor(self.qkv[:, m, :], self.qkv[:, m, :], self.r[:, m, :], ALU.mult)


def stage_gdn_gates(k, hi, lo, w_in, a_log, dt_bias, small, qkv, r):
    nc = k.nc
    s_in, s_hi, s_lo, s_mm, s_row, s_turn, s_act, s_dve, s_sum = (
        k.sem("gate_" + n) for n in ("in", "hi", "lo", "mm", "row", "turn", "act", "dve", "sum"))
    NG = 2 * NH
    with ExitStack() as tmp:
        t = lambda name, shape, dt=F32: tmp.enter_context(nc.sbuf_tensor(name, shape, dt))
        raw, whi, wlo = t("gate_raw", [P, KT, P]), t("gate_whi", [P, KT, P], F32R), t("gate_wlo", [P, KT, P], F32R)
        row = t("gate_row", [NG, SEQ])
        par = t("gate_par", [P, 2, NH])
        z = t("gate_z", [P, 8, NT, NH])
        col = t("gate_col", [P, NT, NG])
        lengths = Lengths(k, tmp, qkv, r)
        with nc.Block() as block:
            @block.sync
            def _(sp):
                sp.dma_start(raw[:], slab(w_in, DM, DIN - P)).then_inc(s_in, 16)
                sp.dma_start(par[:, 0, :], a_log.partition_broadcast(P)).then_inc(s_in, 16)
                sp.dma_start(par[:, 1, :], dt_bias.partition_broadcast(P)).then_inc(s_in, 16)

            @block.scalar
            def _(act):
                act.wait_ge(s_in, 48)
                act.activation(whi[:, :, 0:NG], raw[:, :, P - NG:P], ACT.Copy)
                act.activation(whi[:, :, NG:P], raw[:, :, 0:P - NG], ACT.Copy).then_inc(s_hi, 1)
                lengths.invert(act)
                for half in range(2):
                    act.wait_ge(s_mm, half + 1)
                    act.activation(row[:, half * BANK:(half + 1) * BANK], k.psum[0:NG, half, :], ACT.Copy).then_inc(s_row, 1)
                act.wait_ge(s_dve, 3)
                act.activation(z[:, 2], z[:, 1], ACT.Exp, scale=-1.0).then_inc(s_act, 1)
                act.activation(z[:, 7, 0, :], par[:, 0, :], ACT.Exp).then_inc(s_act, 1)
                act.wait_ge(s_act, 2)
                act.activation(z[:, 3], z[:, 2], ACT.Ln, bias=1.0).then_inc(s_act, 1)
                act.activation(small[:, 1], col[:, :, NH:NG], ACT.Sigmoid).then_inc(s_act, 1)
                act.wait_ge(s_dve, 10)
                act.activation(z[:, 4], small[:, 0], ACT.Exp).then_inc(s_act, 1)
                act.activation(small[:, 3], z[:, 6], ACT.Exp)
                act.activation(small[:, 4], z[:, 5], ACT.Exp)

            @block.tensor
            def _(pe):
                lengths.sum(pe)
                pe.wait_ge(s_lo, 1)
                pe.wait_ge(lengths.logged, 2 * lengths.n)
                for half in range(2):
                    for kt in range(KT):
                        ah = hi[:, kt, half * BANK:(half + 1) * BANK]
                        al = lo[:, kt, half * BANK:(half + 1) * BANK]
                        pe.matmul(k.psum[:, half, :], whi[:, kt, :], ah, start=(kt == 0), stop=False)
                        pe.matmul(k.psum[:, half, :], whi[:, kt, :], al, start=False, stop=False)
                        ins = pe.matmul(k.psum[:, half, :], wlo[:, kt, :], ah, start=False, stop=(kt == KT - 1))
                    ins.then_inc(s_mm, 1)
                pe.wait_ge(s_row, 2)
                for c in range(NT):
                    ins = pe.transpose(k.psum[:, 2, c * NG:(c + 1) * NG], row[:, c * P:(c + 1) * P], k.ident[0:NG, 0:NG])
                ins.then_inc(s_turn, 1)
                pe.wait_ge(s_dve, 7)
                pe.matmul(k.psum[:, 3, 0:NT * NH], k.tri[:], z[:, 0].rearrange("p c h -> p (c h)"), start=True, stop=True)
                pe.matmul(k.psum[:, 4, 0:NT * NH], k.ones[:], z[:, 0].rearrange("p c h -> p (c h)"),
                          start=True, stop=True).then_inc(s_sum, 1)

            @block.vector
            def _(dve):
                def done(ins, n):
                    ins.then_inc(s_dve, 1)
                    dve.wait_ge(s_dve, n)

                lengths.square(dve, range(4))
                dve.wait_ge(s_hi, 1)
                dve.tensor_tensor(wlo[:, :, 0:NG], raw[:, :, P - NG:P], whi[:, :, 0:NG].bitcast(F32), ALU.subtract)
                dve.tensor_tensor(wlo[:, :, NG:P], raw[:, :, 0:P - NG], whi[:, :, NG:P].bitcast(F32), ALU.subtract).then_inc(s_lo, 1)
                lengths.square(dve, range(4, lengths.n))
                lengths.divide(dve)
                dve.wait_ge(s_turn, 1)
                done(dve.tensor_copy(col[:], k.psum[:, 2, 0:NT * NG].rearrange("p (c g) -> p c g", g=NG)), 1)
                bias = par[:, 1, :].unsqueeze(1).broadcast_to([P, NT, NH])
                done(dve.tensor_tensor(z[:, 0], col[:, :, 0:NH], bias, ALU.add), 2)
                done(dve.scalar_tensor_tensor(out=z[:, 1], in0=z[:, 0], scalar=-1.0, in1=z[:, 0], op0=ALU.mult, op1=ALU.max), 3)
                done(dve.tensor_scalar(z[:, 5], z[:, 0], 0.0, None, ALU.max), 4)
                dve.wait_ge(s_act, 4)
                done(dve.tensor_tensor(z[:, 6], z[:, 5], z[:, 3], ALU.add), 5)
                done(dve.tensor_scalar(z[:, 7, 1, :], z[:, 7, 0, :], -1.0, None, ALU.mult), 6)
                done(dve.tensor_tensor(z[:, 0], z[:, 6], z[:, 7, 1, :].unsqueeze(1).broadcast_to([P, NT, NH]), ALU.mult), 7)
                dve.wait_ge(s_sum, 1)
                done(dve.tensor_copy(small[:, 0], k.psum[:, 3, 0:NT * NH].rearrange("p (c h) -> p c h", h=NH)), 8)
                done(dve.tensor_copy(z[:, 5], k.psum[:, 4, 0:NT * NH].rearrange("p (c h) -> p c h", h=NH)), 9)
                done(dve.tensor_tensor(z[:, 6], z[:, 5], small[:, 0], ALU.subtract), 10)
                dve.wait_ge(s_act, 5)
                dve.tensor_tensor(small[:, 2], z[:, 4], small[:, 1], ALU.mult)


def stage_hgrn_project(k, hi, lo, weights, q, f):
    nc = k.nc
    for part, (name, dst, func) in enumerate((("hq", q, ACT.Silu), ("hf", f, ACT.Sigmoid))):
        with ExitStack() as tmp:
            g = Turned(k, name, tmp, hi, lo, 2, weights[part], weights[part + 1])
            with nc.Block() as block:
                @block.sync
                def _(sp):
                    g.load(sp)

                @block.tensor
                def _(pe):
                    g.multiply(pe)

                @block.scalar
                def _(act):
                    g.round(act, 0, 0, first=True)
                    g.round(act, 0, 1, first=True)

                    def pair(i, more):
                        for u in range(2):
                            for half in range(2):
                                act.wait_ge(g.summed, (2 * i + u) * 2 + half + 1)
                                act.activation(dst[:, bass.ds(2 * i + u, 1), half * BANK:(half + 1) * BANK]
                                               .rearrange("p o t -> p (o t)"), g.bank(u, half), func).then_inc(g.taken, 1)
                            if more:
                                g.round(act, i + 1, u)

                    g.each_pair(act, pair)

                @block.vector
                def _(dve):
                    for i in range(NH // 2):
                        for u in range(2):
                            g.remainder(dve, i, u)


def stage_hgrn_decay(k, f, kk):
    nc = k.nc
    bounded, logged = k.sem("hdecay_bounded"), k.sem("hdecay_logged")
    with ExitStack() as tmp:
        keep = tmp.enter_context(nc.sbuf_tensor("hdecay_keep", [P, SEQ], F32))
        with nc.Block() as block:
            @block.vector
            def _(dve):
                for h in range(NH):
                    dve.tensor_scalar(f[:, h, :], f[:, h, :], k.lb[:, NH + h:NH + h + 1], k.lb[:, h:h + 1],
                                      ALU.mult, ALU.add).then_inc(bounded, 1)
                dve.memset(keep[:], 1.0).then_inc(bounded, 1)
                dve.wait_ge(bounded, NH + 1)
                dve.memset(keep[:].rearrange("p (c t) -> p c t", t=P)[:, :, 0:1], 0.0).then_inc(bounded, 1)
                for h in range(NH):
                    dve.tensor_scalar(kk[:, h, :], f[:, h, :], -1.0, 1.0, ALU.mult, ALU.add).then_inc(bounded, 1)
                dve.wait_ge(bounded, NH + 2)
                for h in range(NH):
                    dve.wait_ge(logged, h + 1)
                    dve.tensor_tensor_scan(f[:, h, :], keep[:], f[:, h, :], 0.0, ALU.mult, ALU.add)

            @block.scalar
            def _(act):
                for h in range(NH):
                    act.wait_ge(bounded, NH + 3 + h)
                    act.activation(f[:, h, :], f[:, h, :], ACT.Ln).then_inc(logged, 1)


def stage_scans(k, qkv, small, q, kk, b, v, gate_rows, o_rows, ssq):
    nc = k.nc
    g = {n: k.sem("g_" + n) for n in (
        "staged", "tiles", "spread", "kk", "qk", "vnat", "knat", "shifted", "decay", "eg", "weighed", "lt", "at",
        "factors", "seeded", "y", "yout", "dd", "grown", "uw", "uwout", "ws", "vnew", "outs", "delta", "state",
        "copied", "squared", "gate", "gated", "stored", "passed")}
    hg = {n: k.sem("h_" + n) for n in (
        "staged", "values", "late", "expd", "qs", "level", "placed", "edge", "edged", "qkd",
        "turned", "natural", "outs", "delta", "state", "copied", "squared", "gate", "gated", "zero", "stored")}
    with ExitStack() as tmp:
        t = lambda name, n=DG: tmp.enter_context(nc.sbuf_tensor(name, [P, n], F32))
        kc, qc, vc, egb, dec, lt, at, qd, x, xt, y, kw, kd, vb, w, vn, state, og = (t("g_t_" + n) for n in (
            "kc", "qc", "vc", "egb", "dec", "lt", "at", "qd", "x", "xt", "y", "kw", "kd", "vb", "w", "vn",
            "state", "o"))
        u = y
        hb, hk, hq, hv, sc, hqd, hkdt, hkd, hstate, oh = (t("h_t_" + n) for n in (
            "b", "k", "q", "v", "scores", "qd", "kdt", "kd", "state", "o"))
        RING = 3
        ed = [t(f"h_t_ed{i}") for i in range(2)]
        ql = [t(f"h_t_ql{i}") for i in range(RING)]
        kl = [t(f"h_t_kl{i}") for i in range(RING)]
        gjunk, hjunk = kw, hkdt
        elast, glast = t("h_t_elast", NH), t("g_t_last", NH)
        sc5 = t("g_t_cols", 5 * NH)
        scol = sc5[:].rearrange("p (j h) -> p j h", h=NH)
        ps = k.psum
        ggate, hgate = t("g_t_gate"), t("h_t_gate")
        hs = lambda ap, h: ap[:, h * P:(h + 1) * P]
        both = lambda ap, p: ap[:, p * 2 * P:(p + 1) * 2 * P]
        row = lambda ap, c: ap[:, bass.ds(c, 1), :].rearrange("p o n -> p (o n)")
        GROW = 2 * LEVELS
        HL = LEVELS + 1
        NF = 4

        def half(ap, m, side):
            return ap[:, :].rearrange("p (n two m) -> p n two m", two=2, m=m)[:, :, side, :]

        def halves_of(ap, n_heads, m, side):
            return ap.rearrange("p (h n two m) -> p h n two m", h=n_heads, two=2, m=m)[:, :, :, side, :]

        def mask_for(mask, n_heads, lv, side):
            m = 1 << lv
            v = mask[:, lv, :].bitcast(U32).rearrange("p (n two m) -> p n two m", two=2, m=m)[:, :, side, :]
            return v.unsqueeze(1).broadcast_to([P, n_heads, P // (2 * m), m])

        def middle(m):
            v4 = hb[:].rearrange("p (n two m) -> p n two m", two=2, m=m)[:, :, 0, m - 1:m]
            return v4.broadcast_to([P, DG // (2 * m), m])

        with nc.Block() as block:
            @block.vector
            def _(dve):
                dve.memset(state[:], 0.0).then_inc(g["state"], NH)
                dve.memset(hstate[:], 0.0).then_inc(hg["state"], NH)
                for i in range(RING):
                    dve.memset(ql[i][:], 0.0)
                    dve.memset(kl[i][:], 0.0)
                dve.memset(y[:], 0.0)
                dve.memset(sc[:], 0.0).then_inc(hg["zero"], 1)
                dve.wait_ge(hg["zero"], 1)
                prime(dve, hg["placed"])
                prime(dve, g["factors"], NF)

                def g_stage(c):
                    span = bass.ds(c * P, P)
                    dve.wait_ge(g["factors"], (c + 1) * NF)
                    dve.tensor_copy(scol, small[:, :, bass.ds(c, 1), :].rearrange("p j o h -> p j (o h)")).then_inc(g["staged"], 1)
                    dve.tensor_copy(heads(kc[:]), qkv[:, NH:2 * NH, span])
                    dve.tensor_copy(heads(vc[:]), qkv[:, 2 * NH:3 * NH, span])
                    dve.tensor_copy(heads(qc[:]), qkv[:, 0:NH, span]).then_inc(g["tiles"], 1)

                def g_identity(c):
                    dve.wait_ge(g["uw"], c + 1)
                    dve.tensor_copy(heads(x[:]), over_heads(k.ident[:]))
                    dve.tensor_copy(heads(xt[:]), over_heads(k.ident[:])).then_inc(g["seeded"], 1)

                def g_shift(c):
                    dve.wait_ge(g["spread"], c + 1)
                    for h in range(NH):
                        ins = dve.scalar_tensor_tensor(out=hs(dec, h), in0=hs(ps[:, 0, :], h), scalar=scol[:, 0, h:h + 1],
                                                       in1=k.future[:], op0=ALU.subtract, op1=ALU.add)
                    ins.then_inc(g["shifted"], 1)

                def g_weigh(c):
                    dve.wait_ge(g["decay"], c + 1)
                    dve.tensor_tensor(lt[:], dec[:], ps[:, 1, :], ALU.mult).then_inc(g["weighed"], 1)

                def factor(out, bank, j):
                    dve.tensor_tensor(heads(out[:]), heads(ps[:, bank, :]), over_tokens(scol[:, j, :]),
                                      ALU.mult).then_inc(g["factors"], 1)

                def h_differ(c, lv):
                    m = 1 << lv
                    if lv < 2:
                        dve.wait_ge(hg["staged"], c + 1)
                    dve.wait_ge(hg["qs"], c * LEVELS + (lv - 1 if lv >= 2 else 0) + 1)
                    dve.tensor_tensor(half(ed[lv % 2], m, 1), half(hb, m, 1), middle(m), ALU.subtract)
                    dve.tensor_tensor(half(ed[lv % 2], m, 0), middle(m), half(hb, m, 0), ALU.subtract).then_inc(hg["late"], 1)

                def main(c, more):
                    def h_place(n):
                        dve.wait_ge(hg["level"], c * HL + n + 1 + RING)
                        dve.wait_ge(hg["placed"], c * HL + n + 1)
                        alone(dve, g["passed"])
                        if n:
                            m = 1 << (n - 1)
                            dve.copy_predicated(halves_of(sc[:], NH, m, 1), mask_for(k.mask, NH, n - 1, 1),
                                                halves_of(ps[:, 6 + n % 2, :], NH, m, 1)).then_inc(hg["placed"], 1)
                        else:
                            dve.copy_predicated(heads(sc[:]), over_heads(k.ident[:].bitcast(U32)),
                                                heads(ps[:, 6, :])).then_inc(hg["placed"], 1)

                    def g_grow(lv):
                        m = 1 << lv
                        for p in range(2):
                            dve.wait_ge(g["dd"], c * (GROW - 2) + 2 * (lv - 1) + p + 1)
                            alone(dve, g["passed"])
                            if lv < LEVELS - 1:
                                dve.copy_predicated(halves_of(both(x, p), 2, m, 0), mask_for(k.maskT, 2, lv, 0),
                                                    halves_of(ps[:, 2 + p, 0:2 * P], 2, m, 0))
                            dve.copy_predicated(halves_of(both(xt, p), 2, m, 1), mask_for(k.mask, 2, lv, 1),
                                                halves_of(ps[:, 2 + p, 2 * P:4 * P], 2, m, 1)).then_inc(g["grown"], 1)

                    dve.wait_ge(g["state"], (c + 1) * NH)
                    dve.tensor_copy(glast[:], small[:, 4, bass.ds(c, 1), :].rearrange("p o h -> p (o h)"))
                    dve.wait_ge(g["kk"], c + 1)
                    dve.wait_ge(g["weighed"], c + 1)
                    dve.scalar_tensor_tensor(out=lt[:], in0=ps[:, 2, :], scalar=-1.0, in1=lt[:], op0=ALU.mult,
                                             op1=ALU.mult).then_inc(g["lt"], 1)
                    dve.wait_ge(g["lt"], c + 1)
                    dve.wait_ge(g["seeded"], c + 1)
                    for p in range(2):
                        alone(dve, g["passed"])
                        dve.copy_predicated(halves_of(both(xt, p), 2, 1, 1), mask_for(k.mask, 2, 0, 1),
                                            halves_of(both(lt, p), 2, 1, 1))
                    for p in range(2):
                        dve.wait_ge(g["y"], c * GROW + p + 1)
                        alone(dve, g["passed"])
                        dve.copy_predicated(halves_of(both(x, p), 2, 1, 0), mask_for(k.maskT, 2, 0, 0),
                                            halves_of(ps[:, p, 0:2 * P], 2, 1, 0)).then_inc(g["grown"], 1)
                    dve.wait_ge(g["qk"], c + 1)
                    dve.tensor_tensor(at[:], ps[:, 3, :], dec[:], ALU.mult).then_inc(g["at"], 1)
                    h_place(0)
                    h_differ(c, 2)
                    for lv in range(1, LEVELS):
                        if lv + 2 < LEVELS:
                            h_differ(c, lv + 2)
                        h_place(lv)
                        g_grow(lv)
                        if lv == 1:
                            dve.wait_ge(g["vnat"], c + 1)
                            factor(vb, 5, 1)
                        elif lv == 2:
                            dve.wait_ge(g["knat"], c + 1)
                            dve.wait_ge(g["squared"], c + 1)
                            factor(kw, 4, 2)
                        elif lv == 3:
                            factor(kd, 4, 3)
                            dve.wait_ge(hg["squared"], c + 1)
                            dve.tensor_tensor(heads(hkdt[:]), heads(hb[:])[:, :, P - 1:P].broadcast_to([P, NH, P]),
                                              heads(hb[:]), ALU.subtract).then_inc(hg["edge"], 1)
                        elif lv == 4:
                            dve.wait_ge(g["eg"], c + 1)
                            dve.tensor_tensor(qd[:], qc[:], egb[:], ALU.mult).then_inc(g["factors"], 1)
                        elif lv == 5:
                            dve.wait_ge(hg["edged"], c + 1)
                            dve.tensor_tensor(hkdt[:], hk[:], hkdt[:], ALU.mult)
                            dve.tensor_tensor(hqd[:], hq[:], hqd[:], ALU.mult).then_inc(hg["qkd"], 1)
                            if more:
                                g_stage(c + 1)
                    h_place(LEVELS)
                    if more:
                        h_differ(c + 1, 0)
                        h_differ(c + 1, 1)
                        g_identity(c + 1)
                    dve.wait_ge(g["uwout"], c + 1)
                    dve.wait_ge(g["ws"], c + 1)
                    dve.tensor_tensor(vn[:], u[:], ps[:, 2, :], ALU.subtract).then_inc(g["vnew"], 1)
                    if more:
                        g_shift(c + 1)
                    dve.wait_ge(hg["delta"], c + 2)
                    for h in range(NH):
                        dve.scalar_tensor_tensor(out=hs(hstate, h), in0=hs(hstate, h), scalar=elast[:, h:h + 1],
                                                 in1=hs(ps[:, 6, :], h), op0=ALU.mult, op1=ALU.add).then_inc(hg["state"], 1)
                    if more:
                        g_weigh(c + 1)
                    dve.wait_ge(g["delta"], c + 1)
                    dve.wait_ge(g["outs"], c + 2)
                    for h in range(NH):
                        dve.scalar_tensor_tensor(out=hs(state, h), in0=hs(state, h), scalar=glast[:, h:h + 1],
                                                 in1=hs(ps[:, 4, :], h), op0=ALU.mult, op1=ALU.add).then_inc(g["state"], 1)

                prime(dve, hg["qs"])
                g_stage(0)
                h_differ(0, 0)
                h_differ(0, 1)
                g_identity(0)
                g_shift(0)
                g_weigh(0)
                with dve.Fori(0, NT - 1) as c:
                    main(c, True)
                main(NT - 1, False)

            @block.gpsimd
            def _(pool):
                pool.wait_ge(hg["zero"], 1)

                def put_gate(c, s, o, gate):
                    pool.wait_ge(s["gate"], (c + 1) * 16)
                    pool.wait_ge(s["squared"], c + 2)
                    pool.tensor_tensor(o[:], o[:], gate[:], ALU.mult).then_inc(s["gated"], 1)

                def level(c, lv):
                    m = 1 << lv
                    pool.wait_ge(hg["expd"], c * LEVELS + lv + 1)
                    pool.wait_ge(hg["level"], c * HL + RING + (lv - 1 if lv else 0))
                    pool.tensor_tensor(half(kl[lv % RING], m, 0), half(hk, m, 0), half(ed[lv % 2], m, 0), ALU.mult)
                    pool.tensor_tensor(half(ql[lv % RING], m, 1), half(hq, m, 1), half(ed[lv % 2], m, 1), ALU.mult).then_inc(hg["qs"], 1)

                def chunk(c, first=False):
                    pool.wait_ge(hg["staged"], c + 1)
                    for lv in range(LEVELS):
                        level(c, lv)
                        if not first:
                            if lv == 3:
                                put_gate(c - 1, hg, oh, hgate)
                            elif lv == 5:
                                put_gate(c - 1, g, og, ggate)

                chunk(0, first=True)
                with pool.Fori(1, NT) as c:
                    chunk(c)
                put_gate(NT - 1, hg, oh, hgate)
                put_gate(NT - 1, g, og, ggate)

            @block.scalar
            def _(act):
                def g_exp(c):
                    act.wait_ge(g["shifted"], c + 1)
                    act.activation(dec[:], dec[:], ACT.Exp).then_inc(g["decay"], 1)
                    act.activation(egb[:], ps[:, 0, :], ACT.Exp).then_inc(g["eg"], 1)

                def h_stage(c):
                    span = bass.ds(c * P, P)
                    act.wait_ge(hg["qkd"], c + 1)
                    act.wait_ge(hg["qs"], c * LEVELS + 1)
                    act.activation(heads(hk[:]), kk[:, :, span], ACT.Copy)
                    act.activation(heads(hq[:]), q[:, :, span], ACT.Copy)
                    act.activation(heads(hb[:]), b[:, :, span], ACT.Copy).then_inc(hg["staged"], 1)

                def h_exp(c, lv):
                    act.wait_ge(hg["late"], c * LEVELS + lv + 1)
                    act.activation(ed[lv % 2][:], ed[lv % 2][:], ACT.Exp).then_inc(hg["expd"], 1)

                def h_ready(c):
                    h_exp(c, 0)
                    h_exp(c, 1)

                def outputs(c, s, bank, o, junk, at_col):
                    act.wait_ge(s["outs"], c + 2)
                    act.wait_ge(s["stored"], (c + 1) * 16)
                    act.wait_ge(s["squared"], c + 1)
                    act.activation(o[:], ps[:, bank, :], ACT.Copy).then_inc(s["copied"], 1)
                    act.wait_ge(s["copied"], c + 2)
                    for h in range(NH):
                        ins = act.activation(hs(junk, h), hs(o, h), ACT.Square,
                                             accum_out=ssq[:, bass.ds(c * 2 * NH + (at_col + h), 1)])
                    ins.then_inc(s["squared"], 1)

                def main(c, more):
                    for lv in range(1, LEVELS):
                        m = 1 << lv
                        for p in range(2):
                            act.wait_ge(g["y"], c * GROW + 2 * lv + p + 1)
                            act.activation(half(both(y, p), m, 0), half(ps[:, p, 0:2 * P], m, 0), ACT.Copy).then_inc(g["yout"], 1)
                        if lv == 1:
                            h_exp(c, 2)
                        if lv + 2 < LEVELS:
                            h_exp(c, lv + 2)
                        if lv == 2:
                            act.wait_ge(hg["delta"], c + 1)
                            act.activation(hv[:], row(v, c), ACT.Copy).then_inc(hg["values"], 1)
                            act.activation(hqd[:], hb[:], ACT.Exp)
                            act.wait_ge(hg["state"], (c + 1) * NH)
                            act.activation(elast[:], heads(hb[:])[:, :, P - 1], ACT.Exp)
                        if lv == 4:
                            act.wait_ge(hg["edge"], c + 1)
                            act.activation(hkdt[:], hkdt[:], ACT.Exp).then_inc(hg["edged"], 1)
                    if more:
                        h_stage(c + 1)
                    act.wait_ge(hg["turned"], c + 1)
                    act.activation(hkd[:], ps[:, 6, :], ACT.Copy).then_inc(hg["natural"], 1)
                    act.wait_ge(g["uw"], c + 2)
                    act.activation(w[:], ps[:, 5, :], ACT.Copy)
                    act.activation(u[:], ps[:, 4, :], ACT.Copy).then_inc(g["uwout"], 1)
                    if more:
                        h_ready(c + 1)
                        g_exp(c + 1)
                    outputs(c, hg, 7, oh, hjunk, 0)
                    outputs(c, g, 3, og, gjunk, NH)

                for s in (g, hg):
                    prime(act, s["copied"])
                    prime(act, s["squared"])
                prime(act, hg["qkd"])
                h_stage(0)
                h_ready(0)
                g_exp(0)
                with act.Fori(0, NT - 1) as c:
                    main(c, True)
                main(NT - 1, False)

            @block.sync
            def _(sp):
                prime(sp, g["stored"], 16)
                prime(sp, hg["stored"], 16)
                with sp.Fori(0, NT) as c:
                    for s, gate, o, at in ((hg, hgate, oh, 0), (g, ggate, og, DG)):
                        sp.dma_start(gate[:], gate_rows[bass.ds(c * P, P), at:at + DG]).then_inc(s["gate"], 16)
                    for s, gate, o, at in ((hg, hgate, oh, 0), (g, ggate, og, DG)):
                        sp.wait_ge(s["gated"], c + 1)
                        sp.dma_start(o_rows[bass.ds(c * P, P), at:at + DG], o[:]).then_inc(s["stored"], 16)
                for s in (hg, g):
                    sp.wait_ge(s["stored"], (NT + 1) * 16)

            @block.tensor
            def _(pe):
                def g_spread(c):
                    pe.wait_ge(g["staged"], c + 1)
                    for h in range(NH):
                        pe.transpose(hs(ps[:, 0, :], h), scol[:, 0, h:h + 1].to_broadcast([P, P]), k.ident[:])
                    for h in range(NH):
                        ins = pe.transpose(hs(ps[:, 1, :], h), scol[:, 1, h:h + 1].to_broadcast([P, P]), k.ident[:])
                    ins.then_inc(g["spread"], 1)

                def main(c, more):
                    def h_scores(n):
                        if n:
                            pe.wait_ge(hg["qs"], c * LEVELS + n + 1)
                        else:
                            pe.wait_ge(hg["staged"], c + 1)
                        if n == 1:
                            pe.wait_ge(hg["copied"], c + 1)
                        elif n > 1:
                            pe.wait_ge(hg["placed"], c * HL + n)
                        for h in range(NH):
                            a, bq = (kl[(n - 1) % RING], ql[(n - 1) % RING]) if n else (hk, hq)
                            ins = pe.matmul(hs(ps[:, 6 + n % 2, :], h), hs(a, h), hs(bq, h), start=True, stop=True)
                        ins.then_inc(hg["level"], 1)

                    def g_y(lv, p):
                        if lv:
                            pe.wait_ge(g["grown"], c * GROW + 2 * (lv - 1) + p + 1)
                        for h in (2 * p, 2 * p + 1):
                            ins = pe.matmul(hs(ps[:, p, :], h - 2 * p), hs(lt, h), hs(x, h) if lv else k.ident[:],
                                            start=True, stop=True)
                        ins.then_inc(g["y"], 1)

                    def g_d(lv, p):
                        pe.wait_ge(g["yout"], c * (GROW - 2) + 2 * (lv - 1) + p + 1)
                        for h in (2 * p, 2 * p + 1):
                            if lv < LEVELS - 1:
                                pe.matmul(hs(ps[:, 2 + p, :], h - 2 * p), hs(xt, h), hs(y, h), start=True, stop=True)
                            ins = pe.matmul(hs(ps[:, 2 + p, :], h - 2 * p + 2), hs(y, h), hs(xt, h), start=True, stop=True)
                        ins.then_inc(g["dd"], 1)

                    pe.wait_ge(g["tiles"], c + 1)
                    for h in range(NH):
                        ins = pe.matmul(hs(ps[:, 2, :], h), hs(kc, h), hs(kc, h), start=True, stop=True)
                    ins.then_inc(g["kk"], 1)
                    for h in range(NH):
                        ins = pe.transpose(hs(ps[:, 5, :], h), hs(vc, h), k.ident[:])
                    ins.then_inc(g["vnat"], 1)
                    pe.wait_ge(hg["state"], (c + 1) * NH)
                    h_scores(0)
                    pe.wait_ge(g["copied"], c + 1)
                    for h in range(NH):
                        ins = pe.matmul(hs(ps[:, 3, :], h), hs(kc, h), hs(qc, h), start=True, stop=True)
                    ins.then_inc(g["qk"], 1)
                    pe.wait_ge(g["eg"], c + 1)
                    pe.wait_ge(g["lt"], c + 1)
                    g_y(0, 0)
                    g_y(0, 1)
                    pe.wait_ge(g["state"], (c + 1) * NH)
                    for h in range(NH):
                        ins = pe.transpose(hs(ps[:, 4, :], h), hs(kc, h), k.ident[:])
                    ins.then_inc(g["knat"], 1)
                    h_scores(1)
                    for lv in range(1, LEVELS):
                        g_y(lv, 0)
                        h_scores(lv + 1)
                        g_y(lv, 1)
                        if lv == 1:
                            pe.wait_ge(g["at"], c + 1)
                        g_d(lv, 0)
                        g_d(lv, 1)
                    pe.wait_ge(hg["qkd"], c + 2)
                    pe.wait_ge(hg["placed"], c * HL + LEVELS + 1)
                    for h in range(NH):
                        ins = pe.transpose(hs(ps[:, 6, :], h), hs(hkdt, h), k.ident[:])
                    ins.then_inc(hg["turned"], 1)
                    if more:
                        g_spread(c + 1)
                    pe.wait_ge(g["factors"], (c + 2) * NF)
                    pe.wait_ge(g["grown"], (c + 1) * GROW)
                    for h in range(NH):
                        pe.matmul(hs(ps[:, 4, :], h), hs(xt, h), hs(vb, h), start=True, stop=True)
                        ins = pe.matmul(hs(ps[:, 5, :], h), hs(kw, h), hs(xt, h), start=True, stop=True)
                    ins.then_inc(g["uw"], 1)
                    pe.wait_ge(hg["placed"], (c + 1) * HL + 1)
                    pe.wait_ge(hg["values"], c + 1)
                    for h in range(NH):
                        pe.matmul(hs(ps[:, 7, :], h), hs(hqd, h), hs(hstate, h), start=True, stop=False)
                        ins = pe.matmul(hs(ps[:, 7, :], h), hs(sc, h), hs(hv, h), start=False, stop=True)
                    ins.then_inc(hg["outs"], 1)
                    pe.wait_ge(g["uwout"], c + 1)
                    for h in range(NH):
                        ins = pe.matmul(hs(ps[:, 2, :], h), hs(w, h), hs(state, h), start=True, stop=True)
                    ins.then_inc(g["ws"], 1)
                    pe.wait_ge(hg["natural"], c + 1)
                    for h in range(NH):
                        ins = pe.matmul(hs(ps[:, 6, :], h), hs(hkd, h), hs(hv, h), start=True, stop=True)
                    ins.then_inc(hg["delta"], 1)
                    pe.wait_ge(g["vnew"], c + 1)
                    for h in range(NH):
                        ins = pe.matmul(hs(ps[:, 4, :], h), hs(kd, h), hs(vn, h), start=True, stop=True)
                    ins.then_inc(g["delta"], 1)
                    for h in range(NH):
                        pe.matmul(hs(ps[:, 3, :], h), hs(qd, h), hs(state, h), start=True, stop=False)
                        ins = pe.matmul(hs(ps[:, 3, :], h), hs(at, h), hs(vn, h), start=False, stop=True)
                    ins.then_inc(g["outs"], 1)

                for s in (g["outs"], g["uw"], hg["outs"], hg["delta"]):
                    prime(pe, s)
                prime(pe, hg["level"], RING)
                g_spread(0)
                with pe.Fori(0, NT - 1) as c:
                    main(c, True)
                main(NT - 1, False)


def stage_mix_turn(k, o_rows, ssq, hi, lo):
    nc = k.nc
    rooted, inverted, turned, rounded, rest = (
        k.sem("mix_" + n) for n in ("rooted", "inverted", "turned", "rounded", "rest"))
    divided = [k.sem("mix_divided_" + n) for n in ("even", "odd")]
    loaded = [k.sem(f"mix_loaded{t}") for t in range(NT)]
    quads = [(q, kt) for q in range(NT // 4) for kt in range(KT)]
    scale = lambda kt: k.cols[:, C_HNORM:C_HNORM + 1] if kt < NH else k.cols[:, C_GNORM:C_GNORM + 1]
    with ExitStack() as tmp:
        r = tmp.enter_context(nc.sbuf_tensor("mix_r", [P, 2, 2 * NT * NH], F32))
        o = tmp.enter_context(nc.sbuf_tensor("mix_o", [P, NT, DM], F32))

        def divide(eng, t):
            eng.wait_ge(loaded[t], 16)
            here = o[:, t, :].rearrange("p (h c) -> p h c", c=HD)
            eng.tensor_tensor(here, here, over_tokens(r[:, 1, t * 2 * NH:(t + 1) * 2 * NH]), ALU.mult).then_inc(divided[t % 2], 1)

        with nc.Block() as block:
            @block.sync
            def _(sp):
                for t in range(NT):
                    sp.dma_start(o[:, t, :], o_rows[t * P:(t + 1) * P, :]).then_inc(loaded[t], 16)

            @block.vector
            def _(dve):
                dve.wait_ge(rooted, 1)
                dve.reciprocal(r[:, 1, :], r[:, 0, :]).then_inc(inverted, 1)
                dve.wait_ge(inverted, 1)

                def remainder(j):
                    q, kt = quads[j]
                    dve.wait_ge(rounded, j + 1)
                    dve.scalar_tensor_tensor(out=lo[:, kt, q * BANK:(q + 1) * BANK], in0=k.psum[:, j % 8, :],
                                             scalar=scale(kt), in1=hi[:, kt, q * BANK:(q + 1) * BANK].bitcast(F32),
                                             op0=ALU.mult, op1=ALU.subtract).then_inc(rest, 1)

                for t in range(0, NT, 2):
                    divide(dve, t)
                for j in range(len(quads)):
                    remainder(j)

            @block.gpsimd
            def _(pool):
                pool.wait_ge(inverted, 1)
                for t in range(1, NT, 2):
                    divide(pool, t)

            @block.tensor
            def _(pe):
                for j, (q, kt) in enumerate(quads):
                    if kt == 0:
                        for group in divided:
                            pe.wait_ge(group, 2 * q + 2)
                    if j >= 8:
                        pe.wait_ge(rest, j - 7)
                    for i in range(4):
                        ins = pe.transpose(k.psum[:, j % 8, i * P:(i + 1) * P],
                                           o[:, 4 * q + i, kt * P:(kt + 1) * P], k.ident[:])
                    ins.then_inc(turned, 1)

            @block.scalar
            def _(act):
                act.activation(r[:, 0, :], ssq[:], ACT.Sqrt, bias=k.eps[:, 0:1], scale=1.0 / HD).then_inc(rooted, 1)
                for j, (q, kt) in enumerate(quads):
                    act.wait_ge(turned, j + 1)
                    act.activation(hi[:, kt, q * BANK:(q + 1) * BANK], k.psum[:, j % 8, :], ACT.Copy,
                                   scale=scale(kt)).then_inc(rounded, 1)


def stage_add_normed(k, name, x, tiles, y, squares, weight_row, out=None, rows=None, next_squares=None):
    nc = k.nc
    n = len(tiles)
    loaded, summed, rooted, inverted, scaled, squared, stored = (
        k.sem(name + s) for s in ("_loaded", "_summed", "_rooted", "_inverted", "_scaled", "_squared", "_stored"))
    added = [k.sem(name + s) for s in ("_added_even", "_added_odd")]
    with ExitStack() as tmp:
        stat = tmp.enter_context(nc.sbuf_tensor(name + "_stat", [P, 3, NT], F32))
        wrow = tmp.enter_context(nc.sbuf_tensor(name + "_w", [P, DM], F32))
        junk = tmp.enter_context(nc.sbuf_tensor(name + "_junk", [P, DM], F32))

        def add(eng, i):
            here = x[:, tiles[i], :]
            eng.wait_ge(scaled, i + 1)
            eng.tensor_tensor(here, here, y[:, i, :], ALU.add).then_inc(added[i % 2], 1)

        with nc.Block() as block:
            @block.sync
            def _(sp):
                sp.dma_start(wrow[:], weight_row.partition_broadcast(P)).then_inc(loaded, 16)
                if out is not None:
                    for i, t in enumerate(tiles):
                        sp.wait_ge(added[i % 2], i // 2 + 1)
                        sp.dma_start(out[t * P:(t + 1) * P, :], x[:, t, :]).then_inc(stored, 16)
                    sp.wait_ge(stored, 16 * n)

            @block.scalar
            def _(act):
                act.wait_ge(summed, 1)
                act.activation(stat[:, 1, 0:n], stat[:, 0, 0:n], ACT.Sqrt, bias=k.eps[:, 0:1],
                               scale=1.0 / DM).then_inc(rooted, 1)
                if next_squares is not None:
                    for i in range(n):
                        act.wait_ge(added[i % 2], i // 2 + 1)
                        if i:
                            act.wait_ge(squared, i)
                        act.activation(junk[:], x[:, tiles[i], :], ACT.Square,
                                       accum_out=next_squares[:, i:i + 1]).then_inc(squared, 1)

            @block.vector
            def _(dve):
                dve.tensor_tensor(stat[:, 0, 0:n], squares[:, 0, 0:n], squares[:, 1, 0:n], ALU.add).then_inc(summed, 1)
                dve.wait_ge(rooted, 1)
                dve.reciprocal(stat[:, 2, 0:n], stat[:, 1, 0:n]).then_inc(inverted, 1)
                dve.wait_ge(inverted, 1)
                dve.wait_ge(loaded, 16)
                for i in range(n):
                    dve.scalar_tensor_tensor(out=y[:, i, :], in0=y[:, i, :], scalar=stat[:, 2, i:i + 1], in1=wrow[:],
                                             op0=ALU.mult, op1=ALU.mult).then_inc(scaled, 1)
                    if i >= 2 and i % 2 == 0:
                        if rows:
                            rows.wait(dve, tiles[i - 1])
                        add(dve, i - 1)
                if rows:
                    rows.wait(dve, tiles[n - 1])
                add(dve, n - 1)

            @block.gpsimd
            def _(pool):
                for i in range(0, n, 2):
                    if rows:
                        rows.wait(pool, tiles[i])
                    add(pool, i)


def stage_ffn_up(k, name, part, hi, lo, weights, following, halo, ghi, glo):
    nc = k.nc
    freed, tapped, smooth, gated, split, edge = (
        k.sem(name + s) for s in ("_freed", "_tapped", "_smooth", "_gated", "_split", "_edge"))
    pad = FK - 1
    with ExitStack() as tmp:
        g = Turned(k, name, tmp, hi, lo, 1, weights, following)
        line = [tmp.enter_context(nc.sbuf_tensor(f"{name}_line{u}", [P, pad + HALF], F32)) for u in range(2)]
        acc = [tmp.enter_context(nc.sbuf_tensor(f"{name}_acc{u}", [P, HALF], F32)) for u in range(2)]
        act_out = tmp.enter_context(nc.sbuf_tensor(name + "_silu", [P, HALF], F32))
        product = tmp.enter_context(nc.sbuf_tensor(name + "_product", [P, HALF], F32))
        with nc.Block() as block:
            @block.sync
            def _(sp):
                g.load(sp)

            @block.tensor
            def _(pe):
                g.multiply(pe)

            @block.scalar
            def _(act):
                k.table(act, ACT.Silu)
                g.round(act, 0, 0, first=True)
                g.round(act, 0, 1, first=True)

                def pair(i, more):
                    for u in range(2):
                        if more:
                            g.round(act, i + 1, u)
                        act.wait_ge(freed, 2 * i + u + 1)
                        act.wait_ge(g.summed, 2 * i + u + 1)
                        act.activation(line[u][:, pad:pad + HALF], g.bank(u, 0), ACT.Copy).then_inc(g.taken, 1)
                    act.wait_ge(freed, 2 * i + 3)
                    act.wait_ge(gated, i + 1)
                    act.activation(act_out[:], acc[0][:], ACT.Silu).then_inc(smooth, 1)

                prime(act, smooth)
                g.each_pair(act, pair)

            @block.vector
            def _(dve):
                for u in range(2):
                    dve.memset(line[u][:, 0:pad], 0.0).then_inc(freed, 1)
                for u in range(2):
                    g.remainder(dve, 0, u)
                prime(dve, gated)
                prime(dve, split)

                def pair(i, more):
                    for u in range(2):
                        if more:
                            g.remainder(dve, i + 1, u)
                        tap = lambda q: k.cols[:, bass.ds(i + (C_FCONV + q * 2 * FT + u * FT), 1)]
                        kept = halo[:, bass.ds(i + u * FT, 1), :].rearrange("p o t -> p (o t)")
                        n = 2 * i + u
                        dve.wait_ge(g.taken, n + 1)
                        if part == 0:
                            dve.tensor_copy(kept, line[u][:, HALF:HALF + pad]).then_inc(edge, 1)
                        else:
                            dve.tensor_copy(line[u][:, 0:pad], kept).then_inc(edge, 1)
                            dve.wait_ge(edge, n + 1)
                        if u == 0:
                            dve.wait_ge(smooth, i + 1)
                        else:
                            dve.wait_ge(gated, i + 1)
                        dve.tensor_scalar(acc[u][:], line[u][:, 0:HALF], tap(0), None, ALU.mult).then_inc(tapped, 1)
                        for q in range(1, FK):
                            dve.wait_ge(tapped, n * (FK - 1) + q)
                            dve.scalar_tensor_tensor(out=acc[u][:], in0=line[u][:, q:q + HALF], scalar=tap(q), in1=acc[u][:],
                                                     op0=ALU.mult, op1=ALU.add).then_inc(freed if q == FK - 1 else tapped, 1)
                    dve.wait_ge(smooth, i + 2)
                    dve.wait_ge(freed, 2 * i + 4)
                    dve.wait_ge(split, 2 * i + 1)
                    dve.tensor_tensor(product[:], acc[1][:], act_out[:], ALU.mult).then_inc(gated, 1)
                    high, low = (w[:, bass.ds(i, 1), :].rearrange("p o t -> p (o t)") for w in (ghi, glo))
                    dve.wait_ge(gated, i + 2)
                    dve.tensor_copy(high, product[:]).then_inc(split, 1)
                    dve.wait_ge(split, 2 * i + 2)
                    dve.tensor_tensor(low, product[:], high.bitcast(F32), ALU.subtract).then_inc(split, 1)

                g.each_pair(dve, pair)


def build(nc, a, out):
    w_in, w_up, w_down, w_out = a["w_in"][0], a["w_up"][0], a["w_down"][0], a["w_out"][0]
    x_rows = a["x"][0].rearrange("(t p) d -> p t d", p=P)
    with ExitStack() as ctx:
        k = Kit(nc, ctx)
        w_gates = natural_weights(k, w_in, KT, (3 * DG, 7 * DG), DG)
        w_qkv = turned_weights(k, w_in, 3 * NH // 2, lambda i, u: (2 * i + u) * P + 4 * DG)
        w_values = natural_weights(k, w_in, KT, (2 * DG,), DG)
        w_q = turned_weights(k, w_in, NH // 2, lambda i, u: (2 * i + u) * P)
        w_f = turned_weights(k, w_in, NH // 2, lambda i, u: (2 * i + u) * P + DG)
        w_outp = natural_weights(k, w_out, KT, (0, BANK), BANK)
        w_ffn = []
        for part in range(2):
            w_ffn.append(turned_weights(k, w_up, FT, lambda i, u: i * P + u * DFF))
            w_ffn.append(natural_weights(k, w_down, FT, (0,), DM))
        w_ffn.append(natural_weights(k, a["w_ple_gate"][0], KT, (0, BANK), BANK))
        w_pvals = natural_weights(k, a["w_ple"][0], 2, (0, BANK), BANK)
        gate_rows = nc.dram_tensor("gate_rows", (SEQ, DM), F32, kind="Internal").ap()
        o_rows = nc.dram_tensor("o_rows", (SEQ, DM), F32, kind="Internal").ap()
        with ExitStack() as body:
            new_squares = body.enter_context(nc.sbuf_tensor("new_squares", [P, NT], F32))
            ssq = body.enter_context(nc.sbuf_tensor("out_ssq", [P, 2 * NT * NH], F32))
            with ExitStack() as heads_on:
                s = lambda name, shape: heads_on.enter_context(nc.sbuf_tensor(name, shape, F32))
                qkv, small = s("qkv", [P, 3 * NH, SEQ]), s("gdn_small", [P, 5, NT, NH])
                qf, v = s("hgrn_qf", [P, 2 * NH, SEQ]), s("hgrn_v", [P, NT, DG])
                q, f = qf[:, 0:NH, :], qf[:, NH:2 * NH, :]
                work = qf
                with ExitStack() as projecting:
                    hi = projecting.enter_context(nc.sbuf_tensor("h_hi", [P, KT, SEQ], F32R))
                    lo = projecting.enter_context(nc.sbuf_tensor("h_lo", [P, KT, SEQ], F32R))
                    coming = Rows(k, "x", work, x_rows)
                    stage_setup(k, a, coming, w_gates, new_squares)
                    stage_turn(k, "hturn", work, list(range(NT)), hi, lo, lambda kt: k.cols[:, C_MIXPRE + kt:C_MIXPRE + kt + 1],
                               squares=new_squares, scaled=work)
                    stage_natural(k, "gates", hi, lo, NT, KT, w_gates, w_qkv, DG, 2,
                                  lambda g, t, n: work[:, t, g * DG:(g + 1) * DG], func=ACT.Silu)
                    stage_gdn_project(k, hi, lo, w_qkv, w_values, qkv, work, gate_rows)
                    stage_gdn_gates(k, hi, lo, w_in, a["gdn_a_log"][0], a["gdn_dt_bias"][0], small, qkv, work)
                    stage_natural(k, "values", hi, lo, NT, KT, w_values, w_q, DG, 1,
                                  lambda g, t, n: v[:, t, :])
                    stage_hgrn_project(k, hi, lo, (w_q, w_f, w_outp), q, f)
                kk = s("hgrn_k", [P, NH, SEQ])
                stage_hgrn_decay(k, f, kk)
                k.recycle()
                stage_scans(k, qkv, small, q, kk, f, v, gate_rows, o_rows, ssq)
            x = body.enter_context(nc.sbuf_tensor("x", [P, NT, DM], F32))
            squares = body.enter_context(nc.sbuf_tensor("row_squares", [P, 2, NT], F32))
            with ExitStack() as outp:
                mhi = outp.enter_context(nc.sbuf_tensor("m_hi", [P, KT, SEQ], F32R))
                mlo = outp.enter_context(nc.sbuf_tensor("m_lo", [P, KT, SEQ], F32R))
                stage_mix_turn(k, o_rows, ssq, mhi, mlo)
                y = outp.enter_context(nc.sbuf_tensor("mix_y", [P, NT, DM], F32))
                coming = Rows(k, "x_again", x, x_rows)
                stage_natural(k, "outp", mhi, mlo, NT, KT, w_outp, w_ffn[0], BANK, 2,
                              lambda g, t, n: y[:, t, g * BANK:(g + 1) * BANK], squares=squares, rows_to_come=coming)
                stage_add_normed(k, "mixpost", x, list(range(NT)), y, squares, a["mix_norm_post"][0], rows=coming, next_squares=new_squares)

            halo = body.enter_context(nc.sbuf_tensor("ffn_halo", [P, 2 * FT, FK - 1], F32))
            for part in range(2):
                k.recycle()
                tiles = list(range(part * 4, part * 4 + 4))
                with ExitStack() as ffn:
                    fhi = ffn.enter_context(nc.sbuf_tensor(f"f_hi{part}", [P, KT, HALF], F32R))
                    flo = ffn.enter_context(nc.sbuf_tensor(f"f_lo{part}", [P, KT, HALF], F32R))
                    with ExitStack() as tmp:
                        xn = tmp.enter_context(nc.sbuf_tensor(f"f_xn{part}", [P, 4, DM], F32))
                        stage_turn(k, f"fturn{part}", x, tiles, fhi, flo,
                                   lambda kt: k.cols[:, C_FFNPRE + kt:C_FFNPRE + kt + 1],
                                   squares=new_squares[:, part * 4:part * 4 + 4], scaled=xn)
                    ghi = ffn.enter_context(nc.sbuf_tensor(f"g_hi{part}", [P, FT, HALF], F32R))
                    glo = ffn.enter_context(nc.sbuf_tensor(f"g_lo{part}", [P, FT, HALF], F32R))
                    stage_ffn_up(k, f"up{part}", part, fhi, flo, w_ffn[2 * part], w_ffn[2 * part + 1], halo, ghi, glo)
                    fy = ffn.enter_context(nc.sbuf_tensor(f"f_y{part}", [P, 4, DM], F32))
                    stage_natural(k, f"down{part}", ghi, glo, 4, FT, w_ffn[2 * part + 1], w_ffn[2 * part + 2], DM, 1,
                                  lambda g, t, n: fy[:, t, n * BANK:(n + 1) * BANK], squares=squares)
                    stage_add_normed(k, f"ffnpost{part}", x, tiles, fy, squares, a["ffn_norm_post"][0])

            k.recycle()
            with ExitStack() as ple:
                s = lambda name, shape, dt=F32: ple.enter_context(nc.sbuf_tensor(name, shape, dt))
                phi, plo, e = s("p_hi", [P, 2, SEQ], F32R), s("p_lo", [P, 2, SEQ], F32R), s("ple_e", [P, NT, DM])
                with ExitStack() as gated:
                    s = lambda name, shape, dt=F32: gated.enter_context(nc.sbuf_tensor(name, shape, dt))
                    xhi, xlo, p = s("x_hi", [P, KT, SEQ], F32R), s("x_lo", [P, KT, SEQ], F32R), s("p", [P, NT, DPLE])
                    coming = Rows(k, "p", p, a["p"][0, 0].rearrange("(t p) d -> p t d", p=P))
                    stage_turn(k, "xturn", x, list(range(NT)), xhi, xlo, lambda kt: None, rows_to_come=coming)
                    stage_turn(k, "pturn", p, list(range(NT)), phi, plo, lambda kt: None, n_k=2, rows=coming)
                    stage_natural(k, "pgate", xhi, xlo, NT, KT, w_ffn[4], w_pvals, BANK, 2,
                                  lambda g, t, n: e[:, t, g * BANK:(g + 1) * BANK], func=ACT.Sigmoid)
                stage_natural(k, "pvals", phi, plo, NT, 2, w_pvals, None, BANK, 2,
                              lambda g, t, n: e[:, t, g * BANK:(g + 1) * BANK], squares=squares, product=True)
                stage_add_normed(k, "plepost", x, list(range(NT)), e, squares, a["ple_norm_post"][0], out=out[0])


_INS = ["x", "p", "mix_norm_pre", "mix_norm_post", "w_in", "hgrn_lb_logits", "hgrn_out_norm", "gdn_conv",
        "gdn_a_log", "gdn_dt_bias", "gdn_out_norm", "w_out", "ffn_norm_pre", "ffn_norm_post", "w_up", "ffn_conv",
        "w_down", "w_ple", "w_ple_gate", "ple_norm_post"]


def kernel(**inputs):
    from concourse import bacc
    from concourse.bass_utils import run_bass_kernel_spmd

    nc = bacc.Bacc("TRN2", target_bir_lowering=False, num_devices=1)
    arrays, args = {}, {}
    for name in _INS:
        v = np.ascontiguousarray(inputs[name])
        arrays["in_" + name] = v
        args[name] = nc.dram_tensor("in_" + name, v.shape, mybir.dt.from_np(v.dtype), kind="ExternalInput").ap()
    out = nc.dram_tensor("out", (1, SEQ, DM), F32, kind="ExternalOutput").ap()
    build(nc, args, out)
    r = run_bass_kernel_spmd(nc, [arrays], core_ids=[0])
    return r.results[0]["out"]
```
